# Optimizing a Trainium2 kernel written in Bass

```python
import math
import jax, jax.numpy as jnp
from jax import lax
import numpy as np

D_MODEL = 2048
BATCH = 1
SEQ = 512
DEPTH = 1

CHUNK = 64
N_PREV_CHUNKS = 8
BAND = N_PREV_CHUNKS + 1
REL_CLIP = 128

A_HEADS = 8
A_HEAD_DIM = 128
A_WIDTH = A_HEADS * A_HEAD_DIM

LRU_WIDTH = 512
LRU_BLOCKS = 8
LRU_BLOCK_DIM = LRU_WIDTH // LRU_BLOCKS
CONV_WIDTH = 4
LRU_C = 8.0

N_MEM = 256
C_HEADS = 4
C_HEAD_DIM = 128
C_WIDTH = C_HEADS * C_HEAD_DIM

MIX_WIDTH = A_WIDTH + LRU_WIDTH + C_WIDTH
IN_WIDTH = 3 * A_WIDTH + 2 * LRU_WIDTH + C_WIDTH
N_BRANCHES = 3

PEER_HEADS = 8
N_KEYS = 128
N_EXPERTS = N_KEYS * N_KEYS
PEER_QDIM = 256
PEER_HALF = PEER_QDIM // 2
PEER_TOPK = 16
TOK_BLOCK = 128

EPS = 1e-6
NEG = -1e30

kernel_name = "hybrid_chunk_attn_rglru_memxattn_peer"

def rms_norm(x, g):
    xf = x.astype(jnp.float32)
    y = xf * lax.rsqrt(jnp.mean(xf * xf, axis=-1, keepdims=True) + EPS)
    return (y * g.astype(jnp.float32)).astype(x.dtype)

def chunk_band_attention(q, k, v, rel_bias):
    B, S, H, Dh = q.shape
    nC = S // CHUNK
    qc = q.reshape(B, nC, CHUNK, H, Dh)
    pad = ((0, 0), (N_PREV_CHUNKS, 0), (0, 0), (0, 0), (0, 0))
    kp = jnp.pad(k.reshape(B, nC, CHUNK, H, Dh), pad)
    vp = jnp.pad(v.reshape(B, nC, CHUNK, H, Dh), pad)
    kb = jnp.concatenate([kp[:, j:j + nC] for j in range(BAND)], axis=2)
    vb = jnp.concatenate([vp[:, j:j + nC] for j in range(BAND)], axis=2)
    s = jnp.einsum('bnqhd,bnkhd->bnhqk', qc, kb).astype(jnp.float32) * (Dh ** -0.5)
    qi = np.arange(CHUNK)[:, None]
    km = np.arange(BAND * CHUNK)[None, :]
    dist = N_PREV_CHUNKS * CHUNK + qi - km
    ridx = np.clip(dist, -REL_CLIP, REL_CLIP) + REL_CLIP
    bias = rel_bias[:, ridx].astype(jnp.float32)
    valid = (np.arange(nC)[:, None] + km // CHUNK) >= N_PREV_CHUNKS
    s = jnp.where(valid[None, :, None, None, :], s + bias[None, None], NEG)
    p = jax.nn.softmax(s, axis=-1).astype(v.dtype)
    o = jnp.einsum('bnhqk,bnkhd->bnqhd', p, vb)
    return o.reshape(B, S, H * Dh)

def rg_lru_branch(xl, gl, conv_w, conv_b, wa, ba, wx, bx, lam):
    B, S, W = xl.shape
    xc = lax.conv_general_dilated(
        xl, conv_w.astype(xl.dtype)[:, None, :], window_strides=(1,),
        padding=[(CONV_WIDTH - 1, 0)], dimension_numbers=('NWC', 'WIO', 'NWC'),
        feature_group_count=W) + conv_b
    xg = xc.reshape(B, S, LRU_BLOCKS, LRU_BLOCK_DIM)
    r = jax.nn.sigmoid(jnp.einsum('bsgi,gij->bsgj', xg, wa).reshape(B, S, W) + ba).astype(jnp.float32)
    i = jax.nn.sigmoid(jnp.einsum('bsgi,gij->bsgj', xg, wx).reshape(B, S, W) + bx).astype(jnp.float32)
    log_a = -LRU_C * r * jax.nn.softplus(-lam.astype(jnp.float32))
    a = jnp.exp(log_a)
    mult = jnp.sqrt(jnp.clip(1.0 - jnp.exp(2.0 * log_a), 1e-12, 1.0))
    u = mult * (i * xc.astype(jnp.float32))

    def combine(l, r_):
        a1, b1 = l
        a2, b2 = r_
        return a1 * a2, a2 * b1 + b2

    _, h = lax.associative_scan(combine, (a, u), axis=1)
    return (h * jax.nn.gelu(gl.astype(jnp.float32))).astype(xl.dtype)

def memory_cross_attention(qc, mem, mem_norm_g, w_mem_kv, xq_g, xk_g):
    B, S, _ = qc.shape
    mn = rms_norm(mem, mem_norm_g)
    kv = mn @ w_mem_kv
    k, v = jnp.split(kv, 2, axis=-1)
    q = rms_norm(qc.reshape(B, S, C_HEADS, C_HEAD_DIM), xq_g)
    k = rms_norm(k.reshape(B, N_MEM, C_HEADS, C_HEAD_DIM), xk_g)
    v = v.reshape(B, N_MEM, C_HEADS, C_HEAD_DIM)
    s = jnp.einsum('bshd,bmhd->bhsm', q, k).astype(jnp.float32) * (C_HEAD_DIM ** -0.5)
    p = jax.nn.softmax(s, axis=-1).astype(v.dtype)
    return jnp.einsum('bhsm,bmhd->bshd', p, v).reshape(B, S, C_WIDTH)

def peer(h, w_peer_q, peer_keys, peer_u, peer_v):
    B, S, D = h.shape
    q = (h @ w_peer_q).reshape(B, S, PEER_HEADS, 2, PEER_HALF)
    s = jnp.einsum('bshcd,hckd->bshck', q, peer_keys).astype(jnp.float32)
    sv, si = lax.top_k(s, PEER_TOPK)
    cand = (sv[..., 0, :, None] + sv[..., 1, None, :]).reshape(B, S, PEER_HEADS, PEER_TOPK * PEER_TOPK)
    cidx = (si[..., 0, :, None] * N_KEYS + si[..., 1, None, :]).reshape(B, S, PEER_HEADS, PEER_TOPK * PEER_TOPK)
    fv, fpos = lax.top_k(cand, PEER_TOPK)
    idx = jnp.take_along_axis(cidx, fpos, axis=-1)
    g = jax.nn.softmax(fv, axis=-1).astype(h.dtype)
    nb = (B * S) // TOK_BLOCK
    xb = h.reshape(nb, TOK_BLOCK, D)
    ib = idx.reshape(nb, TOK_BLOCK, PEER_HEADS, PEER_TOPK)
    gb = g.reshape(nb, TOK_BLOCK, PEER_HEADS, PEER_TOPK)

    def block(args):
        xt, it, gt = args
        u = peer_u[it]
        act = jax.nn.gelu(jnp.einsum('thkd,td->thk', u, xt)) * gt
        return jnp.einsum('thk,thkd->td', act, peer_v[it])

    out = lax.map(block, (xb, ib, gb))
    return out.reshape(B, S, D)

def setup_inputs(seed: int = 0) -> dict:
    key = jax.random.key(seed)
    ks = jax.random.split(key, 32)
    f32 = jnp.float32
    D = D_MODEL
    nrm = lambda k, shape, scale: jax.random.normal(k, shape, f32) * scale
    gain = lambda k, shape: 1.0 + 0.02 * jax.random.normal(k, shape, f32)
    a_init = jax.random.uniform(ks[10], (LRU_WIDTH,), f32, 0.9, 0.999) ** (1.0 / LRU_C)
    lru_lambda = jnp.log(a_init) - jnp.log1p(-a_init)
    w_branch = jnp.concatenate([
        nrm(ks[17], (A_WIDTH, D), A_WIDTH ** -0.5),
        nrm(ks[18], (LRU_WIDTH, D), LRU_WIDTH ** -0.5),
        nrm(ks[19], (C_WIDTH, D), C_WIDTH ** -0.5)], axis=0)
    return {
        "x": nrm(ks[0], (BATCH, SEQ, D), 1.0),
        "mem": nrm(ks[1], (BATCH, N_MEM, D), 1.0),
        "norm1_g": gain(ks[2], (D,)),
        "w_in": nrm(ks[3], (D, IN_WIDTH), D ** -0.5),
        "attn_q_norm_g": gain(ks[4], (A_HEAD_DIM,)),
        "attn_k_norm_g": gain(ks[5], (A_HEAD_DIM,)),
        "rel_bias": nrm(ks[6], (A_HEADS, 2 * REL_CLIP + 1), 0.1),
        "conv_w": nrm(ks[7], (CONV_WIDTH, LRU_WIDTH), CONV_WIDTH ** -0.5),
        "conv_b": nrm(ks[8], (LRU_WIDTH,), 0.02),
        "lru_wa": nrm(ks[9], (LRU_BLOCKS, LRU_BLOCK_DIM, LRU_BLOCK_DIM), LRU_BLOCK_DIM ** -0.5),
        "lru_ba": nrm(ks[11], (LRU_WIDTH,), 0.02),
        "lru_wx": nrm(ks[12], (LRU_BLOCKS, LRU_BLOCK_DIM, LRU_BLOCK_DIM), LRU_BLOCK_DIM ** -0.5),
        "lru_bx": nrm(ks[13], (LRU_WIDTH,), 0.02),
        "lru_lambda": lru_lambda,
        "mem_norm_g": gain(ks[14], (D,)),
        "w_mem_kv": nrm(ks[15], (D, 2 * C_WIDTH), D ** -0.5),
        "xq_norm_g": gain(ks[16], (C_HEAD_DIM,)),
        "xk_norm_g": gain(ks[20], (C_HEAD_DIM,)),
        "w_gate": nrm(ks[21], (D, N_BRANCHES * D), D ** -0.5),
        "b_gate": nrm(ks[22], (N_BRANCHES * D,), 0.02),
        "w_branch": w_branch,
        "w_o": nrm(ks[23], (D, D), D ** -0.5),
        "norm2_g": gain(ks[24], (D,)),
        "w_peer_q": nrm(ks[25], (D, PEER_HEADS * PEER_QDIM), D ** -0.5),
        "peer_keys": nrm(ks[26], (PEER_HEADS, 2, N_KEYS, PEER_HALF), PEER_HALF ** -0.5),
        "peer_u": nrm(ks[27], (N_EXPERTS, D), D ** -0.5),
        "peer_v": nrm(ks[28], (N_EXPERTS, D), 0.5),
    }

def reference(x, mem, norm1_g, w_in, attn_q_norm_g, attn_k_norm_g, rel_bias, conv_w, conv_b,
              lru_wa, lru_ba, lru_wx, lru_bx, lru_lambda, mem_norm_g, w_mem_kv, xq_norm_g, xk_norm_g,
              w_gate, b_gate, w_branch, w_o, norm2_g, w_peer_q, peer_keys, peer_u, peer_v):
    B, S, D = x.shape
    for _ in range(DEPTH):
        h = rms_norm(x, norm1_g)
        proj = h @ w_in
        cuts = np.cumsum([A_WIDTH, A_WIDTH, A_WIDTH, LRU_WIDTH, LRU_WIDTH])
        qa, ka, va, xl, gl, qc = jnp.split(proj, cuts, axis=-1)

        qa = rms_norm(qa.reshape(B, S, A_HEADS, A_HEAD_DIM), attn_q_norm_g)
        ka = rms_norm(ka.reshape(B, S, A_HEADS, A_HEAD_DIM), attn_k_norm_g)
        va = va.reshape(B, S, A_HEADS, A_HEAD_DIM)
        o_a = chunk_band_attention(qa, ka, va, rel_bias)

        o_b = rg_lru_branch(xl, gl, conv_w, conv_b, lru_wa, lru_ba, lru_wx, lru_bx, lru_lambda)

        o_c = memory_cross_attention(qc, mem, mem_norm_g, w_mem_kv, xq_norm_g, xk_norm_g)

        y_a = o_a @ w_branch[:A_WIDTH]
        y_b = o_b @ w_branch[A_WIDTH:A_WIDTH + LRU_WIDTH]
        y_c = o_c @ w_branch[A_WIDTH + LRU_WIDTH:]
        g = jax.nn.sigmoid(h @ w_gate + b_gate).reshape(B, S, N_BRANCHES, D)
        merged = g[:, :, 0] * y_a + g[:, :, 1] * y_b + g[:, :, 2] * y_c
        x = x + merged @ w_o

        x = x + peer(rms_norm(x, norm2_g), w_peer_q, peer_keys, peer_u, peer_v)
    return x


_drawn_inputs = setup_inputs


def setup_inputs(seed=0):
    import zlib

    import numpy as np

    out = dict(_drawn_inputs(seed))
    spreads = {}
    factors = {'attn_q_norm_g': 16.2,
     'attn_k_norm_g': 5.679,
     'rel_bias': 17.588,
     'lru_ba': 56.608,
     'lru_bx': 45.128,
     'mem_norm_g': 5.487,
     'xq_norm_g': 6.82,
     'xk_norm_g': 6.632,
     'b_gate': 5.145,
     'conv_b': 4.222,
     'norm2_g': 4.608}
    for name, (base, spread) in spreads.items():
        noise = np.random.default_rng([zlib.crc32(name.encode()), seed]).standard_normal(out[name].shape)
        drawn = base * np.exp(spread * noise) if base else spread * noise
        out[name] = __import__('jax').numpy.asarray(drawn.astype(out[name].dtype))
    for name, factor in factors.items():
        out[name] = (out[name] * factor).astype(out[name].dtype)
    return out
```

```python
from contextlib import ExitStack

import concourse.bass as bass
import numpy as np
from concourse import mybir

F32 = mybir.dt.float32
U32 = mybir.dt.uint32
F32R = mybir.dt.float32r
ALU = mybir.AluOpType
ACT = mybir.ActivationFunctionType
AX_X = mybir.AxisListType.X

P = 128
D = 2048
KC = D // P
S = 512
TT = S // P
MEM = 256
MT = MEM // P
CHUNK = 64
HA = 8
HC = 4
DH = 128
LC = 4
TAPS = 4
CLIP = 128
NREL = 2 * CLIP + 1
EXT = 3 * P
PH = 8
NKEYS = 128
TOPK = 16
JG = 8
NG = NKEYS // JG
ND = S - P
TG = TT - 1
TB = 32
NTB = ND // TB
HT = TB // 4
PAIRS = PH * TOPK
EPS = 1e-6
NEG = -1e30
LOWEST = -3.0e38
SCALE = float(DH) ** -0.5

SLOTS = 4
T_MK = 0
T_MV = T_MK + HC
T_QK = T_MV + 4
N_QK = 2 * HA + HC
T_LRU = T_QK + N_QK
T_V = T_LRU + 2 * LC
T_MIX = T_V + 8
T_WO = T_MIX + 4 * KC
T_PQ = T_WO + KC
S_LRU = T_LRU - T_QK
S_V = T_V - T_QK
S_MIX = T_MIX - T_QK
S_WO = S_MIX + 3 * KC
T_EXP = T_PQ + 2 * PH


class Steps:

    def __init__(self, eng, sem):
        self.eng, self.sem, self.start, self.n, self.turn, self.per = eng, sem, 0, 0, None, 0

    def loop(self, turn, per):
        self.start, self.n, self.turn, self.per = self.start + self.n, 0, turn, per

    def end(self, turns):
        assert self.n == self.per, (self.n, self.per)
        self.start, self.n, self.turn = self.start + turns * self.per, 0, None

    def did(self, ins):
        ins.then_inc(self.sem, 1)
        self.n += 1
        return self.n

    def wait(self, n=None):
        n = self.start + (self.n if n is None else n)
        self.eng.wait_ge(self.sem, n if self.turn is None else self.turn * self.per + n)


def hybrid_block(nc, x_t, mem_t, g1, g2, gmem, head_g, w_memk, w_memv, w_qk, w_lru_in, w_v, rel_rev,
                 lru_w, lru_vec, w_mix, b_gate, w_o, w_pq, keys, w_exp, u_rows, v_rows, out_t):
    ctx = ExitStack()
    with ctx:
        def sb(name, shape, dt=F32):
            return ctx.enter_context(nc.sbuf_tensor(name, shape, dt))

        def sem(name):
            return ctx.enter_context(nc.semaphore(name))

        ones = sb("ones", [P, P])
        ident = sb("ident", [P, P])
        iota = sb("iota", [P, P])
        vecs = sb("vecs", [P, 3 * KC])
        hgain = sb("hgain", [P, 4])
        bgate = sb("bgate", [P, 3 * KC])
        lvec = sb("lvec", [P, 8, LC])
        sp = sb("sp", [P, 6, LC])
        eps = sb("eps", [P, 1])
        rext = sb("rext", [HA, EXT])
        smax = sb("smax", [P, TT])
        nmax = sb("nmax", [P, TT])
        ssum = sb("ssum", [P, TT])
        rinv = sb("rinv", [P, TT])

        QM, KV, QC, GL, XL = 0, 4096, 12288, 14336, 16384
        MK, MV, TZ, Z = 18448, 19472, 20496, 22544
        base = -(-nc.sbuf_base // 64) * 64

        def place(name, kib, dims, dt=F32):
            return nc.alloc_sbuf_tensor_at(name, [P, *dims], dt, offset=base + int(kib * 1024))

        xT = place("xT", 0, [KC, S])
        hT = place("hT", 32, [KC, S])
        ring = [place(f"ring{i}", 64 + 8 * i, [16, P]) for i in range(SLOTS)]
        arena = place("arena", 96, [Z + 4096])
        p_hi = place("p_hi", 80, [16, P], F32R)
        p_lo = place("p_lo", 88, [16, P], F32R)
        norm_hi = place("norm_hi", 0, [KC, S], F32R)
        norm_lo = place("norm_lo", 32, [KC, S], F32R)
        w_hi = [place(f"w_hi{i}", 80 + 16 * i, [16, P], F32R) for i in range(2)]
        w_lo = [place(f"w_lo{i}", 88 + 16 * i, [16, P], F32R) for i in range(2)]
        h_hi = place("h_hi", 32, [KC, S], F32R)
        h_lo = place("h_lo", 112, [KC, S], F32R)
        h_tok = place("h_tok", 32, [KC, S])[:, :, ND:]
        g_acc = place("g_acc", 112, [KC, S])[:, :, ND:]
        wt = [place(f"wt{i}", 80 + 16 * i, [NKEYS, TB]) for i in range(2)]
        ohA = [place(f"ohA{i}", 144 + 4 * i, [HT, P]) for i in range(2)]
        ohB = [place(f"ohB{i}", 152 + 4 * i, [HT, P]) for i in range(2)]
        act_hi = place("act_hi", 144, [JG, ND], F32R)
        act_lo = place("act_lo", 156, [JG, ND], F32R)
        wg = place("wg", 168, [NTB, JG, TB])
        gel = [place(f"gel{i}", 180 + 1.5 * i, [ND]) for i in range(2)]
        grow = [place(f"grow{i}", 183 + 8 * i, [D]) for i in range(2)]
        g_idx = place("g_idx", 200.5, [PAIRS], U32)
        g_w = place("g_w", 201, [PAIRS])
        g_dot = place("g_dot", 201.5, [PAIRS])
        g_act = place("g_act", 202, [PAIRS])
        g_col = [place(f"g_col{i}", 202.5 + i / 16, [1], U32) for i in range(2)]
        ident_r = place("ident_r", 203, [P], F32R)

        def at(offset, *dims):
            n = int(np.prod(dims))
            v = arena[:, offset:offset + n]
            if len(dims) == 1:
                return v
            names = "abcd"[:len(dims)]
            return v.rearrange(f"p ({' '.join(names)}) -> p {' '.join(names)}", **dict(zip(names[1:], dims[1:])))

        memT = at(QM, KC, MEM)
        xsq = at(KV, KC, S)
        msq = at(QC, KC, MEM)
        qT = at(QM, HA, S)
        kT = at(KV, HA, S)
        vA = at(KV + 4096, TT, HA * DH)
        qkc = at(QC, HC, S)
        gl = at(GL, LC, S)
        xl = at(XL, LC, S + TAPS - 1)
        mk = at(MK, HC, MEM)
        mv = at(MV, MT, HC * DH)
        rt = [at(Z + 1024 * i, S) for i in range(2)]
        sq = [at(Z + 1024 * i + 512, S) for i in range(2)]
        lw = at(TZ, 2, LC, P)
        xc = at(Z, LC, S)
        rg = at(Z + 2048, LC, S)
        ig = at(XL, LC, S)
        la = at(TZ + 1024, S)
        lr = at(TZ + 1536, S)
        tb = at(TZ, HA, 2 * P)
        s_sb = at(Z, TT, S)
        pT = [at(Z + 2048 + (0, 512, 896, 1152)[kt], (TT - kt) * P) for kt in range(TT)]
        pTc = [at(Z + 2048 + 512 * kt, S) for kt in range(MT)]
        qs = at(XL, S)
        vs = at(XL + 512, TT, DH)
        merged = at(KV, KC, S)
        sig = at(Z, 3, S)
        prod = at(Z + 1536, 3, S)
        sumsq = at(Z, S)
        sqx = at(Z + 512, S)
        rt2 = at(Z + 1024, S)
        h2 = [at(Z + 1536 + 512 * i, S) for i in range(2)]
        kys = at(QC, 2 * PH, NKEYS)
        qp = at(GL, SLOTS, S)
        sc = at(XL, SLOTS, TT, NKEYS)
        sv = at(MK, 2, 2, TT, TOPK)
        si = at(MK + 256, 2, 2, TT, TOPK).bitcast(U32)
        fpos = at(MK + 512, TT, TOPK).bitcast(U32)
        fa = at(MK + 576, TT * TOPK).bitcast(U32)
        fb = at(MK + 640, TT * TOPK).bitcast(U32)
        fv = at(MK + 704, TT, TOPK)
        ires = at(MK + 768, TT, TOPK)
        jres = at(MK + 832, TT, TOPK)
        cand = at(Z, TT, TOPK, TOPK)
        pick = at(Z + 1024, 2, TT * TOPK, TOPK)
        route = at(TZ, 3, TT, PH, TOPK)
        gmx = at(MV, TT * PH)
        gsum = at(MV + 32, TT * PH)
        grec = at(MV + 64, TT * PH)
        routeT = at(XL, 3, ND)
        bank = [ctx.enter_context(nc.psum_tensor(f"bank{i}", [P, S], F32)) for i in range(8)]
        rel_dram = nc.dram_tensor("rel_ext", [P, HA, EXT], F32)
        table_dram = nc.dram_tensor("tables", [NTB, P, NKEYS * TB], F32).ap()

        slot_in = [sem(f"slot_in{i}") for i in range(SLOTS)]
        tile_done = sem("tile_done")
        mem_in, x_in, vec_in = sem("mem_in"), [sem(f"x_in{i}") for i in range(4)], sem("vec_in")
        const_made = sem("const_made")
        mem_sq, x_sq = sem("mem_sq"), sem("x_sq")
        norm_ss = sem("norm_ss")
        norm_rt = sem("norm_rt")
        mem_h, h_ready = sem("mem_h"), sem("h_ready")
        h_made, h_high = sem("h_made"), sem("h_high")
        pair_in = [sem(f"pair_in{i}") for i in range(2)]
        quarter_hi, quarter_lo = sem("quarter_hi"), sem("quarter_lo")
        part_used = sem("part_used")
        x_back, m_hi_ok, m_ready = sem("x_back"), sem("m_hi_ok"), sem("m_ready")
        acc_copied = sem("acc_copied")
        head_sq, head_ss, head_rt, head_ok = sem("head_sq"), sem("head_ss"), sem("head_rt"), sem("head_ok")
        lin_copied, v_copied = sem("lin_copied"), sem("v_copied")
        xl_zero = sem("xl_zero")
        lw_zero, lw_in = sem("lw_zero"), sem("lw_in")
        lam_abs, lam_exp, sp_ok = sem("lam_abs"), sem("lam_exp"), sem("sp_ok")
        conv_ok, lru_mm, lru_sig, lru_tanh, lru_m2, lru_mult, lru_ok = (
            sem("conv_ok"), sem("lru_mm"), sem("lru_sig"), sem("lru_tanh"), sem("lru_m2"), sem("lru_mult"), sem("lru_ok"))
        rel_in, rel_filled, rel_out, bias_in, bias_ok = (
            sem("rel_in"), sem("rel_filled"), sem("rel_out"), sem("bias_in"), sem("bias_ok"))

        class Attention:
            def __init__(self, n):
                self.staged = sem(f"{n}_staged")
                self.scores = sem(f"{n}_scores")
                self.taken = sem(f"{n}_taken")
                self.shifted = sem(f"{n}_shifted")
                self.exped = sem(f"{n}_exped")
                self.probs = sem(f"{n}_probs")
                self.turned = sem(f"{n}_turned")
                self.probsT = sem(f"{n}_probsT")
                self.mixed = sem(f"{n}_mixed")
                self.out = sem(f"{n}_out")

        at_a, at_c = Attention("band"), Attention("cross")
        gate_ok, y_used, merged_ok = sem("gate_ok"), sem("y_used"), sem("merged_ok")
        x2_ok, x2_sq, x2_sum = sem("x2_ok"), sem("x2_sq"), sem("x2_sum")
        h2_ready = sem("h2_ready")
        h2_made, h2_hi = sem("h2_made"), sem("h2_hi")
        raw_in = [sem(f"raw_in{i}") for i in range(2)]
        split_hi, split_lo = sem("split_hi"), sem("split_lo")
        keys_in, pq_copied, pq_scores, sc_copied, sc_free = (
            sem("keys_in"), sem("pq_copied"), sem("pq_scores"), sem("sc_copied"), sem("sc_free"))
        g_shift, g_exp, route_ok, route_tr, route_copied = (
            sem("g_shift"), sem("g_exp"), sem("route_ok"), sem("route_tr"), sem("route_copied"))
        ident_ok, tok_mm, tok_copied = sem("ident_ok"), sem("tok_mm"), sem("tok_copied")
        acc_zero, gath_col, gath_free, gath_gelu, gath_act = (
            sem("acc_zero"), sem("gath_col"), sem("gath_free"), sem("gath_gelu"), sem("gath_act"))
        gath_in = [sem(f"gath_in{i}") for i in range(2)]
        tail_tr, tail_added = sem("tail_tr"), sem("tail_added")
        oh_a, oh_b = sem("oh_a"), sem("oh_b")
        tab_mm, tab_copied = sem("tab_mm"), sem("tab_copied")
        tab_out = [sem(f"tab_out{i}") for i in range(2)]
        wg_in, u_gelu, act_part, act_ok, y_added = (
            sem("wg_in"), sem("u_gelu"), sem("act_part"), sem("act_ok"), sem("y_added"))
        out_done = sem("out_done")
        wait_held, pool_held = sem("wait_held"), sem("pool_held")
        dve_step, pool_step = sem("dve_step"), sem("pool_step")

        def head_place(t, k):
            return arena[:, bass.ds((4 * t + k) * S + (t // 4) * (QC - 2 * HA * S), S)]

        def landed(eng, tile, turn=None, per=0):
            n = 16 * (tile // SLOTS + 1)
            eng.wait_ge(slot_in[tile % SLOTS], n if turn is None else turn * (16 * (per // SLOTS)) + n)

        block = ctx.enter_context(nc.Block())

        @block.sync
        def _(sync):
            def load(tile, src, turn=None, per=0):
                if tile >= SLOTS or turn is not None:
                    n = tile - SLOTS + 1
                    sync.wait_ge(tile_done, n if turn is None else turn * per + n)
                slot = ring[tile % SLOTS][:, :, :].rearrange("p a b -> p (a b)")
                sync.dma_start(slot, src).then_inc(slot_in[tile % SLOTS], 16)

            def row(w, n):
                return w[bass.ds(n, 1)].rearrange("a p n -> p (a n)")

            sync.dma_start(memT, mem_t).then_inc(mem_in, 16)
            load(0, w_memk[0])
            for q in range(4):
                sync.dma_start(xT[:, 4 * q:4 * q + 4, :], x_t[:, 4 * q:4 * q + 4, :]).then_inc(x_in[q], 16)
            for k in range(1, HC):
                load(T_MK + k, w_memk[k])
            for k in range(4):
                load(T_MV + k, w_memv[k])

            def load_half(slot, src):
                sync.dma_start(ring[slot][:, :, :].rearrange("p a b -> p (a b)"), src).then_inc(pair_in[slot], 16)

            for k in range(2):
                sync.wait_ge(tile_done, T_MV + k + 1)
                load_half(k, w_qk[k])

            def load_pairs(w, split, first, turns):
                with sync.Fori(0, turns) as t:
                    for k in range(2):
                        sync.wait_ge(quarter_lo, 8 * t + 4 * (split + k + 1))
                        load_half(k, row(w, 2 * t + first + k))

            load_pairs(w_qk, 0, 2, N_QK // 2 - 1)
            load_pairs(w_lru_in, S_LRU - 2, 0, LC)
            load_pairs(w_v, S_V - 2, 0, 4)
            with sync.Fori(0, KC) as c:
                sync.wait_ge(quarter_lo, 12 * c + 4 * S_MIX)
                load_half(0, row(w_mix, 4 * c))
                sync.wait_ge(tile_done, 4 * c + T_MIX)
                load_half(1, row(w_mix, 4 * c + 1))
                for k in range(2):
                    sync.wait_ge(quarter_lo, 12 * c + 4 * (S_MIX + k + 1))
                    load_half(k, row(w_mix, 4 * c + 2 + k))
            sync.wait_ge(quarter_lo, 4 * S_WO)
            load_half(0, w_o[0])
            sync.wait_ge(tile_done, T_WO - 1)
            for q in range(4):
                sync.dma_start(xT[:, 4 * q:4 * q + 4, :], x_t[:, 4 * q:4 * q + 4, :]).then_inc(x_back, 16)
            sync.wait_ge(tile_done, T_WO)
            load_half(1, w_o[1])
            load_pairs(w_o, S_WO, 2, KC // 2 - 1)

            def load_raw(m, src):
                sync.wait_ge(split_lo, m - 1)
                sync.dma_start(ring[m_slot][:, :, :].rearrange("p a b -> p (a b)"), src).then_inc(raw_in[m_slot], 16)

            for m_slot in range(2):
                sync.wait_ge(quarter_lo, 4 * (S_WO + KC - 1 + m_slot))
                sync.dma_start(ring[m_slot][:, :, :].rearrange("p a b -> p (a b)"), w_pq[m_slot]).then_inc(raw_in[m_slot], 16)
            with sync.Fori(1, PH) as t:
                for m_slot in range(2):
                    load_raw(2 * t + m_slot, row(w_pq, 2 * t + m_slot))
            with sync.Fori(0, NTB // 2) as t:
                for b in range(2):
                    sync.wait_ge(tab_copied, 16 * t + 8 * b + 8)
                    sync.dma_start(table_dram[bass.ds(2 * t + b, 1)].rearrange("a p n -> p (a n)"),
                                   wt[b][:, :, :].rearrange("p a b -> p (a b)")).then_inc(tab_out[b], 16)
            for b in range(2):
                sync.wait_ge(tab_out[b], 16 * (NTB // 2))
            with sync.Fori(0, NG) as g:
                sync.wait_ge(act_ok, JG * g)
                sync.dma_start(wg[:, :, :, :].rearrange("p a b c -> p a (b c)"),
                               table_dram[:, :, bass.ds(JG * TB * g, JG * TB)].rearrange("t p n -> p t n")
                               ).then_inc(wg_in, 16)
                for q in range(16):
                    m_slot = q % 2
                    load_raw(16 * g + 2 * PH + q, row(w_exp, 16 * g + q))
            for b in range(4):
                sync.wait_ge(tail_added, b + 1)
                sync.dma_start(out_t[:, 4 * b:4 * b + 4, :], xT[:, 4 * b:4 * b + 4, :]).then_inc(out_done, 16)
            sync.wait_ge(out_done, 16 * 4)

        @block.gpsimd
        def _(pool):
            nc.gpsimd.memset(ident[:, :], 0.0).then_inc(pool_step, 1)
            pool.iota(iota[:, :], [[1, P]], base=0, channel_multiplier=0,
                      allow_small_or_imprecise_dtypes=True).then_inc(const_made, 1)
            pool.wait_ge(pool_step, 1)
            pool.affine_select(out=ident[:, :], in_=ident[:, :], compare_op=ALU.not_equal, fill=1.0, base=0,
                               pattern=[[-1, P]], channel_multiplier=1).then_inc(const_made, 1)
            nc.gpsimd.memset(xl[:, :, 0:TAPS - 1], 0.0).then_inc(xl_zero, 1)
            nc.gpsimd.memset(lw, 0.0).then_inc(lw_zero, 1)

            def low_part(slot, number):
                for q in range(4):
                    part = slice(4 * q, 4 * q + 4)
                    pool.wait_ge(quarter_hi, 4 * number + q + 1)
                    nc.gpsimd.tensor_tensor(p_lo[:, part, :], ring[slot][:, part, :], p_hi[:, part, :].bitcast(F32),
                                            ALU.subtract).then_inc(quarter_lo, 1)

            with pool.Fori(0, S_MIX // 2) as t:
                for k in range(2):
                    low_part(k, 2 * t + k)
            low_part(0, S_MIX)

            pool.wait_ge(lru_ok, LC)
            pool.wait_ge(head_ok, HC + N_QK)
            pool.wait_ge(v_copied, MT + 2 * TT)
            with pool.Fori(0, HA) as h:
                pool.wait_ge(at_a.mixed, h)
                nc.gpsimd.tensor_copy(qs, qT[:, bass.ds(h, 1), :].rearrange("p a s -> p (a s)")).then_inc(at_a.staged, 1)
                nc.gpsimd.tensor_copy(vs, vA[:, :, bass.ds(h * DH, DH)]).then_inc(at_a.staged, 1)
            with pool.Fori(0, HC) as h:
                pool.wait_ge(at_c.mixed, h)
                pool.wait_ge(at_a.mixed, HA)
                nc.gpsimd.tensor_copy(qs, qkc[:, bass.ds(h, 1), :].rearrange("p a s -> p (a s)")).then_inc(at_c.staged, 1)
                nc.gpsimd.tensor_copy(vs[:, 0:MT, :], mv[:, :, bass.ds(h * DH, DH)]).then_inc(at_c.staged, 1)

            with pool.Fori(0, KC) as c:
                for slot, k in ((1, 1), (0, 2), (0, 3)):
                    low_part(slot, 3 * c + S_MIX + k)

            pool.wait_ge(merged_ok, KC)
            nc.gpsimd.memset(sumsq, 0.0).then_inc(x2_sum, 1)

            def add_square(c):
                pool.wait_ge(x2_ok, c + 1)
                pool.wait_ge(x2_sum, c + 1)
                xk = xT[:, bass.ds(c, 1), :].rearrange("p a s -> p (a s)")
                nc.gpsimd.tensor_tensor(sqx, xk, xk, ALU.mult).then_inc(x2_sq, 1)
                pool.wait_ge(x2_sq, c + 1)
                nc.gpsimd.tensor_tensor(sumsq, sumsq, sqx, ALU.add).then_inc(x2_sum, 1)

            with pool.Fori(0, KC // 2 - 1) as t:
                for k in range(2):
                    low_part(1 - k, 2 * t + S_WO + 1 + k)
                    add_square(2 * t + k)
            low_part(1, S_WO + KC - 1)
            for c in (KC - 2, KC - 1):
                add_square(c)

            with pool.Fori(0, PH) as t:
                for b in range(2):
                    pool.wait_ge(split_hi, 2 * t + b + 1)
                    nc.gpsimd.tensor_tensor(w_lo[b][:, :, :], ring[b][:, :, :], w_hi[b][:, :, :].bitcast(F32),
                                            ALU.subtract).then_inc(split_lo, 1)

            for number, rows in enumerate((u_rows, v_rows)):
                with pool.Fori(0, PAIRS // 2) as t:
                    for b in range(2):
                        pool.wait_ge(gath_free, 2 * t + b + 1 + number * PAIRS)
                        nc.gpsimd.tensor_copy(g_col[b][:, :], g_idx[:, bass.ds(2 * t + b, 1)]).then_inc(gath_col, 1)
                        pool.wait_ge(gath_col, 2 * t + b + 1 + number * PAIRS)
                        pool.sem_inc(pool_held, 1)
                        pool.indirect_dma_start(grow[b][:, :], None, rows, bass.IndirectOffsetOnAxis(g_col[b][:, :], 0)
                                                ).then_inc(gath_in[b], 16)

        @block.scalar
        def _(act_e):
            def f(out, in_, func=ACT.Copy, **kw):
                return nc.scalar.activation(out, in_, func, **kw)

            for dst, src in ((vecs[:, 0:KC], g1), (vecs[:, KC:2 * KC], g2), (vecs[:, 2 * KC:], gmem),
                             (hgain[:, :], head_g), (bgate[:, :], b_gate), (lvec[:, :, :], lru_vec)):
                act_e.dma_start(dst, src).then_inc(vec_in, 16)
            act_e.dma_start(rext[:, P - 1:], rel_rev).then_inc(rel_in, 16)
            act_e.wait_ge(lw_zero, 1)
            for side in range(2):
                for half in range(2):
                    sl = slice(64 * half, 64 * half + 64)
                    act_e.dma_start(lw[sl, side, :, sl], lru_w[side, half]).then_inc(lw_in, 16)

            act_e.wait_ge(mem_in, 16)
            f(msq, memT, ACT.Square).then_inc(mem_sq, 1)
            act_e.wait_ge(const_made, 4)
            act_e.wait_ge(norm_ss, 1)
            f(rt[0][:, 0:MEM], bank[6][:, 0:MEM], ACT.Sqrt, scale=1.0 / D, bias=eps[:, 0:1]).then_inc(norm_rt, 1)
            for q in range(4):
                act_e.wait_ge(x_in[q], 16)
                f(xsq[:, 4 * q:4 * q + 4, :], xT[:, 4 * q:4 * q + 4, :], ACT.Square).then_inc(x_sq, 1)

            def head_root(n, width, number):
                act_e.wait_ge(head_ss, number)
                f(rt[n % 2][:, 0:width], bank[4 + n % 2][:, 0:width], ACT.Sqrt, scale=1.0 / DH,
                  bias=eps[:, 0:1]).then_inc(head_rt, 1)

            for k in range(HC):
                act_e.wait_ge(tile_done, T_MK + k + 1)
                f(mk[:, k, :], bank[k][:, 0:MEM]).then_inc(acc_copied, 1)
                if k >= 2:
                    act_e.wait_ge(head_ss, k - 1)
                f(sq[k % 2][:, 0:MEM], bank[k][:, 0:MEM], ACT.Square).then_inc(head_sq, 1)
                if k >= 2:
                    act_e.wait_ge(head_ok, k - 1)
                if k == 0:
                    act_e.wait_ge(mem_h, KC)
                head_root(k, MEM, k + 1)
            act_e.wait_ge(norm_ss, 2)
            act_e.wait_ge(head_ok, HC)
            f(rt[0], bank[6][:, :], ACT.Sqrt, scale=1.0 / D, bias=eps[:, 0:1]).then_inc(norm_rt, 1)
            for c in range(KC):
                act_e.wait_ge(h_made, c + 1)
                f(norm_hi[:, c, :], hT[:, c, :]).then_inc(h_high, 1)
            act_e.wait_ge(tile_done, T_MV + 4)
            for m in range(MT):
                f(mv[:, m, :], bank[2 + m][:, :]).then_inc(v_copied, 1)

            def high_part(slot, number, tiles, used, quarters=range(4)):
                act_e.wait_ge(pair_in[slot], 16 * tiles)
                for q in quarters:
                    if q < 3:
                        act_e.wait_ge(part_used, 3 * number + q - 2)
                    else:
                        act_e.wait_ge(tile_done, used)
                    part = slice(4 * q, 4 * q + 4)
                    f(p_hi[:, part, :], ring[slot][:, part, :]).then_inc(quarter_hi, 1)

            act_e.wait_ge(tile_done, T_QK)
            act_e.wait_ge(pair_in[0], 16)
            for q in range(4):
                f(p_hi[:, 4 * q:4 * q + 4, :], ring[0][:, 4 * q:4 * q + 4, :]).then_inc(quarter_hi, 1)
            high_part(1, 1, 1, T_QK + 1)

            act_e.wait_ge(h_ready, KC)
            with act_e.Fori(0, N_QK // 4) as t:
                for k in range(4):
                    act_e.wait_ge(tile_done, 4 * t + T_QK + k + 1)
                    f(head_place(t, k), bank[k][:, :]).then_inc(acc_copied, 1)
                    act_e.wait_ge(head_ss, 4 * t + k + HC - 1)
                    f(sq[k % 2], bank[k][:, :], ACT.Square).then_inc(head_sq, 1)
                    ahead = (k % 2, 4 * t + k + 2, 2 * t + k // 2 + 2, 4 * t + T_QK + k + 2)
                    high_part(*ahead, quarters=(0,))
                    act_e.wait_ge(head_ok, 4 * t + k + HC - 1)
                    head_root(k, S, 4 * t + k + HC + 1)
                    high_part(*ahead, quarters=(1, 2, 3))

            def two_ahead(n):
                high_part(n % 2, n + 2 - T_QK, (n - T_QK) // 2 + 2, n + 2)

            act_e.wait_ge(xl_zero, 1)
            for k in range(LC):
                act_e.wait_ge(tile_done, T_LRU + k + 1)
                f(xl[:, k, TAPS - 1:], bank[k][:, :]).then_inc(lin_copied, 1)
                two_ahead(T_LRU + k)
            for k in range(LC):
                act_e.wait_ge(tile_done, T_LRU + LC + k + 1)
                f(gl[:, k, :], bank[k][:, :], ACT.Gelu_apprx_tanh).then_inc(lin_copied, 1)
                two_ahead(T_LRU + LC + k)
            act_e.wait_ge(vec_in, 16 * 6)
            act_e.wait_ge(lam_abs, 1)
            f(sp[:, 1, :], sp[:, 0, :], ACT.Exp, scale=-1.0).then_inc(lam_exp, 1)
            for half in range(2):
                for n in range(3):
                    two_ahead(T_V + 4 * half + n)
                act_e.wait_ge(tile_done, T_V + 4 * half + 4)
                for m in range(TT):
                    f(vA[:, m, 512 * half:512 * half + 512], bank[4 * (1 - half) + m][:, :]).then_inc(v_copied, 1)
                if half == 0:
                    two_ahead(T_V + 3)
            act_e.wait_ge(conv_ok, LC)
            for side, dst in ((0, rg), (1, ig)):
                for k in range(LC):
                    act_e.wait_ge(lru_mm, LC * side + k + 1)
                    f(dst[:, k, :], bank[LC * side + k][:, :], ACT.Sigmoid,
                      bias=lvec[:, 5 + side, k:k + 1]).then_inc(lru_sig, 1)
            act_e.wait_ge(sp_ok, 1)
            act_e.wait_ge(lru_sig, LC)
            for k in range(LC):
                f(rg[:, k, :], rg[:, k, :], ACT.Tanh, scale=sp[:, 5, k:k + 1]).then_inc(lru_tanh, 1)
            for k in range(LC):
                act_e.wait_ge(lru_m2, k + 1)
                f(rg[:, k, :], rg[:, k, :], ACT.Sqrt).then_inc(lru_mult, 1)

            act_e.wait_ge(rel_filled, 1)
            act_e.dma_start(rel_dram.ap().rearrange("p h n -> h p n"),
                            rext[:, :].unsqueeze(1).to_broadcast([HA, P, EXT])).then_inc(rel_out, 16)
            act_e.wait_ge(rel_out, 16)
            act_e.wait_ge(lru_ok, LC)
            act_e.dma_start(tb, bass.AP(rel_dram, P - 1, [[HA * EXT - 1, P], [EXT, HA], [1, 2 * P]])).then_inc(bias_in, 16)

            def attention(a, turns, tiles, s_width, exp_in):
                with act_e.Fori(0, turns) as h:
                    for q in range(TT):
                        act_e.wait_ge(a.shifted, TT * h + q + 1)
                        w = s_width(q)
                        f(s_sb[:, q, 0:w], exp_in(q, w), ACT.Exp, bias=nmax[:, q:q + 1],
                          scale=1.0 if a is at_a else SCALE, accum_out=ssum[:, q:q + 1]).then_inc(a.exped, 1)
                    for kt in range(tiles):
                        act_e.wait_ge(a.turned, tiles * h + kt + 1)
                        act_e.wait_ge(a.mixed, h)
                        dst = pT[kt] if a is at_a else pTc[kt]
                        f(dst, bank[4 + kt][:, 0:dst.shape[-1]]).then_inc(a.probsT, 1)

            attention(at_a, HA, TT, lambda q: (q + 1) * P, lambda q, w: s_sb[:, q, 0:w])
            attention(at_c, HC, MT, lambda q: MEM, lambda q, w: bank[q][:, 0:w])

            with act_e.Fori(0, KC) as c:
                for b in range(3):
                    slot, tiles = ((1, 1), (0, 2), (0, 3))[b]
                    high_part(slot, 3 * c + S_MIX + b + 1, 2 * c + S_MIX // 2 + tiles, 4 * c + T_MIX + b + 1)
                    act_e.wait_ge(tile_done, 4 * c + T_MIX + b + 1)
                    if b == 0:
                        act_e.wait_ge(merged_ok, c)
                    f(sig[:, b, :], bank[b][:, :], ACT.Sigmoid, bias=bgate[:, bass.ds(KC * b + c, 1)]
                      ).then_inc(gate_ok, 1)

            for c in range(KC):
                act_e.wait_ge(merged_ok, c + 1)
                f(h_hi[:, c, :], merged[:, c, :]).then_inc(m_hi_ok, 1)
            with act_e.Fori(0, KC // 2 - 1) as t:
                for k in range(2):
                    high_part(1 - k, 2 * t + S_WO + 1 + k, t + (S_MIX + 4 * KC) // 2 + 1 + k, 2 * t + T_WO + k + 1)
            high_part(1, S_WO + KC - 1, (S_MIX + 4 * KC + KC) // 2, T_WO + KC - 1)

            act_e.wait_ge(tile_done, T_WO)
            act_e.dma_start(kys, keys).then_inc(keys_in, 16)
            act_e.wait_ge(norm_ss, 3)
            f(rt2, bank[6][:, :], ACT.Sqrt, scale=1.0 / D, bias=eps[:, 0:1]).then_inc(norm_rt, 1)

            for c in range(KC):
                act_e.wait_ge(h2_made, c + 1)
                f(h_hi[:, c, :], h2[c % 2]).then_inc(h2_hi, 1)

            def high(n, b, free):
                act_e.wait_ge(raw_in[b], 16 * (n // 2) + 16)
                if free:
                    act_e.wait_ge(tile_done, n + T_PQ - 1)
                f(w_hi[b][:, :, :], ring[b][:, :, :]).then_inc(split_hi, 1)

            high(0, 0, False)
            high(1, 1, False)
            act_e.wait_ge(keys_in, 16)

            def queries(t, last):
                for k in range(4):
                    act_e.wait_ge(tile_done, 4 * t + T_PQ + k + 1)
                    act_e.wait_ge(pq_scores, 4 * t)
                    f(qp[:, k, :], bank[k][:, :]).then_inc(pq_copied, 1)
                    if not (last and k >= 2):
                        high_in_turn(t, k)
                    act_e.wait_ge(pq_scores, 4 * t + k + 1)
                    act_e.wait_ge(sc_free, 4 * t + k + 1)
                    f(sc[:, k, :, :], bank[4 + k][:, :].rearrange("p (a b) -> p a b", a=TT)).then_inc(sc_copied, 1)

            def high_in_turn(t, k):
                b = k % 2
                act_e.wait_ge(raw_in[b], 32 * t + 16 * (k // 2 + 1) + 16)
                act_e.wait_ge(tile_done, 4 * t + T_PQ + k + 1)
                f(w_hi[b][:, :, :], ring[b][:, :, :]).then_inc(split_hi, 1)

            with act_e.Fori(0, PH // 2 - 1) as t:
                queries(t, False)
            queries(PH // 2 - 1, True)

            act_e.wait_ge(tok_mm, 1)
            for b in range(4):
                f(h_tok[:, 4 * b:4 * b + 4, :], bank[b][:, :].rearrange("p (a n) -> p a n", a=4)).then_inc(tok_copied, 1)
            act_e.wait_ge(g_shift, 1)
            gv = route[:, 2, :, :, :].rearrange("p m h k -> p (m h k)")
            f(gv, gv, ACT.Exp).then_inc(g_exp, 1)
            for k in range(3):
                act_e.wait_ge(route_tr, k + 1)
                f(routeT[:, k, :], bank[4 + k][:, 0:ND]).then_inc(route_copied, 1)

            with act_e.Fori(0, NTB // 2) as t:
                for b in range(2):
                    act_e.wait_ge(tab_out[b], 16 * t)
                    for q in range(8):
                        act_e.wait_ge(tab_mm, 16 * t + 8 * b + q + 1)
                        f(wt[b][:, :, 4 * q:4 * q + 4].rearrange("p j t -> p t j"),
                          bank[q][:, :].rearrange("p (t j) -> p t j", t=4)).then_inc(tab_copied, 1)
            for b in range(2):
                act_e.wait_ge(tab_out[b], 16 * (NTB // 2))

            for m in range(2 * PH, 2 * PH + 2):
                high(m, m % 2, True)

            def experts(g, last):
                for q in range(16):
                    act_e.wait_ge(tile_done, 16 * g + T_EXP + q + 1)
                    if q < JG:
                        act_e.wait_ge(act_ok, JG * g + max(q - 1, 0))
                        f(gel[q % 2][:, :], bank[q % 4][:, 0:ND], ACT.Gelu_apprx_tanh).then_inc(u_gelu, 1)
                    if not (last and q >= 14):
                        act_e.wait_ge(raw_in[q % 2], 128 * g + 16 * (PH + q // 2 + 1) + 16)
                        f(w_hi[q % 2][:, :, :], ring[q % 2][:, :, :]).then_inc(split_hi, 1)

            with act_e.Fori(0, NG // 2) as g:
                experts(g, False)
            act_e.wait_ge(gath_free, 2 + PAIRS)
            f(g_act[:, :], g_dot[:, :], ACT.Gelu_apprx_tanh).then_inc(gath_gelu, 1)
            with act_e.Fori(NG // 2, NG - 1) as g:
                experts(g, False)
            experts(NG - 1, True)

        @block.vector
        def _(dve):
            v = nc.vector
            st = Steps(dve, dve_step)

            v.memset(ones[:, :], 1.0).then_inc(const_made, 1)
            v.memset(eps[:, :], EPS).then_inc(const_made, 1)

            dve.wait_ge(vec_in, 16 * 6)
            dve.wait_ge(norm_rt, 1)
            st.did(v.reciprocal(rt[0][:, 0:MEM], rt[0][:, 0:MEM]))
            st.wait()
            for c in range(KC):
                v.scalar_tensor_tensor(out=memT[:, c, :], in0=memT[:, c, :], scalar=vecs[:, 2 * KC + c:2 * KC + c + 1],
                                       in1=rt[0][:, 0:MEM], op0=ALU.mult, op1=ALU.mult).then_inc(mem_h, 1)

            dve.wait_ge(rel_in, 16)
            v.tensor_copy(rext[:, 0:P - 1], rext[:, P - 1:P].to_broadcast([HA, P - 1])).then_inc(rel_filled, 1)

            lam = lvec[:, 7, :]
            v.scalar_tensor_tensor(out=sp[:, 0, :], in0=lam, scalar=-1.0, in1=lam, op0=ALU.mult, op1=ALU.max).then_inc(lam_abs, 1)

            def head_norm(n, dst, width, gain, number):
                dve.wait_ge(head_rt, number)
                r = rt[n % 2][:, 0:width]
                st.did(v.reciprocal(r, r))
                st.wait()
                v.scalar_tensor_tensor(out=dst, in0=dst, scalar=gain, in1=r, op0=ALU.mult, op1=ALU.mult
                                       ).then_inc(head_ok, 1)

            for k in range(HC):
                head_norm(k, mk[:, k, :], MEM, hgain[:, 3:4], k + 1)

            dve.wait_ge(norm_rt, 2)
            st.did(v.reciprocal(rt[0], rt[0]))
            st.wait()
            for c in range(KC + 1):
                if c < KC:
                    v.scalar_tensor_tensor(out=hT[:, c, :], in0=xT[:, c, :], scalar=vecs[:, c:c + 1],
                                           in1=rt[0], op0=ALU.mult, op1=ALU.mult).then_inc(h_made, 1)
                if c:
                    dve.wait_ge(h_high, c)
                    v.tensor_tensor(norm_lo[:, c - 1, :], hT[:, c - 1, :], norm_hi[:, c - 1, :].bitcast(F32),
                                    ALU.subtract).then_inc(h_ready, 1)

            with dve.Fori(0, N_QK // 4) as t:
                st.loop(t, 4)
                for k in range(4):
                    head_norm(k, head_place(t, k), S, hgain[:, bass.ds(t // 2, 1)], 4 * t + k + HC + 1)
                st.end(N_QK // 4)

            dve.wait_ge(lam_exp, 1)
            y, z, z2, s4 = sp[:, 1, :], sp[:, 2, :], sp[:, 3, :], sp[:, 4, :]

            def step(ins):
                st.did(ins)
                st.wait()

            step(v.tensor_scalar(z, y, 2.0, None, ALU.add))
            step(v.reciprocal(z, z))
            step(v.tensor_tensor(z, z, y, ALU.mult))
            step(v.tensor_tensor(z2, z, z, ALU.mult))
            step(v.memset(s4, 1.0 / 17))
            for odd in (15, 13, 11, 9, 7, 5, 3, 1):
                step(v.tensor_tensor(s4, s4, z2, ALU.mult))
                step(v.tensor_scalar(s4, s4, 1.0 / odd, None, ALU.add))
            step(v.tensor_tensor(s4, s4, z, ALU.mult))
            step(v.tensor_scalar(s4, s4, 8.0, None, ALU.mult))
            step(v.tensor_scalar(z, lam, -4.0, 0.0, ALU.mult, ALU.max))
            v.tensor_tensor(sp[:, 5, :], s4, z, ALU.add).then_inc(sp_ok, 1)

            for k in range(LC):
                dve.wait_ge(lin_copied, k + 1)
                step(v.tensor_scalar(xc[:, k, :], xl[:, k, 0:S], lvec[:, 0, k:k + 1], lvec[:, 4, k:k + 1],
                                     ALU.mult, ALU.add))
                for tap in range(1, TAPS):
                    ins = v.scalar_tensor_tensor(out=xc[:, k, :], in0=xl[:, k, tap:tap + S], scalar=lvec[:, tap, k:k + 1],
                                                 in1=xc[:, k, :], op0=ALU.mult, op1=ALU.add)
                    if tap < TAPS - 1:
                        step(ins)
                    else:
                        ins.then_inc(conv_ok, 1)

            dve.wait_ge(conv_ok, LC)
            dve.wait_ge(lw_in, 64)
            for k in range(LC):
                t, u = rg[:, k, :], ig[:, k, :]
                dve.wait_ge(lru_tanh, k + 1)
                dve.wait_ge(lru_mm, 2 * LC)
                step(v.tensor_scalar(lr, t, 1.0, None, ALU.add))
                step(v.reciprocal(lr, lr))
                step(v.tensor_scalar(la, t, -1.0, 1.0, ALU.mult, ALU.add))
                step(v.tensor_tensor(la, la, lr, ALU.mult))
                step(v.scalar_tensor_tensor(out=t, in0=t, scalar=4.0, in1=lr, op0=ALU.mult, op1=ALU.mult))
                step(v.tensor_tensor(t, t, lr, ALU.mult))
                v.tensor_scalar(t, t, 1e-12, 1.0, ALU.max, ALU.min).then_inc(lru_m2, 1)
                dve.wait_ge(lru_sig, LC + k + 1)
                step(v.tensor_tensor(u, u, xc[:, k, :], ALU.mult))
                dve.wait_ge(lru_mult, k + 1)
                step(v.tensor_tensor(u, u, t, ALU.mult))
                step(v.tensor_tensor_scan(out=xc[:, k, :], data0=la, data1=u, initial=0.0, op0=ALU.mult, op1=ALU.add))
                dve.wait_ge(lin_copied, 2 * LC)
                v.tensor_tensor(gl[:, k, :], gl[:, k, :], xc[:, k, :], ALU.mult).then_inc(lru_ok, 1)

            dve.wait_ge(bias_in, 16)
            v.memset(tb[0:CHUNK, :, 2 * P - CHUNK:], NEG).then_inc(bias_ok, 1)
            dve.wait_ge(bias_ok, 1)

            def soften(a, h, q, w):
                dve.wait_ge(a.exped, TT * h + q + 1)
                st.did(v.reciprocal(rinv[:, q:q + 1], ssum[:, q:q + 1]))
                st.wait()
                v.tensor_scalar(s_sb[:, q, 0:w], s_sb[:, q, 0:w], rinv[:, q:q + 1], None, ALU.mult).then_inc(a.probs, 1)

            with dve.Fori(0, HA) as h:
                st.loop(h, 2 * TT + 2)
                dve.wait_ge(at_a.turned, TT * h)
                for q in range(TT):
                    dve.wait_ge(at_a.scores, TT * h + q + 1)
                    near = max(q - 1, 0) * P
                    w = (q + 1) * P
                    if near:
                        st.did(v.tensor_scalar(s_sb[:, q, 0:near], bank[q][:, 0:near], SCALE,
                                               tb[:, bass.ds(h, 1), 0:1].rearrange("p a b -> p (a b)"), ALU.mult, ALU.add))
                    v.scalar_tensor_tensor(
                        out=s_sb[:, q, near:w], in0=bank[q][:, near:w], scalar=SCALE,
                        in1=tb[:, bass.ds(h, 1), 2 * P - (w - near):].rearrange("p a b -> p (a b)"),
                        op0=ALU.mult, op1=ALU.add).then_inc(at_a.taken, 1)
                    st.wait()
                    dve.wait_ge(at_a.taken, TT * h + q + 1)
                    st.did(v.reduce_max(smax[:, q:q + 1], s_sb[:, q, 0:w], AX_X))
                    st.wait()
                    v.tensor_scalar(nmax[:, q:q + 1], smax[:, q:q + 1], -1.0, None, ALU.mult).then_inc(at_a.shifted, 1)
                    if q:
                        soften(at_a, h, q - 1, q * P)
                soften(at_a, h, TT - 1, S)
                dve.wait_ge(at_a.mixed, h + 1)
                dve.wait_ge(at_a.scores, TT * h + TT)
                v.tensor_scalar(qT[:, bass.ds(h, 1), :].rearrange("p a s -> p (a s)"), bank[0][:, :], 1.0, None,
                                ALU.mult).then_inc(at_a.out, 1)
                st.end(HA)

            with dve.Fori(0, HC) as h:
                st.loop(h, 2 * TT)
                dve.wait_ge(at_c.turned, MT * h)
                for q in range(TT):
                    dve.wait_ge(at_c.scores, TT * h + q + 1)
                    st.did(v.reduce_max(smax[:, q:q + 1], bank[q][:, 0:MEM], AX_X))
                    st.wait()
                    v.tensor_scalar(nmax[:, q:q + 1], smax[:, q:q + 1], -SCALE, None, ALU.mult).then_inc(at_c.shifted, 1)
                    if q:
                        soften(at_c, h, q - 1, MEM)
                soften(at_c, h, TT - 1, MEM)
                dve.wait_ge(at_c.mixed, h + 1)
                v.tensor_scalar(qkc[:, bass.ds(h, 1), :].rearrange("p a s -> p (a s)"), bank[0][:, :], 1.0, None,
                                ALU.mult).then_inc(at_c.out, 1)
                st.end(HC)

            with dve.Fori(0, KC) as c:
                st.loop(c, 1)
                dve.wait_ge(tile_done, 4 * c + T_MIX + 4)
                for b in range(3):
                    dve.wait_ge(gate_ok, 3 * c + b + 1)
                    v.tensor_tensor(prod[:, b, :], sig[:, b, :], bank[3 + b][:, :], ALU.mult).then_inc(y_used, 1)
                dve.wait_ge(y_used, 3 * c + 3)
                st.did(v.tensor_tensor(prod[:, 0, :], prod[:, 0, :], prod[:, 1, :], ALU.add))
                st.wait()
                v.tensor_tensor(merged[:, bass.ds(c, 1), :].rearrange("p a s -> p (a s)"), prod[:, 0, :], prod[:, 2, :],
                                ALU.add).then_inc(merged_ok, 1)
                st.end(KC)

            for c in range(KC):
                dve.wait_ge(m_hi_ok, c + 1)
                v.tensor_tensor(h_lo[:, c, :], merged[:, c, :], h_hi[:, c, :].bitcast(F32), ALU.subtract
                                ).then_inc(m_ready, 1)

            dve.wait_ge(x_back, 64)
            with dve.Fori(0, KC // 4) as t:
                for k in range(4):
                    dve.wait_ge(tile_done, 4 * t + T_WO + k + 1)
                    xk = xT[:, bass.ds(4 * t + k, 1), :].rearrange("p a s -> p (a s)")
                    v.tensor_tensor(xk, xk, bank[k][:, :], ALU.add).then_inc(x2_ok, 1)
            dve.wait_ge(norm_rt, 3)
            step(v.reciprocal(rt2, rt2))
            for c in range(KC + 1):
                if c < KC:
                    if c >= 2:
                        dve.wait_ge(h2_ready, c - 1)
                    v.scalar_tensor_tensor(out=h2[c % 2], in0=xT[:, c, :], scalar=vecs[:, KC + c:KC + c + 1],
                                           in1=rt2, op0=ALU.mult, op1=ALU.mult).then_inc(h2_made, 1)
                if c:
                    dve.wait_ge(h2_hi, c)
                    v.tensor_tensor(h_lo[:, c - 1, :], h2[(c - 1) % 2], h_hi[:, c - 1, :].bitcast(F32), ALU.subtract
                                    ).then_inc(h2_ready, 1)
            dve.wait_ge(const_made, 4)
            v.tensor_copy(ident_r[:, :], ident[:, :]).then_inc(ident_ok, 1)
            dve.sem_inc(sc_free, 4)

            def best16(groups):
                def pause():
                    st.wait()
                    dve.sem_inc(wait_held, 1)

                dve.sem_inc(wait_held, 1)
                for half in (slice(0, 8), slice(8, 16)):
                    for s, val, idx in groups:
                        st.did(v.max(val[:, half], s))
                    pause()
                    for s, val, idx in groups:
                        st.did(v.max_index(idx[:, half], val[:, half], s))
                    pause()
                    if half.start == 0:
                        for s, val, idx in groups:
                            st.did(v.match_replace(s, val[:, half], s, LOWEST))
                        pause()

            with dve.Fori(0, PH // 2) as t:
                st.loop(t, 2 * (15 * TT + 12))
                for e in range(2):
                    for side in range(2):
                        k = 2 * e + side
                        dve.wait_ge(sc_copied, 4 * t + k + 1)
                        best16([(sc[:, k, m, :], sv[:, e, side, m, :], si[:, e, side, m, :]) for m in range(TT)])
                        dve.sem_inc(sc_free, 1)
                    step(v.tensor_tensor(cand, sv[:, e, 0, :, :].unsqueeze(3).to_broadcast([P, TT, TOPK, TOPK]),
                                         sv[:, e, 1, :, :].unsqueeze(2).to_broadcast([P, TT, TOPK, TOPK]), ALU.add))
                    best16([(cand[:, m, :, :].rearrange("p a b -> p (a b)"), fv[:, m, :], fpos[:, m, :]) for m in range(TT)])
                    pos = fpos.rearrange("p a b -> p (a b)")
                    st.did(v.tensor_scalar(fa, pos, 4, None, ALU.logical_shift_right))
                    step(v.tensor_scalar(fb, pos, TOPK - 1, None, ALU.bitwise_and))
                    for side, which in ((0, fa), (1, fb)):
                        st.did(v.tensor_tensor(pick[:, side, :, :], which.unsqueeze(2).to_broadcast([P, TT * TOPK, TOPK]),
                                               iota[:, 0:TOPK].unsqueeze(1).to_broadcast([P, TT * TOPK, TOPK]), ALU.is_equal))
                    st.wait()
                    for side in range(2):
                        pk = pick[:, side, :, :].rearrange("p (m k) n -> p m k n", m=TT)
                        st.did(v.tensor_tensor(pk, pk, si[:, e, side, :, :].unsqueeze(2).to_broadcast([P, TT, TOPK, TOPK]), ALU.mult))
                    st.wait()
                    for side, dst in ((0, ires), (1, jres)):
                        st.did(v.reduce_sum(dst.rearrange("p m k -> p (m k)"), pick[:, side, :, :], AX_X))
                    st.wait()
                    for which, src in ((0, ires), (1, jres), (2, fv)):
                        dst = route[:, which, :, bass.ds(2 * t + e, 1), :].rearrange("p m a k -> p m (a k)")
                        st.did(v.tensor_scalar(dst, src, 0.0, None, ALU.add))
                    st.wait()
                st.end(PH // 2)

            gv = route[:, 2, :, :, :].rearrange("p m h k -> p (m h) k")
            step(v.reduce_max(gmx, gv, AX_X))
            v.tensor_tensor(gv, gv, gmx.unsqueeze(2).to_broadcast([P, TT * PH, TOPK]), ALU.subtract).then_inc(g_shift, 1)
            dve.wait_ge(g_exp, 1)
            step(v.reduce_sum(gsum, gv, AX_X))
            step(v.reciprocal(grec, gsum))
            v.tensor_tensor(gv, gv, grec.unsqueeze(2).to_broadcast([P, TT * PH, TOPK]), ALU.mult).then_inc(route_ok, 1)

            gi, gj, gw = (route[:, w, TG, :, :].rearrange("p h k -> p (h k)") for w in range(3))
            step(v.scalar_tensor_tensor(out=g_idx[:, :], in0=gi, scalar=float(NKEYS), in1=gj, op0=ALU.mult, op1=ALU.add))
            step(v.tensor_copy(g_w[:, :], gw))
            dve.wait_ge(route_tr, 3)
            dve.sem_inc(gath_free, 2)
            dve.wait_ge(tok_mm, 1)
            v.memset(g_acc, 0.0).then_inc(acc_zero, 1)

            dve.wait_ge(route_copied, 3)

            def one_hots(t, first):
                for q in range(4):
                    if not first or q >= 2:
                        dve.wait_ge(tab_mm, 8 * t + 2 * q - 2)
                    v.tensor_tensor(ohA[q % 2][:, :, :], iota[:, :].unsqueeze(1).to_broadcast([P, HT, P]),
                                    routeT[:, 0, bass.ds(TB * t + HT * q, HT)].unsqueeze(2).to_broadcast([P, HT, P]),
                                    ALU.is_equal).then_inc(oh_a, 1)
                    for n in range(HT):
                        tok = TB * t + HT * q + n
                        ins = v.tensor_scalar(ohB[q % 2][:, n, :], iota[:, :], routeT[:, 1, bass.ds(tok, 1)],
                                              routeT[:, 2, bass.ds(tok, 1)], ALU.is_equal, ALU.mult)
                    ins.then_inc(oh_b, 1)

            one_hots(0, True)
            with dve.Fori(1, NTB) as t:
                one_hots(t, False)

            def low(b, number):
                dve.wait_ge(split_hi, number)
                v.tensor_tensor(w_lo[b][:, :, :], ring[b][:, :, :], w_hi[b][:, :, :].bitcast(F32), ALU.subtract
                                ).then_inc(split_lo, 1)

            for m in range(2 * PH, 2 * PH + 2):
                low(m % 2, m + 1)
            dve.wait_ge(tok_copied, 4)

            def dot(g, q):
                dve.wait_ge(gath_in[q % 2], 128 * g + 16 * (q // 2) + 16)
                row = grow[q % 2][:, :].rearrange("p (a n) -> p a n", a=KC)
                v.scalar_tensor_tensor(out=row, in0=row, scalar=1.0, in1=h_tok, op0=ALU.mult, op1=ALU.mult,
                                       accum_out=g_dot[:, bass.ds(16 * g + q, 1)]).then_inc(gath_free, 1)

            def gather_add(g, q):
                dve.wait_ge(gath_in[q % 2], 128 * g + 16 * (q // 2) + 16)
                dve.wait_ge(gath_free, 16 * g + q + 2)
                row = grow[q % 2][:, :].rearrange("p (a n) -> p a n", a=KC)
                v.scalar_tensor_tensor(out=g_acc, in0=row, scalar=g_act[:, bass.ds(16 * g + q - PAIRS, 1)], in1=g_acc,
                                       op0=ALU.mult, op1=ALU.add).then_inc(gath_free, 1)

            def experts(g, last, gathered):
                dve.wait_ge(wg_in, 16 * g + 16)
                for q in range(16):
                    if q < JG:
                        dve.wait_ge(u_gelu, JG * g + q + 1)
                        prod = gel[q % 2][:, :]
                        v.tensor_tensor(prod.rearrange("p (a b) -> p a b", a=NTB), prod.rearrange("p (a b) -> p a b", a=NTB),
                                        wg[:, :, q, :], ALU.mult).then_inc(act_part, 1)
                        dve.wait_ge(act_part, 2 * JG * g + 2 * q + 1)
                        v.tensor_copy(act_hi[:, q, :], prod).then_inc(act_part, 1)
                        dve.wait_ge(act_part, 2 * JG * g + 2 * q + 2)
                        v.tensor_tensor(act_lo[:, q, :], prod, act_hi[:, q, :].bitcast(F32), ALU.subtract).then_inc(act_ok, 1)
                    else:
                        dve.wait_ge(tile_done, 16 * g + T_EXP + q + 1)
                        for c in (2 * (q - JG), 2 * (q - JG) + 1):
                            v.tensor_tensor(xT[:, c, 0:ND], xT[:, c, 0:ND], bank[4 + c % 4][:, 0:ND], ALU.add
                                            ).then_inc(y_added, 1)
                    if not (last and q >= 14):
                        low(q % 2, 16 * g + q + 2 * PH + 3)
                    gathered(g, q)

            with dve.Fori(0, NG // 2) as g:
                experts(g, False, dot)
            dve.wait_ge(gath_gelu, 1)
            v.tensor_tensor(g_act[:, :], g_act[:, :], g_w[:, :], ALU.mult).then_inc(gath_act, 1)
            dve.wait_ge(gath_act, 1)
            dve.wait_ge(acc_zero, 1)
            with dve.Fori(NG // 2, NG - 1) as g:
                experts(g, False, gather_add)
            experts(NG - 1, True, gather_add)
            for b in range(4):
                dve.wait_ge(tail_tr, b + 1)
                v.tensor_tensor(xT[:, 4 * b:4 * b + 4, ND:], xT[:, 4 * b:4 * b + 4, ND:],
                                bank[b][:, :].rearrange("p (a n) -> p a n", a=4), ALU.add).then_inc(tail_added, 1)

        @block.tensor
        def _(pe):
            def mm(out, lhsT, rhs, start=True, stop=True):
                return nc.tensor.matmul(out, lhsT, rhs, start=start, stop=stop)

            def project(n, out, rhs, turn=None, per=0, ks=range(KC), inc=True):
                landed(pe, n, turn, per)
                for k in ks:
                    ins = mm(out, ring[n % SLOTS][:, k, :], rhs(k), start=(k == ks[0]), stop=(k == ks[-1]))
                if inc:
                    ins.then_inc(tile_done, 1)

            def head_sum(n, width, number):
                pe.wait_ge(head_sq, number)
                mm(bank[4 + n % 2][:, 0:width], ones[:, :], sq[n % 2][:, 0:width]).then_inc(head_ss, 1)

            pe.wait_ge(const_made, 4)
            pe.wait_ge(mem_sq, 1)
            for c in range(KC):
                ins = mm(bank[6][:, 0:MEM], ones[:, :], msq[:, c, :], start=(c == 0), stop=(c == KC - 1))
            ins.then_inc(norm_ss, 1)
            pe.wait_ge(mem_h, KC)
            for k in range(HC):
                project(T_MK + k, bank[k][:, 0:MEM], lambda c: memT[:, c, :])
                if k:
                    if k >= 3:
                        pe.wait_ge(head_rt, k - 2)
                    head_sum(k - 1, MEM, k)
            for c in range(KC):
                pe.wait_ge(x_sq, c // 4 + 1)
                ins = mm(bank[6][:, :], ones[:, :], xsq[:, c, :], start=(c == 0), stop=(c == KC - 1))
            ins.then_inc(norm_ss, 1)
            pe.wait_ge(head_rt, HC - 2)
            head_sum(HC - 1, MEM, HC)

            pe.wait_ge(acc_copied, HC)
            pe.wait_ge(head_sq, HC)
            for n in range(4):
                landed(pe, T_MV + n)
                w = ring[n][:, :, :].rearrange("p (c a) b -> p c (a b)", c=4)
                for c in range(4):
                    for m in range(MT):
                        ins = mm(bank[2 + m][:, :], memT[:, 4 * n + c, m * P:(m + 1) * P], w[:, c, :],
                                 start=(n == 0 and c == 0), stop=(n == 3 and c == 3))
                ins.then_inc(tile_done, 1)

            def split_mm(out, wh, wl, rh, rl, start, stop):
                mm(out, wh, rh, start=start, stop=False)
                mm(out, wh, rl, start=False, stop=False)
                return mm(out, wl, rh, start=False, stop=stop)

            def project_split(number, out, r_hi, r_lo, between=None):
                for q in range(4):
                    pe.wait_ge(quarter_lo, 4 * number + q + 1)
                    for c in range(4 * q, 4 * q + 4):
                        ins = split_mm(out, p_hi[:, c, :], p_lo[:, c, :], r_hi[:, c, :], r_lo[:, c, :], c == 0, c == KC - 1)
                    ins.then_inc(part_used if q < 3 else tile_done, 1)
                    if q == 0 and between is not None:
                        between()

            pe.wait_ge(h_ready, KC)
            pe.wait_ge(v_copied, MT)
            pe.wait_ge(head_rt, HC)

            def last_head(t, k):
                pe.wait_ge(head_rt, 4 * t + k + HC - 2)
                head_sum((k - 1) % 4, S, 4 * t + k + HC)

            def heads(t, first):
                for k in range(4):
                    if not first:
                        pe.wait_ge(head_sq, 4 * t + HC + k - 3)
                    project_split(4 * t + k, bank[k][:, :], norm_hi, norm_lo,
                                  None if first and k == 0 else lambda: last_head(t, k))

            heads(0, True)
            with pe.Fori(1, N_QK // 4) as t:
                heads(t, False)
            for k in range(2 * LC):
                if k < LC:
                    pe.wait_ge(head_sq, HC + N_QK - LC + k + 1)
                else:
                    pe.wait_ge(lin_copied, k - LC + 1)
                project_split(S_LRU + k, bank[k % LC][:, :], norm_hi, norm_lo,
                              (lambda: last_head(N_QK // 4, 0)) if k == 0 else None)
            pe.wait_ge(head_rt, HC + N_QK)
            for half in range(2):
                if half:
                    pe.wait_ge(lin_copied, 2 * LC)
                for n in range(4):
                    wh, wl = (w[:, :, :].rearrange("p (c a) b -> p c (a b)", c=4) for w in (p_hi, p_lo))
                    for c in range(4):
                        pe.wait_ge(quarter_lo, 4 * (S_V + 4 * half + n) + c + 1)
                        for m in range(TT):
                            tok = slice(m * P, (m + 1) * P)
                            ins = split_mm(bank[4 * (1 - half) + m][:, :], norm_hi[:, 4 * n + c, tok], norm_lo[:, 4 * n + c, tok],
                                           wh[:, c, :], wl[:, c, :], n == 0 and c == 0, n == 3 and c == 3)
                        ins.then_inc(part_used if c < 3 else tile_done, 1)
            pe.wait_ge(lw_in, 64)
            pe.wait_ge(conv_ok, LC)
            pe.wait_ge(v_copied, MT + 2 * TT)
            for side in range(2):
                for k in range(LC):
                    mm(bank[LC * side + k][:, :], lw[:, side, k, :], xc[:, k, :]).then_inc(lru_mm, 1)

            pe.wait_ge(lru_sig, 2 * LC)
            with pe.Fori(0, HA) as h:
                pe.wait_ge(at_a.staged, 2 * h + 2)
                for q in range(TT):
                    pe.wait_ge(at_a.out, h)
                    mm(bank[q][:, 0:(q + 1) * P], qs[:, q * P:(q + 1) * P],
                       kT[:, bass.ds(h, 1), 0:(q + 1) * P].rearrange("p a s -> p (a s)")).then_inc(at_a.scores, 1)
                pe.wait_ge(at_a.probsT, TT * h)
                for q in range(TT):
                    pe.wait_ge(at_a.probs, TT * h + q + 1)
                    for kt in range(q + 1):
                        ins = nc.tensor.transpose(bank[4 + kt][:, (q - kt) * P:(q - kt + 1) * P],
                                                  s_sb[:, q, kt * P:(kt + 1) * P], ident[:, :])
                        if q == TT - 1:
                            ins.then_inc(at_a.turned, 1)
                for kt in range(TT):
                    pe.wait_ge(at_a.probsT, TT * h + kt + 1)
                    ins = mm(bank[0][:, kt * P:], vs[:, kt, :], pT[kt], start=(kt == 0), stop=(kt == TT - 1))
                ins.then_inc(at_a.mixed, 1)
            pe.wait_ge(at_a.out, HA)
            with pe.Fori(0, HC) as h:
                pe.wait_ge(at_c.staged, 2 * h + 2)
                pe.wait_ge(at_c.out, h)
                for q in range(TT):
                    mm(bank[q][:, 0:MEM], qs[:, q * P:(q + 1) * P],
                       mk[:, bass.ds(h, 1), :].rearrange("p a s -> p (a s)")).then_inc(at_c.scores, 1)
                pe.wait_ge(at_c.probsT, MT * h)
                for q in range(TT):
                    pe.wait_ge(at_c.probs, TT * h + q + 1)
                    for kt in range(MT):
                        ins = nc.tensor.transpose(bank[4 + kt][:, q * P:(q + 1) * P], s_sb[:, q, kt * P:(kt + 1) * P],
                                                  ident[:, :])
                        if q == TT - 1:
                            ins.then_inc(at_c.turned, 1)
                for kt in range(MT):
                    pe.wait_ge(at_c.probsT, MT * h + kt + 1)
                    ins = mm(bank[0][:, :], vs[:, kt, :], pTc[kt], start=(kt == 0), stop=(kt == MT - 1))
                ins.then_inc(at_c.mixed, 1)

            pe.wait_ge(at_c.out, HC)
            branch = ([qT[:, k, :] for k in range(HA)], [gl[:, k, :] for k in range(LC)], [qkc[:, k, :] for k in range(HC)])
            with pe.Fori(0, KC) as c:
                for b in range(3):
                    pe.wait_ge(gate_ok, 3 * c)
                    project_split(3 * c + S_MIX + b, bank[b][:, :], norm_hi, norm_lo)
                pe.wait_ge(y_used, 3 * c)
                pe.wait_ge(pair_in[1], 32 * c + 16 * (S_MIX // 2 + 2))
                n = 0
                for b, parts in enumerate(branch):
                    for k, part in enumerate(parts):
                        ins = mm(bank[3 + b][:, :], ring[1][:, n, :], part, start=(k == 0), stop=(k == len(parts) - 1))
                        n += 1
                ins.then_inc(tile_done, 1)

            pe.wait_ge(m_ready, KC)
            with pe.Fori(0, KC // 4) as t:
                for k in range(4):
                    pe.wait_ge(x2_ok, 4 * t)
                    project_split(4 * t + S_WO + k, bank[k][:, :], h_hi, h_lo)
            pe.wait_ge(x2_sum, KC + 1)
            mm(bank[6][:, :], ones[:, :], sumsq).then_inc(norm_ss, 1)

            pe.wait_ge(keys_in, 16)

            def scores(n, k):
                pe.wait_ge(pq_copied, n + 1)
                for m in range(TT):
                    ins = mm(bank[4 + k][:, m * P:(m + 1) * P], qp[:, k, m * P:(m + 1) * P],
                             kys[:, bass.ds(n, 1), :].rearrange("p a n -> p (a n)"))
                ins.then_inc(pq_scores, 1)

            def queries(t, first):
                for k in range(4):
                    b = k % 2
                    pe.wait_ge(split_lo, 4 * t + k + 1)
                    for c in range(KC):
                        pe.wait_ge(h2_ready, c + 1)
                        ins = split_mm(bank[k][:, :], w_hi[b][:, c, :], w_lo[b][:, c, :], h_hi[:, c, :], h_lo[:, c, :],
                                       c == 0, c == KC - 1)
                        if c == KC // 2 - 1 and not (first and k == 0):
                            if not first:
                                pe.wait_ge(sc_copied, 4 * t + k - 4)
                            scores(4 * t + k - 1, (k - 1) % 4)
                    ins.then_inc(tile_done, 1)

            queries(0, True)
            with pe.Fori(1, PH // 2) as t:
                queries(t, False)
            scores(2 * PH - 1, 3)

            pe.wait_ge(ident_ok, 1)
            pe.wait_ge(pq_copied, 2 * PH)
            for c in range(KC):
                dst = bank[c // 4][:, (c % 4) * P:(c % 4 + 1) * P]
                mm(dst, h_hi[:, c, ND:], ident_r[:, :], start=True, stop=False)
                ins = mm(dst, h_lo[:, c, ND:], ident_r[:, :], start=False, stop=True)
            ins.then_inc(tok_mm, 1)

            pe.wait_ge(route_ok, 1)
            pe.wait_ge(sc_copied, 2 * PH)
            for w in range(3):
                for m in range(TG):
                    ins = nc.tensor.transpose(bank[4 + w][:, m * P:(m + 1) * P],
                                              route[:, w, m, :, :].rearrange("p h k -> p (h k)"), ident[:, :])
                ins.then_inc(route_tr, 1)

            pe.wait_ge(route_copied, 3)
            pe.wait_ge(tok_copied, 4)

            def tables(t, first):
                for q in range(4):
                    pe.wait_ge(oh_a, 4 * t + q + 1)
                    pe.wait_ge(oh_b, 4 * t + q + 1)
                    for b in (2 * q, 2 * q + 1):
                        if not first:
                            pe.wait_ge(tab_copied, 8 * t + b - 7)
                        for n in range(4):
                            row = 4 * (b % 2) + n
                            ins = mm(bank[b][:, n * P:(n + 1) * P], ohA[q % 2][:, row, :], ohB[q % 2][:, row, :])
                        ins.then_inc(tab_mm, 1)

            tables(0, True)
            with pe.Fori(1, NTB) as t:
                tables(t, False)

            pe.wait_ge(tab_copied, 8 * NTB)
            with pe.Fori(0, NG) as g:
                for j in range(JG):
                    b = j % 2
                    pe.wait_ge(split_lo, 16 * g + 2 * PH + j + 1)
                    pe.wait_ge(u_gelu, JG * g + max(j - 3, 0))
                    for c in range(KC):
                        ins = split_mm(bank[j % 4][:, 0:ND], w_hi[b][:, c, :], w_lo[b][:, c, :],
                                       h_hi[:, c, 0:ND], h_lo[:, c, 0:ND], c == 0, c == KC - 1)
                    ins.then_inc(tile_done, 1)
                for c in range(KC):
                    b = (c // 2) % 2
                    if c % 2 == 0:
                        pe.wait_ge(split_lo, 16 * g + 2 * PH + JG + c // 2 + 1)
                    pe.wait_ge(y_added, KC * g + max(c - 3, 0))
                    for j in range(JG):
                        if c == 0:
                            pe.wait_ge(act_ok, JG * g + j + 1)
                        part = JG * (c % 2) + j
                        ins = split_mm(bank[4 + c % 4][:, 0:ND], w_hi[b][:, part, :], w_lo[b][:, part, :],
                                       act_hi[:, j, :], act_lo[:, j, :], j == 0, j == JG - 1)
                    if c % 2:
                        ins.then_inc(tile_done, 1)

            pe.wait_ge(gath_free, 2 + 2 * PAIRS)
            for c in range(KC):
                ins = nc.tensor.transpose(bank[c // 4][:, (c % 4) * P:(c % 4 + 1) * P], g_acc[:, c, :], ident[:, :])
                if c % 4 == 3:
                    ins.then_inc(tail_tr, 1)


def stationary(w):
    k, n = w.shape
    return np.ascontiguousarray(w.reshape(k // P, P, n // P, P).transpose(2, 1, 0, 3)).reshape(n // P, P, -1)


def moving(w):
    k, n = w.shape
    v = w.reshape(4, 4, P, n // 512, 512).transpose(3, 0, 2, 1, 4)
    return np.ascontiguousarray(v).reshape(-1, P, 2048)


def by_partition(vec):
    return np.ascontiguousarray(vec.reshape(-1, P).T)


def layout(a):
    w_in = a["w_in"]
    qkv = HA * DH
    lru0 = 3 * qkv
    xq0 = lru0 + 2 * LC * P
    lru_w = np.stack([a[n].reshape(LC, 2, 64, 64).transpose(1, 2, 0, 3) for n in ("lru_wa", "lru_wx")])
    lru_vec = np.stack([*(a["conv_w"][i] for i in range(TAPS)), a["conv_b"], a["lru_ba"], a["lru_bx"], a["lru_lambda"]])
    mix = np.stack([*(stationary(a["w_gate"][:, b * D:(b + 1) * D]) for b in range(3)), stationary(a["w_branch"])], axis=1)
    u = a["peer_u"].reshape(P, NG, JG, KC, P).transpose(1, 2, 4, 3, 0).reshape(NG, JG, P, 2048)
    v = a["peer_v"].reshape(P, NG, JG, KC // 2, 2, P).transpose(1, 3, 0, 4, 2, 5).reshape(NG, KC // 2, P, 2048)
    tokens = lambda x: np.ascontiguousarray(x[0].T.reshape(KC, P, -1).transpose(1, 0, 2))
    return {
        "x_t": tokens(a["x"]), "mem_t": tokens(a["mem"]),
        "g1": by_partition(a["norm1_g"]), "g2": by_partition(a["norm2_g"]), "gmem": by_partition(a["mem_norm_g"]),
        "head_g": np.stack([a[n] for n in ("attn_q_norm_g", "attn_k_norm_g", "xq_norm_g", "xk_norm_g")], axis=1),
        "w_memk": stationary(a["w_mem_kv"][:, :HC * DH]), "w_memv": moving(a["w_mem_kv"][:, HC * DH:]),
        "w_qk": np.concatenate([stationary(w_in[:, :2 * qkv]), stationary(w_in[:, xq0:])]),
        "w_lru_in": stationary(w_in[:, lru0:xq0]), "w_v": moving(w_in[:, 2 * qkv:lru0]),
        "rel_rev": np.ascontiguousarray(a["rel_bias"][:, ::-1]), "lru_w": np.ascontiguousarray(lru_w),
        "lru_vec": np.ascontiguousarray(lru_vec.reshape(8, LC, P).transpose(2, 0, 1)),
        "w_mix": mix.reshape(4 * KC, P, 2048), "b_gate": by_partition(a["b_gate"]),
        "w_o": stationary(a["w_o"]), "w_pq": stationary(a["w_peer_q"]),
        "keys": np.ascontiguousarray(a["peer_keys"].reshape(2 * PH, NKEYS, P).transpose(2, 0, 1)),
        "w_exp": np.concatenate([u, v], axis=1).reshape(16 * NG, P, 2048),
        "u_rows": a["peer_u"], "v_rows": a["peer_v"],
    }


def kernel(**inputs):
    import concourse.bacc as bacc
    from concourse.bass_utils import run_bass_kernel_spmd

    nc = bacc.Bacc("TRN2", target_bir_lowering=False, num_devices=1)
    arrays = {n: np.ascontiguousarray(v) for n, v in layout({n: np.asarray(v) for n, v in inputs.items()}).items()}
    args = [nc.dram_tensor(n, v.shape, mybir.dt.from_np(v.dtype), kind="ExternalInput").ap() for n, v in arrays.items()]
    out_t = nc.dram_tensor("out_t", (P, KC, S), F32, kind="ExternalOutput").ap()
    hybrid_block(nc, *args, out_t)
    r = run_bass_kernel_spmd(nc, [arrays], core_ids=[0])
    o = r.results[0]["out_t"]
    return np.ascontiguousarray(o.transpose(2, 1, 0).reshape(1, S, D))
```

```python
from contextlib import ExitStack

import concourse.bass as bass
import numpy as np
from concourse import mybir

F32 = mybir.dt.float32
U32 = mybir.dt.uint32
F32R = mybir.dt.float32r
ALU = mybir.AluOpType
ACT = mybir.ActivationFunctionType
AX_X = mybir.AxisListType.X

P = 128
D = 2048
KC = D // P
S = 512
TT = S // P
MEM = 256
MT = MEM // P
CHUNK = 64
HA = 8
HC = 4
DH = 128
LC = 4
TAPS = 4
CLIP = 128
NREL = 2 * CLIP + 1
EXT = 3 * P
PH = 8
NKEYS = 128
TOPK = 16
JG = 8
NG = NKEYS // JG
ND = S - P
TG = TT - 1
TB = 32
NTB = ND // TB
HT = TB // 4
PAIRS = PH * TOPK
EARLY = 4
EPS = 1e-6
NEG = -1e30
LOWEST = -3.0e38
SCALE = float(DH) ** -0.5

SLOTS = 4
T_MK = 0
T_MV = T_MK + HC
T_LRU = T_MV + 4
T_QK = T_LRU + 2 * LC
N_QK = 2 * HA + HC
T_V = T_QK + N_QK
T_MIX = T_V + 8
T_WO = T_MIX + 4 * KC
T_PQ = T_WO + KC
S_QK = T_QK - T_LRU
S_V = T_V - T_LRU
S_MIX = T_MIX - T_LRU
S_WO = S_MIX + 3 * KC
T_EXP = T_PQ + 2 * PH


class Steps:

    def __init__(self, eng, sem):
        self.eng, self.sem, self.start, self.n, self.turn, self.per = eng, sem, 0, 0, None, 0

    def loop(self, turn, per, first=0):
        self.start, self.n, self.turn, self.per = self.start + self.n - first * per, 0, turn, per

    def end(self, turns):
        assert self.n == self.per, (self.n, self.per)
        self.start, self.n, self.turn = self.start + turns * self.per, 0, None

    def did(self, ins):
        ins.then_inc(self.sem, 1)
        self.n += 1
        return self.n

    def wait(self, n=None):
        n = self.start + (self.n if n is None else n)
        self.eng.wait_ge(self.sem, n if self.turn is None else self.turn * self.per + n)


def hybrid_block(nc, x_t, mem_t, g1, g2, gmem, head_g, w_memk, w_memv, w_qk, w_lru_in, w_v, rel_rev,
                 lru_w, lru_vec, w_mix, b_gate, w_o, w_pq, keys, w_exp, u_rows, v_rows, out_t):
    ctx = ExitStack()
    with ctx:
        def sb(name, shape, dt=F32):
            return ctx.enter_context(nc.sbuf_tensor(name, shape, dt))

        def sem(name):
            return ctx.enter_context(nc.semaphore(name))

        ones = sb("ones", [P, P])
        ident = sb("ident", [P, P])
        iota = sb("iota", [P, P])
        vecs = sb("vecs", [P, 3 * KC])
        hgain = sb("hgain", [P, 4])
        bgate = sb("bgate", [P, 3 * KC])
        lvec = sb("lvec", [P, 8, LC])
        sp = sb("sp", [P, 6, LC])
        eps = sb("eps", [P, 1])
        rext = sb("rext", [HA, EXT])
        smax = sb("smax", [P, 2, TT])
        nmax = sb("nmax", [P, 2, TT])
        ssum = sb("ssum", [P, 2, TT])
        rinv = sb("rinv", [P, 2, TT])

        QM, KV, QC, GL, XL = 0, 4096, 12288, 14336, 16384
        MK, MV, TZ, Z = 18448, 19472, 20496, 22544
        base = -(-nc.sbuf_base // 64) * 64

        def place(name, kib, dims, dt=F32):
            return nc.alloc_sbuf_tensor_at(name, [P, *dims], dt, offset=base + int(kib * 1024))

        xT = place("xT", 0, [KC, S])
        hT = place("hT", 32, [KC, S])
        ring = [place(f"ring{i}", 64 + 8 * i, [16, P]) for i in range(SLOTS)]
        arena = place("arena", 96, [Z + 4096])
        p_hi = place("p_hi", 80, [16, P], F32R)
        p_lo = place("p_lo", 88, [16, P], F32R)
        norm_hi = place("norm_hi", 0, [KC, S], F32R)
        norm_lo = place("norm_lo", 32, [KC, S], F32R)
        w_hi = [place(f"w_hi{i}", 80 + 16 * i, [16, P], F32R) for i in range(2)]
        w_lo = [place(f"w_lo{i}", 88 + 16 * i, [16, P], F32R) for i in range(2)]
        h_hi = place("h_hi", 32, [KC, S], F32R)
        h_lo = place("h_lo", 112, [KC, S], F32R)
        h_tok = place("h_tok", 32, [KC, S])[:, :, ND:]
        g_acc = place("g_acc", 112, [KC, S])[:, :, ND:]
        wt = [place(f"wt{i}", 80 + 16 * i, [NKEYS, TB]) for i in range(2)]
        ohA = [place(f"ohA{i}", 165 + 4 * i, [HT, P]) for i in range(2)]
        ohB = [place(f"ohB{i}", 173 + 4 * i, [HT, P]) for i in range(2)]
        gel_first = place("gel_first", 144, [JG, ND])
        act_hi = place("act_hi", 144, [JG, ND], F32R)
        act_lo = place("act_lo", 156, [JG, ND], F32R)
        wg = place("wg", 168, [NTB, JG, TB])
        gel = [place(f"gel{i}", 180 + 1.5 * i, [ND]) for i in range(2)]
        grow = [place(f"grow{i}", 183 + 8 * i, [D]) for i in range(2)]
        g_idx = place("g_idx", 200.5, [PAIRS], U32)
        g_w = place("g_w", 201, [PAIRS])
        g_dot = place("g_dot", 201.5, [PAIRS])
        g_act = place("g_act", 202, [PAIRS])
        g_col = [place(f"g_col{i}", 202.5 + i / 16, [1], U32) for i in range(2)]
        ident_r = place("ident_r", 203, [P], F32R)

        def at(offset, *dims):
            n = int(np.prod(dims))
            v = arena[:, offset:offset + n]
            if len(dims) == 1:
                return v
            names = "abcd"[:len(dims)]
            return v.rearrange(f"p ({' '.join(names)}) -> p {' '.join(names)}", **dict(zip(names[1:], dims[1:])))

        memT = at(QM, KC, MEM)
        xsq = at(KV, KC, S)
        msq = at(QC, KC, MEM)
        qT = at(QM, HA, S)
        kT = at(KV, HA, S)
        vA = at(KV + 4096, TT, HA * DH)
        qkc = at(QC, HC, S)
        gl = at(GL, LC, S)
        xl = at(XL, LC, S + TAPS - 1)
        mk = at(MK, HC, MEM)
        mv = at(MV, MT, HC * DH)
        rt = [at(Z + 1024 * i, S) for i in range(2)]
        sq = [at(Z + 1024 * i + 512, S) for i in range(2)]
        lw = at(TZ, 2, LC, P)
        xc = at(KV + 4096, LC, S)
        rg = at(KV + 6144, LC, S)
        ig = at(XL, LC, S)
        la = at(TZ + 1024, S)
        lr = at(TZ + 1536, S)
        tb = at(TZ, HA, 2 * P)
        s_at = [P * q * (q + 1) // 2 for q in range(TT + 1)]
        s_sb = [at(Z + s_at[TT] * e, s_at[TT]) for e in range(2)]
        pT = [at(Z + 2 * s_at[TT] + (0, 512, 896, 1152)[kt], (TT - kt) * P) for kt in range(TT)]
        pTc = [at(Z + 2 * s_at[TT] + 512 * kt, S) for kt in range(MT)]
        qs = [at(XL + 512 * e, S) for e in range(2)]
        vs = [at(XL + 1024 + 512 * e, TT, DH) for e in range(2)]
        merged = at(KV, KC, S)
        sig = at(Z, 3, S)
        prod = at(Z + 1536, 3, S)
        sumsq = at(Z, S)
        sqx = at(Z + 512, S)
        rt2 = at(Z + 1024, S)
        h2 = [at(Z + 1536 + 512 * i, S) for i in range(2)]
        kys = at(QC, 2 * PH, NKEYS)
        qp = at(GL, SLOTS, S)
        sc = at(XL, SLOTS, TT, NKEYS)
        sv = at(MK, 2, 2, TT, TOPK)
        si = at(MK + 256, 2, 2, TT, TOPK).bitcast(U32)
        fpos = at(MK + 512, TT, TOPK).bitcast(U32)
        fa = at(MK + 576, TT * TOPK).bitcast(U32)
        fb = at(MK + 640, TT * TOPK).bitcast(U32)
        fv = at(MK + 704, TT, TOPK)
        ires = at(MK + 768, TT, TOPK)
        jres = at(MK + 832, TT, TOPK)
        cand = at(Z, TT, TOPK, TOPK)
        pick = at(Z + 1024, 2, TT * TOPK, TOPK)
        route = at(TZ, 3, TT, PH, TOPK)
        gmx = at(MV, TT * PH)
        gsum = at(MV + 32, TT * PH)
        grec = at(MV + 64, TT * PH)
        routeT = at(XL, 3, ND)
        bank = [ctx.enter_context(nc.psum_tensor(f"bank{i}", [P, S], F32)) for i in range(8)]
        t_ps = [bank[4][:, :], bank[5][:, 0:3 * P], bank[6][:, 0:2 * P], bank[5][:, 3 * P:]]
        rel_dram = nc.dram_tensor("rel_ext", [P, HA, EXT], F32)
        table_dram = nc.dram_tensor("tables", [NTB, P, NKEYS * TB], F32).ap()

        slot_in = [sem(f"slot_in{i}") for i in range(SLOTS)]
        tile_done = sem("tile_done")
        mem_in, x_in, vec_in = sem("mem_in"), [sem(f"x_in{i}") for i in range(4)], sem("vec_in")
        const_made = sem("const_made")
        mem_sq, x_sq = sem("mem_sq"), sem("x_sq")
        norm_ss = sem("norm_ss")
        norm_rt = sem("norm_rt")
        mem_h, h_ready = sem("mem_h"), sem("h_ready")
        h_made, h_high = sem("h_made"), sem("h_high")
        pair_in = [sem(f"pair_in{i}") for i in range(2)]
        quarter_hi, quarter_lo = sem("quarter_hi"), sem("quarter_lo")
        part_used = sem("part_used")
        x_back, m_hi_ok, m_ready = sem("x_back"), sem("m_hi_ok"), sem("m_ready")
        acc_copied = sem("acc_copied")
        head_sq, head_ss, head_rt, head_ok = sem("head_sq"), sem("head_ss"), sem("head_rt"), sem("head_ok")
        lin_copied, v_copied = sem("lin_copied"), sem("v_copied")
        xl_zero = sem("xl_zero")
        lw_zero, lw_in = sem("lw_zero"), sem("lw_in")
        lam_abs, lam_exp, sp_ok = sem("lam_abs"), sem("lam_exp"), sem("sp_ok")
        conv_ok, lru_mm, lru_sig, lru_tanh, lru_m2, lru_mult, lru_ok = (
            sem("conv_ok"), sem("lru_mm"), sem("lru_sig"), sem("lru_tanh"), sem("lru_m2"), sem("lru_mult"), sem("lru_ok"))
        rel_in, rel_filled, rel_out, bias_in, bias_ok = (
            sem("rel_in"), sem("rel_filled"), sem("rel_out"), sem("bias_in"), sem("bias_ok"))

        class Attention:
            def __init__(self, n):
                self.staged_q = sem(f"{n}_staged_q")
                self.staged_v = sem(f"{n}_staged_v")
                self.scores = sem(f"{n}_scores")
                self.taken = sem(f"{n}_taken")
                self.shifted = sem(f"{n}_shifted")
                self.exped = sem(f"{n}_exped")
                self.probs = sem(f"{n}_probs")
                self.turned = sem(f"{n}_turned")
                self.probsT = sem(f"{n}_probsT")
                self.mixed = sem(f"{n}_mixed")
                self.out = sem(f"{n}_out")

        at_a, at_c = Attention("band"), Attention("cross")
        gate_ok, y_used, merged_ok = sem("gate_ok"), sem("y_used"), sem("merged_ok")
        x2_ok, x2_sq, x2_sum = sem("x2_ok"), sem("x2_sq"), sem("x2_sum")
        h2_ready = sem("h2_ready")
        h2_made, h2_hi = sem("h2_made"), sem("h2_hi")
        raw_in = [sem(f"raw_in{i}") for i in range(2)]
        split_hi, split_lo = sem("split_hi"), sem("split_lo")
        keys_in, pq_copied, pq_scores, sc_copied, sc_free = (
            sem("keys_in"), sem("pq_copied"), sem("pq_scores"), sem("sc_copied"), sem("sc_free"))
        g_shift, g_exp, route_ok, route_tr, route_copied = (
            sem("g_shift"), sem("g_exp"), sem("route_ok"), sem("route_tr"), sem("route_copied"))
        ident_ok, tok_mm, tok_copied = sem("ident_ok"), sem("tok_mm"), sem("tok_copied")
        acc_zero, gath_col, gath_free, gath_gelu, gath_act = (
            sem("acc_zero"), sem("gath_col"), sem("gath_free"), sem("gath_gelu"), sem("gath_act"))
        gath_in = [sem(f"gath_in{i}") for i in range(2)]
        tail_tr, tail_added = sem("tail_tr"), sem("tail_added")
        oh_a, oh_b = sem("oh_a"), sem("oh_b")
        tab_mm, tab_copied = sem("tab_mm"), sem("tab_copied")
        tab_out = [sem(f"tab_out{i}") for i in range(2)]
        wg_in, u_gelu, act_part, act_ok, y_added = (
            sem("wg_in"), sem("u_gelu"), sem("act_part"), sem("act_ok"), sem("y_added"))
        out_done = sem("out_done")
        wait_held, pool_held = sem("wait_held"), sem("pool_held")
        dve_step, pool_step = sem("dve_step"), sem("pool_step")

        def band_s(e, q):
            return s_sb[e][:, s_at[q]:s_at[q + 1]]

        def cross_s(e, q):
            return s_sb[e][:, MEM * q:MEM * (q + 1)]

        def head_place(t, k):
            return arena[:, bass.ds((4 * t + k) * S + (t // 4) * (QC - 2 * HA * S), S)]

        def in_pairs(eng, heads, start, step):
            for e in range(2):
                start(e, e)
            with eng.Fori(0, heads // 2 - 1) as t:
                for e in range(2):
                    step(2 * t + e, e, True)
            for e in range(2):
                step(heads - 2 + e, e, False)

        def landed(eng, tile, turn=None, per=0):
            n = 16 * (tile // SLOTS + 1)
            eng.wait_ge(slot_in[tile % SLOTS], n if turn is None else turn * (16 * (per // SLOTS)) + n)

        block = ctx.enter_context(nc.Block())

        @block.sync
        def _(sync):
            def load(tile, src, turn=None, per=0):
                if tile >= SLOTS or turn is not None:
                    n = tile - SLOTS + 1
                    sync.wait_ge(tile_done, n if turn is None else turn * per + n)
                slot = ring[tile % SLOTS][:, :, :].rearrange("p a b -> p (a b)")
                sync.dma_start(slot, src).then_inc(slot_in[tile % SLOTS], 16)

            def row(w, n):
                return w[bass.ds(n, 1)].rearrange("a p n -> p (a n)")

            sync.dma_start(memT, mem_t).then_inc(mem_in, 16)
            load(0, w_memk[0])
            for q in range(4):
                sync.dma_start(xT[:, 4 * q:4 * q + 4, :], x_t[:, 4 * q:4 * q + 4, :]).then_inc(x_in[q], 16)
            for k in range(1, HC):
                load(T_MK + k, w_memk[k])
            for k in range(4):
                load(T_MV + k, w_memv[k])

            def load_half(slot, src):
                sync.dma_start(ring[slot][:, :, :].rearrange("p a b -> p (a b)"), src).then_inc(pair_in[slot], 16)

            for k in range(2):
                sync.wait_ge(tile_done, T_MV + k + 1)
                load_half(k, w_lru_in[k])

            def load_pairs(w, split, first, turns):
                with sync.Fori(0, turns) as t:
                    for k in range(2):
                        sync.wait_ge(quarter_lo, 8 * t + 4 * (split + k + 1))
                        load_half(k, row(w, 2 * t + first + k))

            load_pairs(w_lru_in, 0, 2, LC - 1)
            load_pairs(w_qk, S_QK - 2, 0, N_QK // 2)
            load_pairs(w_v, S_V - 2, 0, 4)
            with sync.Fori(0, KC) as c:
                sync.wait_ge(quarter_lo, 12 * c + 4 * S_MIX)
                load_half(0, row(w_mix, 4 * c))
                sync.wait_ge(tile_done, 4 * c + T_MIX)
                load_half(1, row(w_mix, 4 * c + 1))
                for k in range(2):
                    sync.wait_ge(quarter_lo, 12 * c + 4 * (S_MIX + k + 1))
                    load_half(k, row(w_mix, 4 * c + 2 + k))
            sync.wait_ge(quarter_lo, 4 * S_WO)
            load_half(0, w_o[0])
            sync.wait_ge(tile_done, T_WO - 1)
            for q in range(4):
                sync.dma_start(xT[:, 4 * q:4 * q + 4, :], x_t[:, 4 * q:4 * q + 4, :]).then_inc(x_back, 16)
            sync.wait_ge(tile_done, T_WO)
            load_half(1, w_o[1])
            load_pairs(w_o, S_WO, 2, KC // 2 - 1)

            def load_raw(m, src):
                sync.wait_ge(split_lo, m - 1)
                sync.dma_start(ring[m_slot][:, :, :].rearrange("p a b -> p (a b)"), src).then_inc(raw_in[m_slot], 16)

            for m_slot in range(2):
                sync.wait_ge(quarter_lo, 4 * (S_WO + KC - 1 + m_slot))
                sync.dma_start(ring[m_slot][:, :, :].rearrange("p a b -> p (a b)"), w_pq[m_slot]).then_inc(raw_in[m_slot], 16)
            with sync.Fori(1, PH) as t:
                for m_slot in range(2):
                    load_raw(2 * t + m_slot, row(w_pq, 2 * t + m_slot))
            for q in range(JG + 2):
                m_slot = q % 2
                load_raw(2 * PH + q, w_exp[q])
            with sync.Fori(0, NTB // 2) as t:
                for b in range(2):
                    sync.wait_ge(tab_copied, 16 * t + 8 * b + 8)
                    sync.dma_start(table_dram[bass.ds(2 * t + b, 1)].rearrange("a p n -> p (a n)"),
                                   wt[b][:, :, :].rearrange("p a b -> p (a b)")).then_inc(tab_out[b], 16)
            for b in range(2):
                sync.wait_ge(tab_out[b], 16 * (NTB // 2))

            def load_tables(g):
                sync.dma_start(wg[:, :, :, :].rearrange("p a b c -> p a (b c)"),
                               table_dram[:, :, bass.ds(JG * TB * g, JG * TB)].rearrange("t p n -> p t n")
                               ).then_inc(wg_in, 16)

            load_tables(0)
            for q in range(JG + 2, 16):
                m_slot = q % 2
                load_raw(2 * PH + q, w_exp[q])
            with sync.Fori(1, NG) as g:
                sync.wait_ge(act_ok, JG * g)
                load_tables(g)
                for q in range(16):
                    m_slot = q % 2
                    load_raw(16 * g + 2 * PH + q, row(w_exp, 16 * g + q))
            for b in range(4):
                sync.wait_ge(tail_added, b + 1)
                sync.dma_start(out_t[:, 4 * b:4 * b + 4, :], xT[:, 4 * b:4 * b + 4, :]).then_inc(out_done, 16)
            sync.wait_ge(out_done, 16 * 4)

        @block.gpsimd
        def _(pool):
            nc.gpsimd.memset(ident[:, :], 0.0).then_inc(pool_step, 1)
            pool.iota(iota[:, :], [[1, P]], base=0, channel_multiplier=0,
                      allow_small_or_imprecise_dtypes=True).then_inc(const_made, 1)
            pool.wait_ge(pool_step, 1)
            pool.affine_select(out=ident[:, :], in_=ident[:, :], compare_op=ALU.not_equal, fill=1.0, base=0,
                               pattern=[[-1, P]], channel_multiplier=1).then_inc(const_made, 1)
            nc.gpsimd.memset(xl[:, :, 0:TAPS - 1], 0.0).then_inc(xl_zero, 1)
            nc.gpsimd.memset(lw, 0.0).then_inc(lw_zero, 1)

            def low_part(slot, number):
                for q in range(4):
                    part = slice(4 * q, 4 * q + 4)
                    pool.wait_ge(quarter_hi, 4 * number + q + 1)
                    nc.gpsimd.tensor_tensor(p_lo[:, part, :], ring[slot][:, part, :], p_hi[:, part, :].bitcast(F32),
                                            ALU.subtract).then_inc(quarter_lo, 1)

            with pool.Fori(0, S_MIX // 2) as t:
                for k in range(2):
                    low_part(k, 2 * t + k)
            low_part(0, S_MIX)

            pool.wait_ge(lru_ok, LC)
            pool.wait_ge(head_ok, HC + N_QK)
            pool.wait_ge(v_copied, MT + 2 * TT)

            def stage(a, heads, q_of, v_of, v_tiles):
                def q_stage(h, e):
                    nc.gpsimd.tensor_copy(qs[e], q_of[:, bass.ds(h, 1), :].rearrange("p a s -> p (a s)")).then_inc(a.staged_q, 1)

                def v_stage(h, e):
                    nc.gpsimd.tensor_copy(vs[e][:, 0:v_tiles, :], v_of[:, :, bass.ds(h * DH, DH)]).then_inc(a.staged_v, 1)

                for e in range(2):
                    q_stage(e, e)
                    v_stage(e, e)
                with pool.Fori(0, heads // 2 - 1) as t:
                    for e in range(2):
                        pool.wait_ge(a.scores, TT * (2 * t + e + 1))
                        q_stage(2 * t + e + 2, e)
                        pool.wait_ge(a.mixed, 2 * t + e + 1)
                        v_stage(2 * t + e + 2, e)

            stage(at_a, HA, qT, vA, TT)
            pool.wait_ge(at_a.mixed, HA)
            stage(at_c, HC, qkc, mv, MT)

            with pool.Fori(0, KC) as c:
                for slot, k in ((1, 1), (0, 2), (0, 3)):
                    low_part(slot, 3 * c + S_MIX + k)

            pool.wait_ge(merged_ok, KC)
            nc.gpsimd.memset(sumsq, 0.0).then_inc(x2_sum, 1)

            def add_square(c):
                pool.wait_ge(x2_ok, c + 1)
                pool.wait_ge(x2_sum, c + 1)
                xk = xT[:, bass.ds(c, 1), :].rearrange("p a s -> p (a s)")
                nc.gpsimd.tensor_tensor(sqx, xk, xk, ALU.mult).then_inc(x2_sq, 1)
                pool.wait_ge(x2_sq, c + 1)
                nc.gpsimd.tensor_tensor(sumsq, sumsq, sqx, ALU.add).then_inc(x2_sum, 1)

            with pool.Fori(0, KC // 2 - 1) as t:
                for k in range(2):
                    low_part(1 - k, 2 * t + S_WO + 1 + k)
                    add_square(2 * t + k)
            low_part(1, S_WO + KC - 1)
            for c in (KC - 2, KC - 1):
                add_square(c)

            with pool.Fori(0, PH + JG // 2) as t:
                for b in range(2):
                    pool.wait_ge(split_hi, 2 * t + b + 1)
                    nc.gpsimd.tensor_tensor(w_lo[b][:, :, :], ring[b][:, :, :], w_hi[b][:, :, :].bitcast(F32),
                                            ALU.subtract).then_inc(split_lo, 1)

            for number, rows in enumerate((u_rows, v_rows)):
                with pool.Fori(0, PAIRS // 2) as t:
                    for b in range(2):
                        pool.wait_ge(gath_free, 2 * t + b + 1 + number * PAIRS)
                        nc.gpsimd.tensor_copy(g_col[b][:, :], g_idx[:, bass.ds(2 * t + b, 1)]).then_inc(gath_col, 1)
                        pool.wait_ge(gath_col, 2 * t + b + 1 + number * PAIRS)
                        pool.sem_inc(pool_held, 1)
                        pool.indirect_dma_start(grow[b][:, :], None, rows, bass.IndirectOffsetOnAxis(g_col[b][:, :], 0)
                                                ).then_inc(gath_in[b], 16)

        @block.scalar
        def _(act_e):
            def f(out, in_, func=ACT.Copy, **kw):
                return nc.scalar.activation(out, in_, func, **kw)

            for dst, src in ((vecs[:, 0:KC], g1), (vecs[:, KC:2 * KC], g2), (vecs[:, 2 * KC:], gmem),
                             (hgain[:, :], head_g), (bgate[:, :], b_gate), (lvec[:, :, :], lru_vec)):
                act_e.dma_start(dst, src).then_inc(vec_in, 16)
            act_e.dma_start(rext[:, P - 1:], rel_rev).then_inc(rel_in, 16)
            act_e.wait_ge(lw_zero, 1)
            for side in range(2):
                for half in range(2):
                    sl = slice(64 * half, 64 * half + 64)
                    act_e.dma_start(lw[sl, side, :, sl], lru_w[side, half]).then_inc(lw_in, 16)

            act_e.wait_ge(mem_in, 16)
            f(msq, memT, ACT.Square).then_inc(mem_sq, 1)
            act_e.wait_ge(const_made, 4)
            act_e.wait_ge(norm_ss, 1)
            f(rt[0][:, 0:MEM], bank[6][:, 0:MEM], ACT.Sqrt, scale=1.0 / D, bias=eps[:, 0:1]).then_inc(norm_rt, 1)
            for q in range(4):
                act_e.wait_ge(x_in[q], 16)
                f(xsq[:, 4 * q:4 * q + 4, :], xT[:, 4 * q:4 * q + 4, :], ACT.Square).then_inc(x_sq, 1)

            def head_root(n, width, number):
                act_e.wait_ge(head_ss, number)
                f(rt[n % 2][:, 0:width], bank[4 + n % 2][:, 0:width], ACT.Sqrt, scale=1.0 / DH,
                  bias=eps[:, 0:1]).then_inc(head_rt, 1)

            for k in range(HC):
                act_e.wait_ge(tile_done, T_MK + k + 1)
                f(mk[:, k, :], bank[k][:, 0:MEM]).then_inc(acc_copied, 1)
                if k >= 2:
                    act_e.wait_ge(head_ss, k - 1)
                f(sq[k % 2][:, 0:MEM], bank[k][:, 0:MEM], ACT.Square).then_inc(head_sq, 1)
                if k >= 2:
                    act_e.wait_ge(head_ok, k - 1)
                if k == 0:
                    act_e.wait_ge(mem_h, KC)
                head_root(k, MEM, k + 1)
            act_e.wait_ge(norm_ss, 2)
            act_e.wait_ge(head_ok, HC)
            f(rt[0], bank[6][:, :], ACT.Sqrt, scale=1.0 / D, bias=eps[:, 0:1]).then_inc(norm_rt, 1)
            for c in range(KC):
                act_e.wait_ge(h_made, c + 1)
                f(norm_hi[:, c, :], hT[:, c, :]).then_inc(h_high, 1)
            act_e.wait_ge(tile_done, T_MV + 4)
            for m in range(MT):
                f(mv[:, m, :], bank[2 + m][:, :]).then_inc(v_copied, 1)

            def high_part(slot, number, tiles, used, quarters=range(4)):
                act_e.wait_ge(pair_in[slot], 16 * tiles)
                for q in quarters:
                    if q < 3:
                        act_e.wait_ge(part_used, 3 * number + q - 2)
                    else:
                        act_e.wait_ge(tile_done, used)
                    part = slice(4 * q, 4 * q + 4)
                    f(p_hi[:, part, :], ring[slot][:, part, :]).then_inc(quarter_hi, 1)

            act_e.wait_ge(tile_done, T_LRU)
            act_e.wait_ge(pair_in[0], 16)
            for q in range(4):
                f(p_hi[:, 4 * q:4 * q + 4, :], ring[0][:, 4 * q:4 * q + 4, :]).then_inc(quarter_hi, 1)
            high_part(1, 1, 1, T_LRU + 1)

            act_e.wait_ge(vec_in, 16 * 6)
            act_e.wait_ge(lam_abs, 1)
            f(sp[:, 1, :], sp[:, 0, :], ACT.Exp, scale=-1.0).then_inc(lam_exp, 1)
            act_e.wait_ge(rel_filled, 1)
            act_e.dma_start(rel_dram.ap().rearrange("p h n -> h p n"),
                            rext[:, :].unsqueeze(1).to_broadcast([HA, P, EXT])).then_inc(rel_out, 16)

            def two_ahead(n, quarters=range(4)):
                high_part(n % 2, n + 2 - T_LRU, (n - T_LRU) // 2 + 2, n + 2, quarters)

            def gates(side, dst):
                for k in range(LC):
                    act_e.wait_ge(lru_mm, LC * side + k + 1)
                    f(dst[:, k, :], bank[4 + k][:, :], ACT.Sigmoid, bias=lvec[:, 5 + side, k:k + 1]).then_inc(lru_sig, 1)

            act_e.wait_ge(xl_zero, 1)
            for k in range(LC):
                act_e.wait_ge(tile_done, T_LRU + k + 1)
                f(xl[:, k, TAPS - 1:], bank[k][:, :]).then_inc(lin_copied, 1)
                two_ahead(T_LRU + k)
            for k in range(LC):
                act_e.wait_ge(tile_done, T_LRU + LC + k + 1)
                f(gl[:, k, :], bank[k][:, :], ACT.Gelu_apprx_tanh).then_inc(lin_copied, 1)
                if k < LC - 1:
                    two_ahead(T_LRU + LC + k)
            gates(0, rg)
            two_ahead(T_QK - 1, (0,))
            act_e.wait_ge(conv_ok, LC)
            gates(1, ig)
            act_e.wait_ge(sp_ok, 1)
            act_e.wait_ge(lru_sig, LC)
            for k in range(LC):
                f(rg[:, k, :], rg[:, k, :], ACT.Tanh, scale=sp[:, 5, k:k + 1]).then_inc(lru_tanh, 1)
            two_ahead(T_QK - 1, (1, 2, 3))

            act_e.wait_ge(h_ready, KC)

            def heads(t, first):
                for k in range(4):
                    act_e.wait_ge(tile_done, 4 * t + T_QK + k + 1)
                    f(head_place(t, k), bank[k][:, :]).then_inc(acc_copied, 1)
                    act_e.wait_ge(head_ss, 4 * t + k + HC - 1)
                    f(sq[k % 2], bank[k][:, :], ACT.Square).then_inc(head_sq, 1)
                    ahead = (k % 2, 4 * t + S_QK + k + 2, 2 * t + S_QK // 2 + k // 2 + 2, 4 * t + T_QK + k + 2)
                    high_part(*ahead, quarters=(0,))
                    act_e.wait_ge(head_ok, 4 * t + k + HC - 1)
                    head_root(k, S, 4 * t + k + HC + 1)
                    high_part(*ahead, quarters=(1, 2, 3))
                    if first:
                        act_e.wait_ge(lru_m2, k + 1)
                        f(rg[:, k, :], rg[:, k, :], ACT.Sqrt).then_inc(lru_mult, 1)

            heads(0, True)
            with act_e.Fori(1, N_QK // 4) as t:
                heads(t, False)
            act_e.wait_ge(lru_ok, LC)
            act_e.wait_ge(rel_out, 16)
            act_e.dma_start(tb, bass.AP(rel_dram, P - 1, [[HA * EXT - 1, P], [EXT, HA], [1, 2 * P]])).then_inc(bias_in, 16)
            for half in range(2):
                for n in range(3):
                    two_ahead(T_V + 4 * half + n)
                act_e.wait_ge(tile_done, T_V + 4 * half + 4)
                for m in range(TT):
                    f(vA[:, m, 512 * half:512 * half + 512], bank[4 * half + m][:, :]).then_inc(v_copied, 1)
                if half == 0:
                    two_ahead(T_V + 3)

            def attention(a, heads, tiles, s_of, exp_in, turned_ps, dst, scale):
                def exps(h, e):
                    for q in range(TT):
                        act_e.wait_ge(a.shifted, TT * h + q + 1)
                        f(s_of(e, q), exp_in(e, q), ACT.Exp, bias=nmax[:, e, q:q + 1], scale=scale,
                          accum_out=ssum[:, e, q:q + 1]).then_inc(a.exped, 1)

                def copies(h, e, more):
                    act_e.wait_ge(a.mixed, h)
                    for kt in range(tiles):
                        act_e.wait_ge(a.turned, tiles * h + (tiles if kt else 1))
                        f(dst[kt], turned_ps[kt]).then_inc(a.probsT, 1)
                    if more:
                        exps(h + 2, e)

                in_pairs(act_e, heads, exps, copies)

            attention(at_a, HA, TT, band_s, band_s, t_ps, pT, 1.0)
            attention(at_c, HC, MT, cross_s, lambda e, q: bank[q][:, 0:MEM], [bank[4][:, :], bank[5][:, :]], pTc, SCALE)

            with act_e.Fori(0, KC) as c:
                for b in range(3):
                    slot, tiles = ((1, 1), (0, 2), (0, 3))[b]
                    high_part(slot, 3 * c + S_MIX + b + 1, 2 * c + S_MIX // 2 + tiles, 4 * c + T_MIX + b + 1)
                    act_e.wait_ge(tile_done, 4 * c + T_MIX + b + 1)
                    if b == 0:
                        act_e.wait_ge(merged_ok, c)
                    f(sig[:, b, :], bank[b][:, :], ACT.Sigmoid, bias=bgate[:, bass.ds(KC * b + c, 1)]
                      ).then_inc(gate_ok, 1)

            for c in range(KC):
                act_e.wait_ge(merged_ok, c + 1)
                f(h_hi[:, c, :], merged[:, c, :]).then_inc(m_hi_ok, 1)
            with act_e.Fori(0, KC // 2 - 1) as t:
                for k in range(2):
                    high_part(1 - k, 2 * t + S_WO + 1 + k, t + (S_MIX + 4 * KC) // 2 + 1 + k, 2 * t + T_WO + k + 1)
            high_part(1, S_WO + KC - 1, (S_MIX + 4 * KC + KC) // 2, T_WO + KC - 1)

            act_e.wait_ge(tile_done, T_WO)
            act_e.dma_start(kys, keys).then_inc(keys_in, 16)
            act_e.wait_ge(norm_ss, 3)
            f(rt2, bank[6][:, :], ACT.Sqrt, scale=1.0 / D, bias=eps[:, 0:1]).then_inc(norm_rt, 1)

            for c in range(KC):
                act_e.wait_ge(h2_made, c + 1)
                f(h_hi[:, c, :], h2[c % 2]).then_inc(h2_hi, 1)

            def high(n, b, free):
                act_e.wait_ge(raw_in[b], 16 * (n // 2) + 16)
                if free:
                    act_e.wait_ge(tile_done, n + T_PQ - 1)
                f(w_hi[b][:, :, :], ring[b][:, :, :]).then_inc(split_hi, 1)

            high(0, 0, False)
            high(1, 1, False)
            act_e.wait_ge(keys_in, 16)

            def queries(t):
                for k in range(4):
                    act_e.wait_ge(tile_done, 4 * t + T_PQ + k + 1)
                    act_e.wait_ge(pq_scores, 4 * t)
                    f(qp[:, k, :], bank[k][:, :]).then_inc(pq_copied, 1)
                    high_in_turn(t, k)
                    act_e.wait_ge(pq_scores, 4 * t + k + 1)
                    act_e.wait_ge(sc_free, 4 * t + k + 1)
                    f(sc[:, k, :, :], bank[4 + k][:, :].rearrange("p (a b) -> p a b", a=TT)).then_inc(sc_copied, 1)

            def high_in_turn(t, k):
                b = k % 2
                act_e.wait_ge(raw_in[b], 32 * t + 16 * (k // 2 + 1) + 16)
                act_e.wait_ge(tile_done, 4 * t + T_PQ + k + 1)
                f(w_hi[b][:, :, :], ring[b][:, :, :]).then_inc(split_hi, 1)

            with act_e.Fori(0, PH // 2) as t:
                queries(t)

            act_e.wait_ge(tok_mm, 1)
            for b in range(4):
                f(h_tok[:, 4 * b:4 * b + 4, :], bank[b][:, :].rearrange("p (a n) -> p a n", a=4)).then_inc(tok_copied, 1)
            for q in range(JG):
                act_e.wait_ge(tile_done, T_EXP + q + 1)
                f(gel_first[:, q, :], bank[q % 4][:, 0:ND], ACT.Gelu_apprx_tanh).then_inc(u_gelu, 1)
                if q < JG - 2:
                    high(2 * PH + q + 2, q % 2, True)
            act_e.wait_ge(g_shift, 1)
            gv = route[:, 2, :, :, :].rearrange("p m h k -> p (m h k)")
            f(gv, gv, ACT.Exp).then_inc(g_exp, 1)
            for k in range(3):
                act_e.wait_ge(route_tr, k + 1)
                f(routeT[:, k, :], bank[4 + k][:, 0:ND]).then_inc(route_copied, 1)

            with act_e.Fori(0, NTB // 2) as t:
                for b in range(2):
                    act_e.wait_ge(tab_out[b], 16 * t)
                    for q in range(8):
                        act_e.wait_ge(tab_mm, 16 * t + 8 * b + q + 1)
                        f(wt[b][:, :, 4 * q:4 * q + 4].rearrange("p j t -> p t j"),
                          bank[q][:, :].rearrange("p (t j) -> p t j", t=4)).then_inc(tab_copied, 1)
            for b in range(2):
                act_e.wait_ge(tab_out[b], 16 * (NTB // 2))

            for m in range(2 * PH + JG, 2 * PH + JG + 2):
                high(m, m % 2, True)

            def experts(g, last, steps=range(16)):
                for q in steps:
                    act_e.wait_ge(tile_done, 16 * g + T_EXP + q + 1)
                    if q < JG:
                        act_e.wait_ge(act_ok, JG * g + max(q - 1, 0))
                        f(gel[q % 2][:, :], bank[q % 4][:, 0:ND], ACT.Gelu_apprx_tanh).then_inc(u_gelu, 1)
                    if not (last and q >= 14):
                        act_e.wait_ge(raw_in[q % 2], 128 * g + 16 * (PH + q // 2 + 1) + 16)
                        f(w_hi[q % 2][:, :, :], ring[q % 2][:, :, :]).then_inc(split_hi, 1)

            experts(0, False, range(JG, 16))
            with act_e.Fori(1, NG // 2) as g:
                experts(g, False)
            act_e.wait_ge(gath_free, 2 + PAIRS)
            f(g_act[:, :], g_dot[:, :], ACT.Gelu_apprx_tanh).then_inc(gath_gelu, 1)
            with act_e.Fori(NG // 2, NG - 1) as g:
                experts(g, False)
            experts(NG - 1, True)

        @block.vector
        def _(dve):
            v = nc.vector
            st = Steps(dve, dve_step)

            v.memset(ones[:, :], 1.0).then_inc(const_made, 1)
            v.memset(eps[:, :], EPS).then_inc(const_made, 1)

            dve.wait_ge(vec_in, 16 * 6)
            dve.wait_ge(norm_rt, 1)
            st.did(v.reciprocal(rt[0][:, 0:MEM], rt[0][:, 0:MEM]))
            st.wait()
            for c in range(KC):
                v.scalar_tensor_tensor(out=memT[:, c, :], in0=memT[:, c, :], scalar=vecs[:, 2 * KC + c:2 * KC + c + 1],
                                       in1=rt[0][:, 0:MEM], op0=ALU.mult, op1=ALU.mult).then_inc(mem_h, 1)

            dve.wait_ge(rel_in, 16)
            v.tensor_copy(rext[:, 0:P - 1], rext[:, P - 1:P].to_broadcast([HA, P - 1])).then_inc(rel_filled, 1)

            lam = lvec[:, 7, :]
            v.scalar_tensor_tensor(out=sp[:, 0, :], in0=lam, scalar=-1.0, in1=lam, op0=ALU.mult, op1=ALU.max).then_inc(lam_abs, 1)

            def head_norm(n, dst, width, gain, number):
                dve.wait_ge(head_rt, number)
                r = rt[n % 2][:, 0:width]
                st.did(v.reciprocal(r, r))
                st.wait()
                v.scalar_tensor_tensor(out=dst, in0=dst, scalar=gain, in1=r, op0=ALU.mult, op1=ALU.mult
                                       ).then_inc(head_ok, 1)

            for k in range(HC):
                head_norm(k, mk[:, k, :], MEM, hgain[:, 3:4], k + 1)

            dve.wait_ge(norm_rt, 2)
            st.did(v.reciprocal(rt[0], rt[0]))
            st.wait()
            for c in range(KC + 1):
                if c < KC:
                    v.scalar_tensor_tensor(out=hT[:, c, :], in0=xT[:, c, :], scalar=vecs[:, c:c + 1],
                                           in1=rt[0], op0=ALU.mult, op1=ALU.mult).then_inc(h_made, 1)
                if c:
                    dve.wait_ge(h_high, c)
                    v.tensor_tensor(norm_lo[:, c - 1, :], hT[:, c - 1, :], norm_hi[:, c - 1, :].bitcast(F32),
                                    ALU.subtract).then_inc(h_ready, 1)

            dve.wait_ge(lam_exp, 1)
            y, z, z2, s4 = sp[:, 1, :], sp[:, 2, :], sp[:, 3, :], sp[:, 4, :]

            def step(ins):
                st.did(ins)
                st.wait()

            step(v.tensor_scalar(z, y, 2.0, None, ALU.add))
            step(v.reciprocal(z, z))
            step(v.tensor_tensor(z, z, y, ALU.mult))
            step(v.tensor_tensor(z2, z, z, ALU.mult))
            step(v.memset(s4, 1.0 / 17))
            for odd in (15, 13, 11, 9, 7, 5, 3, 1):
                step(v.tensor_tensor(s4, s4, z2, ALU.mult))
                step(v.tensor_scalar(s4, s4, 1.0 / odd, None, ALU.add))
            step(v.tensor_tensor(s4, s4, z, ALU.mult))
            step(v.tensor_scalar(s4, s4, 8.0, None, ALU.mult))
            step(v.tensor_scalar(z, lam, -4.0, 0.0, ALU.mult, ALU.max))
            v.tensor_tensor(sp[:, 5, :], s4, z, ALU.add).then_inc(sp_ok, 1)

            for k in range(LC):
                dve.wait_ge(lin_copied, k + 1)
                step(v.tensor_scalar(xc[:, k, :], xl[:, k, 0:S], lvec[:, 0, k:k + 1], lvec[:, 4, k:k + 1],
                                     ALU.mult, ALU.add))
                for tap in range(1, TAPS):
                    ins = v.scalar_tensor_tensor(out=xc[:, k, :], in0=xl[:, k, tap:tap + S], scalar=lvec[:, tap, k:k + 1],
                                                 in1=xc[:, k, :], op0=ALU.mult, op1=ALU.add)
                    if tap < TAPS - 1:
                        step(ins)
                    else:
                        ins.then_inc(conv_ok, 1)

            def lru_factors(k):
                t = rg[:, k, :]
                dve.wait_ge(lru_tanh, k + 1)
                dve.wait_ge(lru_ok, k)
                step(v.tensor_scalar(lr, t, 1.0, None, ALU.add))
                step(v.reciprocal(lr, lr))
                step(v.tensor_scalar(la, t, -1.0, 1.0, ALU.mult, ALU.add))
                step(v.tensor_tensor(la, la, lr, ALU.mult))
                step(v.scalar_tensor_tensor(out=t, in0=t, scalar=4.0, in1=lr, op0=ALU.mult, op1=ALU.mult))
                step(v.tensor_tensor(t, t, lr, ALU.mult))
                v.tensor_scalar(t, t, 1e-12, 1.0, ALU.max, ALU.min).then_inc(lru_m2, 1)

            def lru_scan(k):
                u = ig[:, k, :]
                dve.wait_ge(lru_sig, LC + k + 1)
                step(v.tensor_tensor(u, u, xc[:, k, :], ALU.mult))
                dve.wait_ge(lru_mult, k + 1)
                step(v.tensor_tensor(u, u, rg[:, k, :], ALU.mult))
                step(v.tensor_tensor_scan(out=xc[:, k, :], data0=la, data1=u, initial=0.0, op0=ALU.mult, op1=ALU.add))
                dve.wait_ge(lin_copied, 2 * LC)
                v.tensor_tensor(gl[:, k, :], gl[:, k, :], xc[:, k, :], ALU.mult).then_inc(lru_ok, 1)

            dve.wait_ge(conv_ok, LC)
            for k in range(LC):
                lru_factors(k)
                head_norm(k, head_place(0, k), S, hgain[:, 0:1], k + HC + 1)
                lru_scan(k)
            with dve.Fori(1, N_QK // 4) as t:
                st.loop(t, 4, 1)
                for k in range(4):
                    head_norm(k, head_place(t, k), S, hgain[:, bass.ds(t // 2, 1)], 4 * t + k + HC + 1)
                st.end(N_QK // 4)

            dve.wait_ge(bias_in, 16)
            v.memset(tb[0:CHUNK, :, 2 * P - CHUNK:], NEG).then_inc(bias_ok, 1)
            dve.wait_ge(bias_ok, 1)

            def attention(a, heads, scores, s_of, dst, steps):
                def step(h, e, more):
                    for q in range(TT):
                        dve.wait_ge(a.exped, TT * h + q + 1)
                        st.did(v.reciprocal(rinv[:, e, q:q + 1], ssum[:, e, q:q + 1]))
                        st.wait()
                        v.tensor_scalar(s_of(e, q), s_of(e, q), rinv[:, e, q:q + 1], None, ALU.mult).then_inc(a.probs, 1)
                    if more:
                        scores(h + 2, e)
                    dve.wait_ge(a.mixed, h + 1)
                    v.tensor_scalar(dst[:, bass.ds(h, 1), :].rearrange("p a s -> p (a s)"), bank[7][:, :], 1.0, None,
                                    ALU.mult).then_inc(a.out, 1)

                for e in range(2):
                    scores(e, e)
                with dve.Fori(0, heads // 2 - 1) as t:
                    st.loop(t, 2 * (steps + TT))
                    for e in range(2):
                        step(2 * t + e, e, True)
                    st.end(heads // 2 - 1)
                for e in range(2):
                    step(heads - 2 + e, e, False)

            def band_scores(h, e):
                if not isinstance(h, int):
                    dve.wait_ge(at_a.turned, TT * (h - 1))
                for q in range(TT):
                    dve.wait_ge(at_a.scores, TT * h + q + 1)
                    near = max(q - 1, 0) * P
                    w = (q + 1) * P
                    row = band_s(e, q)
                    if near:
                        st.did(v.tensor_scalar(row[:, 0:near], bank[q][:, 0:near], SCALE,
                                               tb[:, bass.ds(h, 1), 0:1].rearrange("p a b -> p (a b)"), ALU.mult, ALU.add))
                    v.scalar_tensor_tensor(
                        out=row[:, near:w], in0=bank[q][:, near:w], scalar=SCALE,
                        in1=tb[:, bass.ds(h, 1), 2 * P - (w - near):].rearrange("p a b -> p (a b)"),
                        op0=ALU.mult, op1=ALU.add).then_inc(at_a.taken, 1)
                    if near:
                        st.wait()
                    dve.wait_ge(at_a.taken, TT * h + q + 1)
                    st.did(v.reduce_max(smax[:, e, q:q + 1], row, AX_X))
                    st.wait()
                    v.tensor_scalar(nmax[:, e, q:q + 1], smax[:, e, q:q + 1], -1.0, None, ALU.mult).then_inc(at_a.shifted, 1)

            def cross_scores(h, e):
                for q in range(TT):
                    dve.wait_ge(at_c.scores, TT * h + q + 1)
                    st.did(v.reduce_max(smax[:, e, q:q + 1], bank[q][:, 0:MEM], AX_X))
                    st.wait()
                    v.tensor_scalar(nmax[:, e, q:q + 1], smax[:, e, q:q + 1], -SCALE, None, ALU.mult).then_inc(at_c.shifted, 1)

            attention(at_a, HA, band_scores, band_s, qT, TT + 2)
            attention(at_c, HC, cross_scores, cross_s, qkc, TT)

            with dve.Fori(0, KC) as c:
                st.loop(c, 1)
                dve.wait_ge(tile_done, 4 * c + T_MIX + 4)
                for b in range(3):
                    dve.wait_ge(gate_ok, 3 * c + b + 1)
                    v.tensor_tensor(prod[:, b, :], sig[:, b, :], bank[3 + b][:, :], ALU.mult).then_inc(y_used, 1)
                dve.wait_ge(y_used, 3 * c + 3)
                st.did(v.tensor_tensor(prod[:, 0, :], prod[:, 0, :], prod[:, 1, :], ALU.add))
                st.wait()
                v.tensor_tensor(merged[:, bass.ds(c, 1), :].rearrange("p a s -> p (a s)"), prod[:, 0, :], prod[:, 2, :],
                                ALU.add).then_inc(merged_ok, 1)
                st.end(KC)

            for c in range(KC):
                dve.wait_ge(m_hi_ok, c + 1)
                v.tensor_tensor(h_lo[:, c, :], merged[:, c, :], h_hi[:, c, :].bitcast(F32), ALU.subtract
                                ).then_inc(m_ready, 1)

            dve.wait_ge(x_back, 64)
            with dve.Fori(0, KC // 4) as t:
                for k in range(4):
                    dve.wait_ge(tile_done, 4 * t + T_WO + k + 1)
                    xk = xT[:, bass.ds(4 * t + k, 1), :].rearrange("p a s -> p (a s)")
                    v.tensor_tensor(xk, xk, bank[k][:, :], ALU.add).then_inc(x2_ok, 1)
            dve.wait_ge(norm_rt, 3)
            step(v.reciprocal(rt2, rt2))
            for c in range(KC + 1):
                if c < KC:
                    if c >= 2:
                        dve.wait_ge(h2_ready, c - 1)
                    v.scalar_tensor_tensor(out=h2[c % 2], in0=xT[:, c, :], scalar=vecs[:, KC + c:KC + c + 1],
                                           in1=rt2, op0=ALU.mult, op1=ALU.mult).then_inc(h2_made, 1)
                if c:
                    dve.wait_ge(h2_hi, c)
                    v.tensor_tensor(h_lo[:, c - 1, :], h2[(c - 1) % 2], h_hi[:, c - 1, :].bitcast(F32), ALU.subtract
                                    ).then_inc(h2_ready, 1)
            dve.wait_ge(const_made, 4)
            v.tensor_copy(ident_r[:, :], ident[:, :]).then_inc(ident_ok, 1)
            dve.sem_inc(sc_free, 4)

            def best16(groups):
                def pause():
                    st.wait()
                    dve.sem_inc(wait_held, 1)

                dve.sem_inc(wait_held, 1)
                for half in (slice(0, 8), slice(8, 16)):
                    for s, val, idx in groups:
                        st.did(v.max(val[:, half], s))
                    pause()
                    for s, val, idx in groups:
                        st.did(v.max_index(idx[:, half], val[:, half], s))
                    pause()
                    if half.start == 0:
                        for s, val, idx in groups:
                            st.did(v.match_replace(s, val[:, half], s, LOWEST))
                        pause()

            with dve.Fori(0, PH // 2) as t:
                st.loop(t, 2 * (15 * TT + 12))
                for e in range(2):
                    for side in range(2):
                        k = 2 * e + side
                        dve.wait_ge(sc_copied, 4 * t + k + 1)
                        best16([(sc[:, k, m, :], sv[:, e, side, m, :], si[:, e, side, m, :]) for m in range(TT)])
                        dve.sem_inc(sc_free, 1)
                    step(v.tensor_tensor(cand, sv[:, e, 0, :, :].unsqueeze(3).to_broadcast([P, TT, TOPK, TOPK]),
                                         sv[:, e, 1, :, :].unsqueeze(2).to_broadcast([P, TT, TOPK, TOPK]), ALU.add))
                    best16([(cand[:, m, :, :].rearrange("p a b -> p (a b)"), fv[:, m, :], fpos[:, m, :]) for m in range(TT)])
                    pos = fpos.rearrange("p a b -> p (a b)")
                    st.did(v.tensor_scalar(fa, pos, 4, None, ALU.logical_shift_right))
                    step(v.tensor_scalar(fb, pos, TOPK - 1, None, ALU.bitwise_and))
                    for side, which in ((0, fa), (1, fb)):
                        st.did(v.tensor_tensor(pick[:, side, :, :], which.unsqueeze(2).to_broadcast([P, TT * TOPK, TOPK]),
                                               iota[:, 0:TOPK].unsqueeze(1).to_broadcast([P, TT * TOPK, TOPK]), ALU.is_equal))
                    st.wait()
                    for side in range(2):
                        pk = pick[:, side, :, :].rearrange("p (m k) n -> p m k n", m=TT)
                        st.did(v.tensor_tensor(pk, pk, si[:, e, side, :, :].unsqueeze(2).to_broadcast([P, TT, TOPK, TOPK]), ALU.mult))
                    st.wait()
                    for side, dst in ((0, ires), (1, jres)):
                        st.did(v.reduce_sum(dst.rearrange("p m k -> p (m k)"), pick[:, side, :, :], AX_X))
                    st.wait()
                    for which, src in ((0, ires), (1, jres), (2, fv)):
                        dst = route[:, which, :, bass.ds(2 * t + e, 1), :].rearrange("p m a k -> p m (a k)")
                        st.did(v.tensor_scalar(dst, src, 0.0, None, ALU.add))
                    st.wait()
                st.end(PH // 2)

            gv = route[:, 2, :, :, :].rearrange("p m h k -> p (m h) k")
            step(v.reduce_max(gmx, gv, AX_X))
            v.tensor_tensor(gv, gv, gmx.unsqueeze(2).to_broadcast([P, TT * PH, TOPK]), ALU.subtract).then_inc(g_shift, 1)
            dve.wait_ge(g_exp, 1)
            step(v.reduce_sum(gsum, gv, AX_X))
            step(v.reciprocal(grec, gsum))
            v.tensor_tensor(gv, gv, grec.unsqueeze(2).to_broadcast([P, TT * PH, TOPK]), ALU.mult).then_inc(route_ok, 1)

            gi, gj, gw = (route[:, w, TG, :, :].rearrange("p h k -> p (h k)") for w in range(3))
            step(v.scalar_tensor_tensor(out=g_idx[:, :], in0=gi, scalar=float(NKEYS), in1=gj, op0=ALU.mult, op1=ALU.add))
            step(v.tensor_copy(g_w[:, :], gw))
            dve.wait_ge(route_tr, 3)
            dve.sem_inc(gath_free, 2)
            dve.wait_ge(tok_mm, 1)
            v.memset(g_acc, 0.0).then_inc(acc_zero, 1)

            dve.wait_ge(route_copied, 3)

            def one_hots(t, first):
                for q in range(4):
                    if not first or q >= 2:
                        dve.wait_ge(tab_mm, 8 * t + 2 * q - 2)
                    v.tensor_tensor(ohA[q % 2][:, :, :], iota[:, :].unsqueeze(1).to_broadcast([P, HT, P]),
                                    routeT[:, 0, bass.ds(TB * t + HT * q, HT)].unsqueeze(2).to_broadcast([P, HT, P]),
                                    ALU.is_equal).then_inc(oh_a, 1)
                    for n in range(HT):
                        tok = TB * t + HT * q + n
                        ins = v.tensor_scalar(ohB[q % 2][:, n, :], iota[:, :], routeT[:, 1, bass.ds(tok, 1)],
                                              routeT[:, 2, bass.ds(tok, 1)], ALU.is_equal, ALU.mult)
                    ins.then_inc(oh_b, 1)

            one_hots(0, True)
            with dve.Fori(1, NTB) as t:
                one_hots(t, False)

            def low(b, number):
                dve.wait_ge(split_hi, number)
                v.tensor_tensor(w_lo[b][:, :, :], ring[b][:, :, :], w_hi[b][:, :, :].bitcast(F32), ALU.subtract
                                ).then_inc(split_lo, 1)

            for m in range(2 * PH + JG, 2 * PH + JG + 2):
                low(m % 2, m + 1)
            dve.wait_ge(tok_copied, 4)

            def dot(g, q):
                dve.wait_ge(gath_in[q % 2], 128 * g + 16 * (q // 2) + 16)
                row = grow[q % 2][:, :].rearrange("p (a n) -> p a n", a=KC)
                v.scalar_tensor_tensor(out=row, in0=row, scalar=1.0, in1=h_tok, op0=ALU.mult, op1=ALU.mult,
                                       accum_out=g_dot[:, bass.ds(16 * g + q, 1)]).then_inc(gath_free, 1)

            def gather_add(g, q):
                dve.wait_ge(gath_in[q % 2], 128 * g + 16 * (q // 2) + 16)
                dve.wait_ge(gath_free, 16 * g + q + 2)
                row = grow[q % 2][:, :].rearrange("p (a n) -> p a n", a=KC)
                v.scalar_tensor_tensor(out=g_acc, in0=row, scalar=g_act[:, bass.ds(16 * g + q - PAIRS, 1)], in1=g_acc,
                                       op0=ALU.mult, op1=ALU.add).then_inc(gath_free, 1)

            def weigh(g, q, gelu):
                prod = gel[q % 2][:, :]
                v.tensor_tensor(prod.rearrange("p (a b) -> p a b", a=NTB), gelu.rearrange("p (a b) -> p a b", a=NTB),
                                wg[:, :, q, :], ALU.mult).then_inc(act_part, 1)
                dve.wait_ge(act_part, 2 * JG * g + 2 * q + 1)
                v.tensor_copy(act_hi[:, q, :], prod).then_inc(act_part, 1)
                dve.wait_ge(act_part, 2 * JG * g + 2 * q + 2)
                v.tensor_tensor(act_lo[:, q, :], prod, act_hi[:, q, :].bitcast(F32), ALU.subtract).then_inc(act_ok, 1)

            def add_outputs(g, q):
                dve.wait_ge(tile_done, 16 * g + T_EXP + q + 1)
                for c in (2 * (q - JG), 2 * (q - JG) + 1):
                    v.tensor_tensor(xT[:, c, 0:ND], xT[:, c, 0:ND], bank[4 + c % 4][:, 0:ND], ALU.add).then_inc(y_added, 1)

            def experts(g, last, gathered):
                dve.wait_ge(wg_in, 16 * g + 16)
                for q in range(16):
                    if q < JG:
                        dve.wait_ge(u_gelu, JG * g + q + 1)
                        weigh(g, q, gel[q % 2][:, :])
                    else:
                        add_outputs(g, q)
                    if not (last and q >= 14):
                        low(q % 2, 16 * g + q + 2 * PH + 3)
                    gathered(g, q)

            for n in range(EARLY):
                dot(0, n)
            dve.wait_ge(wg_in, 16)
            dve.wait_ge(u_gelu, JG)
            for q in range(JG):
                if q >= 2:
                    dve.wait_ge(act_ok, q - 1)
                weigh(0, q, gel_first[:, q, :])
            for q in range(JG, 16):
                add_outputs(0, q)
                low(q % 2, q + 2 * PH + 3)
                for n in range(EARLY + (16 - EARLY) * (q - JG) // JG, EARLY + (16 - EARLY) * (q - JG + 1) // JG):
                    dot(0, n)
            with dve.Fori(1, NG // 2) as g:
                experts(g, False, dot)
            dve.wait_ge(gath_gelu, 1)
            v.tensor_tensor(g_act[:, :], g_act[:, :], g_w[:, :], ALU.mult).then_inc(gath_act, 1)
            dve.wait_ge(gath_act, 1)
            dve.wait_ge(acc_zero, 1)
            with dve.Fori(NG // 2, NG - 1) as g:
                experts(g, False, gather_add)
            experts(NG - 1, True, gather_add)
            for b in range(4):
                dve.wait_ge(tail_tr, b + 1)
                v.tensor_tensor(xT[:, 4 * b:4 * b + 4, ND:], xT[:, 4 * b:4 * b + 4, ND:],
                                bank[b][:, :].rearrange("p (a n) -> p a n", a=4), ALU.add).then_inc(tail_added, 1)

        @block.tensor
        def _(pe):
            def mm(out, lhsT, rhs, start=True, stop=True):
                return nc.tensor.matmul(out, lhsT, rhs, start=start, stop=stop)

            def project(n, out, rhs, turn=None, per=0, ks=range(KC), inc=True):
                landed(pe, n, turn, per)
                for k in ks:
                    ins = mm(out, ring[n % SLOTS][:, k, :], rhs(k), start=(k == ks[0]), stop=(k == ks[-1]))
                if inc:
                    ins.then_inc(tile_done, 1)

            def head_sum(n, width, number):
                pe.wait_ge(head_sq, number)
                mm(bank[4 + n % 2][:, 0:width], ones[:, :], sq[n % 2][:, 0:width]).then_inc(head_ss, 1)

            pe.wait_ge(const_made, 4)
            pe.wait_ge(mem_sq, 1)
            for c in range(KC):
                ins = mm(bank[6][:, 0:MEM], ones[:, :], msq[:, c, :], start=(c == 0), stop=(c == KC - 1))
            ins.then_inc(norm_ss, 1)
            pe.wait_ge(mem_h, KC)
            for k in range(HC):
                project(T_MK + k, bank[k][:, 0:MEM], lambda c: memT[:, c, :])
                if k:
                    if k >= 3:
                        pe.wait_ge(head_rt, k - 2)
                    head_sum(k - 1, MEM, k)
            for c in range(KC):
                pe.wait_ge(x_sq, c // 4 + 1)
                ins = mm(bank[6][:, :], ones[:, :], xsq[:, c, :], start=(c == 0), stop=(c == KC - 1))
            ins.then_inc(norm_ss, 1)
            pe.wait_ge(head_rt, HC - 2)
            head_sum(HC - 1, MEM, HC)

            pe.wait_ge(acc_copied, HC)
            pe.wait_ge(head_sq, HC)
            for n in range(4):
                landed(pe, T_MV + n)
                w = ring[n][:, :, :].rearrange("p (c a) b -> p c (a b)", c=4)
                for c in range(4):
                    for m in range(MT):
                        ins = mm(bank[2 + m][:, :], memT[:, 4 * n + c, m * P:(m + 1) * P], w[:, c, :],
                                 start=(n == 0 and c == 0), stop=(n == 3 and c == 3))
                ins.then_inc(tile_done, 1)

            def split_mm(out, wh, wl, rh, rl, start, stop):
                mm(out, wh, rh, start=start, stop=False)
                mm(out, wh, rl, start=False, stop=False)
                return mm(out, wl, rh, start=False, stop=stop)

            def project_split(number, out, r_hi, r_lo, between=None):
                for q in range(4):
                    pe.wait_ge(quarter_lo, 4 * number + q + 1)
                    for c in range(4 * q, 4 * q + 4):
                        ins = split_mm(out, p_hi[:, c, :], p_lo[:, c, :], r_hi[:, c, :], r_lo[:, c, :], c == 0, c == KC - 1)
                    ins.then_inc(part_used if q < 3 else tile_done, 1)
                    if q == 0 and between is not None:
                        between()

            pe.wait_ge(h_ready, KC)
            pe.wait_ge(v_copied, MT)
            pe.wait_ge(head_rt, HC)

            def lru_gates(side):
                pe.wait_ge(lw_in, 64)
                pe.wait_ge(conv_ok, LC)
                for k in range(LC):
                    if side:
                        pe.wait_ge(lru_sig, k + 1)
                    mm(bank[4 + k][:, :], lw[:, side, k, :], xc[:, k, :]).then_inc(lru_mm, 1)

            for k in range(2 * LC):
                if k >= LC:
                    pe.wait_ge(lin_copied, k - LC + 1)
                project_split(k, bank[k % LC][:, :], norm_hi, norm_lo, (lambda: lru_gates(0)) if k == 2 * LC - 1 else None)

            def last_head(t, k):
                pe.wait_ge(head_rt, 4 * t + k + HC - 2)
                head_sum((k - 1) % 4, S, 4 * t + k + HC)

            def heads(t, first):
                for k in range(4):
                    if first:
                        pe.wait_ge(lin_copied, LC + k + 1)
                    else:
                        pe.wait_ge(head_sq, 4 * t + HC + k - 3)
                    if first and k == 1:
                        pe.wait_ge(lru_sig, 2 * LC)
                    project_split(4 * t + S_QK + k, bank[k][:, :], norm_hi, norm_lo,
                                  (lambda: lru_gates(1)) if first and k == 0 else lambda: last_head(t, k))

            heads(0, True)
            with pe.Fori(1, N_QK // 4) as t:
                heads(t, False)
            for half in range(2):
                if half:
                    pe.wait_ge(head_rt, HC + N_QK)
                for n in range(4):
                    wh, wl = (w[:, :, :].rearrange("p (c a) b -> p c (a b)", c=4) for w in (p_hi, p_lo))
                    for c in range(4):
                        pe.wait_ge(quarter_lo, 4 * (S_V + 4 * half + n) + c + 1)
                        for m in range(TT):
                            if half == 0 and n == 0 and c == 0:
                                pe.wait_ge(head_sq, HC + N_QK - TT + m + 1)
                            tok = slice(m * P, (m + 1) * P)
                            ins = split_mm(bank[4 * half + m][:, :], norm_hi[:, 4 * n + c, tok], norm_lo[:, 4 * n + c, tok],
                                           wh[:, c, :], wl[:, c, :], n == 0 and c == 0, n == 3 and c == 3)
                        ins.then_inc(part_used if c < 3 else tile_done, 1)
                        if half == 0 and n == 0 and c == 0:
                            last_head(N_QK // 4, 0)


            def band_scores(h, e):
                pe.wait_ge(at_a.staged_q, h + 1)
                pe.wait_ge(at_a.taken, TT * h)
                for q in range(TT):
                    mm(bank[q][:, 0:(q + 1) * P], qs[e][:, q * P:(q + 1) * P],
                       kT[:, bass.ds(h, 1), 0:(q + 1) * P].rearrange("p a s -> p (a s)")).then_inc(at_a.scores, 1)

            def cross_scores(h, e):
                pe.wait_ge(at_c.staged_q, h + 1)
                pe.wait_ge(at_c.exped, TT * h)
                for q in range(TT):
                    mm(bank[q][:, 0:MEM], qs[e][:, q * P:(q + 1) * P],
                       mk[:, bass.ds(h, 1), :].rearrange("p a s -> p (a s)")).then_inc(at_c.scores, 1)

            def attention(a, heads, scores, turn, tiles, mix):
                def step(h, e, more):
                    pe.wait_ge(a.probsT, tiles * h)
                    for q in range(TT):
                        pe.wait_ge(a.probs, TT * h + q + 1)
                        turn(e, q)
                    if more:
                        scores(h + 2, e)
                    pe.wait_ge(a.staged_v, h + 1)
                    pe.wait_ge(a.out, h)
                    for kt in range(tiles):
                        pe.wait_ge(a.probsT, tiles * h + kt + 1)
                        ins = mix(e, kt)
                    ins.then_inc(a.mixed, 1)

                in_pairs(pe, heads, scores, step)

            def band_turn(e, q):
                for kt in range(q + 1):
                    ins = nc.tensor.transpose(t_ps[kt][:, (q - kt) * P:(q - kt + 1) * P],
                                              band_s(e, q)[:, kt * P:(kt + 1) * P], ident[:, :])
                    if q == TT - 1:
                        ins.then_inc(at_a.turned, 1)

            def cross_turn(e, q):
                for kt in range(MT):
                    ins = nc.tensor.transpose(bank[4 + kt][:, q * P:(q + 1) * P], cross_s(e, q)[:, kt * P:(kt + 1) * P],
                                              ident[:, :])
                    if q == TT - 1:
                        ins.then_inc(at_c.turned, 1)

            attention(at_a, HA, band_scores, band_turn, TT,
                      lambda e, kt: mm(bank[7][:, kt * P:], vs[e][:, kt, :], pT[kt], start=(kt == 0), stop=(kt == TT - 1)))
            pe.wait_ge(at_a.out, HA)
            attention(at_c, HC, cross_scores, cross_turn, MT,
                      lambda e, kt: mm(bank[7][:, :], vs[e][:, kt, :], pTc[kt], start=(kt == 0), stop=(kt == MT - 1)))

            pe.wait_ge(at_c.out, HC)
            branch = ([qT[:, k, :] for k in range(HA)], [gl[:, k, :] for k in range(LC)], [qkc[:, k, :] for k in range(HC)])
            with pe.Fori(0, KC) as c:
                for b in range(3):
                    pe.wait_ge(gate_ok, 3 * c)
                    project_split(3 * c + S_MIX + b, bank[b][:, :], norm_hi, norm_lo)
                pe.wait_ge(y_used, 3 * c)
                pe.wait_ge(pair_in[1], 32 * c + 16 * (S_MIX // 2 + 2))
                n = 0
                for b, parts in enumerate(branch):
                    for k, part in enumerate(parts):
                        ins = mm(bank[3 + b][:, :], ring[1][:, n, :], part, start=(k == 0), stop=(k == len(parts) - 1))
                        n += 1
                ins.then_inc(tile_done, 1)

            pe.wait_ge(m_ready, KC)
            with pe.Fori(0, KC // 4) as t:
                for k in range(4):
                    pe.wait_ge(x2_ok, 4 * t)
                    project_split(4 * t + S_WO + k, bank[k][:, :], h_hi, h_lo)
            pe.wait_ge(x2_sum, KC + 1)
            mm(bank[6][:, :], ones[:, :], sumsq).then_inc(norm_ss, 1)

            pe.wait_ge(keys_in, 16)

            def scores(n, k):
                pe.wait_ge(pq_copied, n + 1)
                for m in range(TT):
                    ins = mm(bank[4 + k][:, m * P:(m + 1) * P], qp[:, k, m * P:(m + 1) * P],
                             kys[:, bass.ds(n, 1), :].rearrange("p a n -> p (a n)"))
                ins.then_inc(pq_scores, 1)

            def queries(t, first):
                for k in range(4):
                    b = k % 2
                    pe.wait_ge(split_lo, 4 * t + k + 1)
                    for c in range(KC):
                        pe.wait_ge(h2_ready, c + 1)
                        ins = split_mm(bank[k][:, :], w_hi[b][:, c, :], w_lo[b][:, c, :], h_hi[:, c, :], h_lo[:, c, :],
                                       c == 0, c == KC - 1)
                        if c == KC // 2 - 1 and not (first and k == 0):
                            if not first:
                                pe.wait_ge(sc_copied, 4 * t + k - 4)
                            scores(4 * t + k - 1, (k - 1) % 4)
                    ins.then_inc(tile_done, 1)

            queries(0, True)
            with pe.Fori(1, PH // 2) as t:
                queries(t, False)
            scores(2 * PH - 1, 3)

            pe.wait_ge(ident_ok, 1)
            pe.wait_ge(pq_copied, 2 * PH)
            for c in range(KC):
                dst = bank[c // 4][:, (c % 4) * P:(c % 4 + 1) * P]
                mm(dst, h_hi[:, c, ND:], ident_r[:, :], start=True, stop=False)
                ins = mm(dst, h_lo[:, c, ND:], ident_r[:, :], start=False, stop=True)
            ins.then_inc(tok_mm, 1)

            def u_products(g):
                for j in range(JG):
                    b = j % 2
                    pe.wait_ge(split_lo, 16 * g + 2 * PH + j + 1)
                    pe.wait_ge(u_gelu, JG * g + max(j - 3, 0))
                    for c in range(KC):
                        ins = split_mm(bank[j % 4][:, 0:ND], w_hi[b][:, c, :], w_lo[b][:, c, :],
                                       h_hi[:, c, 0:ND], h_lo[:, c, 0:ND], c == 0, c == KC - 1)
                    ins.then_inc(tile_done, 1)

            pe.wait_ge(tok_copied, 4)
            u_products(0)

            pe.wait_ge(route_ok, 1)
            pe.wait_ge(sc_copied, 2 * PH)
            for w in range(3):
                for m in range(TG):
                    ins = nc.tensor.transpose(bank[4 + w][:, m * P:(m + 1) * P],
                                              route[:, w, m, :, :].rearrange("p h k -> p (h k)"), ident[:, :])
                ins.then_inc(route_tr, 1)

            pe.wait_ge(route_copied, 3)
            pe.wait_ge(u_gelu, JG)

            def tables(t, first):
                for q in range(4):
                    pe.wait_ge(oh_a, 4 * t + q + 1)
                    pe.wait_ge(oh_b, 4 * t + q + 1)
                    for b in (2 * q, 2 * q + 1):
                        if not first:
                            pe.wait_ge(tab_copied, 8 * t + b - 7)
                        for n in range(4):
                            row = 4 * (b % 2) + n
                            ins = mm(bank[b][:, n * P:(n + 1) * P], ohA[q % 2][:, row, :], ohB[q % 2][:, row, :])
                        ins.then_inc(tab_mm, 1)

            tables(0, True)
            with pe.Fori(1, NTB) as t:
                tables(t, False)

            pe.wait_ge(tab_copied, 8 * NTB)

            def v_products(g):
                for c in range(KC):
                    b = (c // 2) % 2
                    if c % 2 == 0:
                        pe.wait_ge(split_lo, 16 * g + 2 * PH + JG + c // 2 + 1)
                    pe.wait_ge(y_added, KC * g + max(c - 3, 0))
                    for j in range(JG):
                        if c == 0:
                            pe.wait_ge(act_ok, JG * g + j + 1)
                        part = JG * (c % 2) + j
                        ins = split_mm(bank[4 + c % 4][:, 0:ND], w_hi[b][:, part, :], w_lo[b][:, part, :],
                                       act_hi[:, j, :], act_lo[:, j, :], j == 0, j == JG - 1)
                    if c % 2:
                        ins.then_inc(tile_done, 1)

            v_products(0)
            with pe.Fori(1, NG) as g:
                u_products(g)
                v_products(g)

            pe.wait_ge(gath_free, 2 + 2 * PAIRS)
            for c in range(KC):
                ins = nc.tensor.transpose(bank[c // 4][:, (c % 4) * P:(c % 4 + 1) * P], g_acc[:, c, :], ident[:, :])
                if c % 4 == 3:
                    ins.then_inc(tail_tr, 1)


def stationary(w):
    k, n = w.shape
    return np.ascontiguousarray(w.reshape(k // P, P, n // P, P).transpose(2, 1, 0, 3)).reshape(n // P, P, -1)


def moving(w):
    k, n = w.shape
    v = w.reshape(4, 4, P, n // 512, 512).transpose(3, 0, 2, 1, 4)
    return np.ascontiguousarray(v).reshape(-1, P, 2048)


def by_partition(vec):
    return np.ascontiguousarray(vec.reshape(-1, P).T)


def layout(a):
    w_in = a["w_in"]
    qkv = HA * DH
    lru0 = 3 * qkv
    xq0 = lru0 + 2 * LC * P
    lru_w = np.stack([a[n].reshape(LC, 2, 64, 64).transpose(1, 2, 0, 3) for n in ("lru_wa", "lru_wx")])
    lru_vec = np.stack([*(a["conv_w"][i] for i in range(TAPS)), a["conv_b"], a["lru_ba"], a["lru_bx"], a["lru_lambda"]])
    mix = np.stack([*(stationary(a["w_gate"][:, b * D:(b + 1) * D]) for b in range(3)), stationary(a["w_branch"])], axis=1)
    u = a["peer_u"].reshape(P, NG, JG, KC, P).transpose(1, 2, 4, 3, 0).reshape(NG, JG, P, 2048)
    v = a["peer_v"].reshape(P, NG, JG, KC // 2, 2, P).transpose(1, 3, 0, 4, 2, 5).reshape(NG, KC // 2, P, 2048)
    tokens = lambda x: np.ascontiguousarray(x[0].T.reshape(KC, P, -1).transpose(1, 0, 2))
    return {
        "x_t": tokens(a["x"]), "mem_t": tokens(a["mem"]),
        "g1": by_partition(a["norm1_g"]), "g2": by_partition(a["norm2_g"]), "gmem": by_partition(a["mem_norm_g"]),
        "head_g": np.stack([a[n] for n in ("attn_q_norm_g", "attn_k_norm_g", "xq_norm_g", "xk_norm_g")], axis=1),
        "w_memk": stationary(a["w_mem_kv"][:, :HC * DH]), "w_memv": moving(a["w_mem_kv"][:, HC * DH:]),
        "w_qk": np.concatenate([stationary(w_in[:, :2 * qkv]), stationary(w_in[:, xq0:])]),
        "w_lru_in": stationary(w_in[:, lru0:xq0]), "w_v": moving(w_in[:, 2 * qkv:lru0]),
        "rel_rev": np.ascontiguousarray(a["rel_bias"][:, ::-1]), "lru_w": np.ascontiguousarray(lru_w),
        "lru_vec": np.ascontiguousarray(lru_vec.reshape(8, LC, P).transpose(2, 0, 1)),
        "w_mix": mix.reshape(4 * KC, P, 2048), "b_gate": by_partition(a["b_gate"]),
        "w_o": stationary(a["w_o"]), "w_pq": stationary(a["w_peer_q"]),
        "keys": np.ascontiguousarray(a["peer_keys"].reshape(2 * PH, NKEYS, P).transpose(2, 0, 1)),
        "w_exp": np.concatenate([u, v], axis=1).reshape(16 * NG, P, 2048),
        "u_rows": a["peer_u"], "v_rows": a["peer_v"],
    }


def kernel(**inputs):
    import concourse.bacc as bacc
    from concourse.bass_utils import run_bass_kernel_spmd

    nc = bacc.Bacc("TRN2", target_bir_lowering=False, num_devices=1)
    arrays = {n: np.ascontiguousarray(v) for n, v in layout({n: np.asarray(v) for n, v in inputs.items()}).items()}
    args = [nc.dram_tensor(n, v.shape, mybir.dt.from_np(v.dtype), kind="ExternalInput").ap() for n, v in arrays.items()]
    out_t = nc.dram_tensor("out_t", (P, KC, S), F32, kind="ExternalOutput").ap()
    hybrid_block(nc, *args, out_t)
    r = run_bass_kernel_spmd(nc, [arrays], core_ids=[0])
    o = r.results[0]["out_t"]
    return np.ascontiguousarray(o.transpose(2, 1, 0).reshape(1, S, D))
```

```python
from contextlib import ExitStack

import concourse.bass as bass
import numpy as np
from concourse import mybir

F32 = mybir.dt.float32
U32 = mybir.dt.uint32
F32R = mybir.dt.float32r
ALU = mybir.AluOpType
ACT = mybir.ActivationFunctionType
AX_X = mybir.AxisListType.X

P = 128
D = 2048
KC = D // P
S = 512
TT = S // P
MEM = 256
MT = MEM // P
CHUNK = 64
HA = 8
HC = 4
DH = 128
LC = 4
TAPS = 4
CLIP = 128
NREL = 2 * CLIP + 1
EXT = 3 * P
PH = 8
NKEYS = 128
TOPK = 16
JG = 8
NG = NKEYS // JG
ND = S - P
TG = TT - 1
TB = 32
NTB = ND // TB
HT = TB // 4
PAIRS = PH * TOPK
EPS = 1e-6
NEG = -1e30
LOWEST = -3.0e38
SCALE = float(DH) ** -0.5

SLOTS = 4
T_MK = 0
T_MV = T_MK + HC
T_LRU = T_MV + 4
T_QK = T_LRU + 2 * LC
N_QK = 2 * HA + HC
T_V = T_QK + N_QK
T_MIX = T_V + 8
T_WO = T_MIX + 4 * KC
T_PQ = T_WO + KC
S_QK = T_QK - T_LRU
S_V = T_V - T_LRU
S_MIX = T_MIX - T_LRU
S_WO = T_WO - T_LRU
T_EXP = T_PQ + 2 * PH


class Steps:

    def __init__(self, eng, sem):
        self.eng, self.sem, self.start, self.n, self.turn, self.per = eng, sem, 0, 0, None, 0

    def loop(self, turn, per, first=0):
        self.start, self.n, self.turn, self.per = self.start + self.n - first * per, 0, turn, per

    def end(self, turns):
        assert self.n == self.per, (self.n, self.per)
        self.start, self.n, self.turn = self.start + turns * self.per, 0, None

    def did(self, ins):
        ins.then_inc(self.sem, 1)
        self.n += 1
        return self.n

    def wait(self, n=None):
        n = self.start + (self.n if n is None else n)
        self.eng.wait_ge(self.sem, n if self.turn is None else self.turn * self.per + n)


def hybrid_block(nc, x_t, mem_t, g1, g2, gmem, head_g, w_memk, w_memv, w_qk, w_lru_in, w_v, rel_rev,
                 lru_w, lru_vec, w_mix, b_gate, w_o, w_pq, keys, w_exp, u_rows, v_rows, out_t):
    ctx = ExitStack()
    with ctx:
        def sb(name, shape, dt=F32):
            return ctx.enter_context(nc.sbuf_tensor(name, shape, dt))

        def sem(name):
            return ctx.enter_context(nc.semaphore(name))

        ones = sb("ones", [P, P])
        ident = sb("ident", [P, P])
        iota = sb("iota", [P, P])
        vecs = sb("vecs", [P, 3 * KC])
        hgain = sb("hgain", [P, 4])
        bgate = sb("bgate", [P, 3 * KC])
        lvec = sb("lvec", [P, 8, LC])
        sp = sb("sp", [P, 6, LC])
        eps = sb("eps", [P, 1])
        rext = sb("rext", [HA, EXT])
        smax = sb("smax", [P, 2, TT])
        nmax = sb("nmax", [P, 2, TT])
        ssum = sb("ssum", [P, 2, TT])
        rinv = sb("rinv", [P, 2, TT])

        QM, KV, QC, GL, XL = 0, 4096, 12288, 14336, 16384
        MK, MV, TZ, Z = 18448, 19472, 20496, 22544
        base = -(-nc.sbuf_base // 64) * 64

        def place(name, kib, dims, dt=F32):
            return nc.alloc_sbuf_tensor_at(name, [P, *dims], dt, offset=base + int(kib * 1024))

        xT = place("xT", 0, [KC, S])
        hT = place("hT", 32, [KC, S])
        ring = [place(f"ring{i}", 64 + 8 * i, [16, P]) for i in range(SLOTS)]
        arena = place("arena", 96, [Z + 4096])
        p_hi = place("p_hi", 80, [16, P], F32R)
        p_lo = place("p_lo", 88, [16, P], F32R)
        norm_hi = place("norm_hi", 0, [KC, S], F32R)
        norm_lo = place("norm_lo", 32, [KC, S], F32R)
        mix_hi = [place("mix_hi_a", 160, [12, S], F32R), place("mix_hi_b", 190.25, [4, S], F32R)]
        mix_lo = [place("mix_lo_a", 96, [HA, S], F32R), place("mix_lo_b", 152, [LC, S], F32R),
                  place("mix_lo_c", 144, [HC, S], F32R)]
        w_hi = [place(f"w_hi{i}", 80 + 16 * i, [16, P], F32R) for i in range(2)]
        w_lo = [place(f"w_lo{i}", 88 + 16 * i, [16, P], F32R) for i in range(2)]
        h_hi = place("h_hi", 32, [KC, S], F32R)
        h_lo = place("h_lo", 112, [KC, S], F32R)
        h_tok = place("h_tok", 32, [KC, S])[:, :, ND:]
        g_acc = place("g_acc", 112, [KC, S])[:, :, ND:]
        wt = [place(f"wt{i}", 80 + 16 * i, [NKEYS, TB]) for i in range(2)]
        ohA = [place(f"ohA{i}", 165 + 4 * i, [HT, P]) for i in range(2)]
        ohB = [place(f"ohB{i}", (156, 173, 177)[i], [HT, P]) for i in range(3)]
        gel_first = place("gel_first", 144, [JG, ND])
        act_hi = place("act_hi", 144, [JG, ND], F32R)
        act_lo = place("act_lo", 156, [JG, ND], F32R)
        wg = place("wg", 168, [NTB, JG, TB])
        gel = [place(f"gel{i}", 180 + 1.5 * i, [ND]) for i in range(2)]
        grow = [place(f"grow{i}", 183 + 8 * i, [D]) for i in range(2)]
        g_idx = place("g_idx", 200.5, [PAIRS], U32)
        g_w = place("g_w", 201, [PAIRS])
        g_dot = place("g_dot", 201.5, [PAIRS])
        g_act = place("g_act", 202, [PAIRS])
        g_col = [place(f"g_col{i}", 202.5 + i / 16, [1], U32) for i in range(2)]
        ident_r = place("ident_r", 203, [P], F32R)

        def at(offset, *dims):
            n = int(np.prod(dims))
            v = arena[:, offset:offset + n]
            if len(dims) == 1:
                return v
            names = "abcd"[:len(dims)]
            return v.rearrange(f"p ({' '.join(names)}) -> p {' '.join(names)}", **dict(zip(names[1:], dims[1:])))

        memT = at(QM, KC, MEM)
        xsq = at(KV, KC, S)
        msq = at(QC, KC, MEM)
        qT = at(QM, HA, S)
        kT = at(KV, HA, S)
        vA = at(KV + 4096, TT, HA * DH)
        qkc = at(QC, HC, S)
        gl = at(GL, LC, S)
        xl = at(XL, LC, S + TAPS - 1)
        mk = at(MK, HC, MEM)
        mv = at(MV, MT, HC * DH)
        rt = [at(Z + 1024 * i, S) for i in range(2)]
        sq = [at(Z + 1024 * i + 512, S) for i in range(2)]
        lw = at(TZ, 2, LC, P)
        xc = at(KV + 4096, LC, S)
        rg = at(KV + 6144, LC, S)
        ig = at(XL, LC, S)
        la = at(TZ + 1024, S)
        lr = at(TZ + 1536, S)
        tb = at(TZ, HA, 2 * P)
        s_at = [P * q * (q + 1) // 2 for q in range(TT + 1)]
        s_sb = [at(Z + s_at[TT] * e, s_at[TT]) for e in range(2)]
        pT = [at(Z + 2 * s_at[TT] + (0, 512, 896, 1152)[kt], (TT - kt) * P) for kt in range(TT)]
        pTc = [at(Z + 2 * s_at[TT] + 512 * kt, S) for kt in range(MT)]
        qs = [at(XL + 512 * e, S) for e in range(2)]
        vs = [at(XL + 1024 + 512 * e, TT, DH) for e in range(2)]
        merged = at(KV, KC, S)
        sig = at(Z, 3, S)
        branches = [qT[:, k, :] for k in range(HA)] + [gl[:, k, :] for k in range(LC)] + [qkc[:, k, :] for k in range(HC)]
        branch_hi = [mix_hi[k // 12][:, k % 12, :] for k in range(KC)]
        branch_lo = [mix_lo[w][:, k, :] for w, n in enumerate((HA, LC, HC)) for k in range(n)]
        sumsq = at(Z, S)
        sqx = at(Z + 512, S)
        rt2 = at(Z + 1024, S)
        h2 = [at(Z + 1536 + 512 * i, S) for i in range(2)]
        kys = at(QC, 2 * PH, NKEYS)
        qp = at(GL, SLOTS, S)
        sc = at(XL, SLOTS, TT, NKEYS)
        sv = at(MK, 2, 2, TT, TOPK)
        si = at(MK + 256, 2, 2, TT, TOPK).bitcast(U32)
        fpos = at(MK + 512, TT, TOPK).bitcast(U32)
        fa = at(MK + 576, TT * TOPK).bitcast(U32)
        fb = at(MK + 640, TT * TOPK).bitcast(U32)
        fv = at(MK + 704, TT, TOPK)
        ires = at(MK + 768, TT, TOPK)
        jres = at(MK + 832, TT, TOPK)
        cand = at(Z, TT, TOPK, TOPK)
        pick = at(Z + 1024, 2, TT * TOPK, TOPK)
        route = at(TZ, 3, TT, PH, TOPK)
        gmx = at(MV, TT * PH)
        gsum = at(MV + 32, TT * PH)
        grec = at(MV + 64, TT * PH)
        routeT = at(XL, 3, ND)
        bank = [ctx.enter_context(nc.psum_tensor(f"bank{i}", [P, S], F32)) for i in range(8)]
        t_ps = [bank[4][:, :], bank[5][:, 0:3 * P], bank[6][:, 0:2 * P], bank[5][:, 3 * P:]]
        rel_dram = nc.dram_tensor("rel_ext", [P, HA, EXT], F32)
        table_dram = nc.dram_tensor("tables", [NTB, P, NKEYS * TB], F32).ap()

        slot_in = [sem(f"slot_in{i}") for i in range(SLOTS)]
        tile_done = sem("tile_done")
        mem_in, x_in, vec_in = [sem(f"mem_in{i}") for i in range(4)], [sem(f"x_in{i}") for i in range(4)], sem("vec_in")
        const_made = sem("const_made")
        mem_sq, x_sq = sem("mem_sq"), sem("x_sq")
        norm_ss = sem("norm_ss")
        norm_rt = sem("norm_rt")
        mem_h, h_ready = sem("mem_h"), sem("h_ready")
        h_made, h_high = sem("h_made"), sem("h_high")
        pair_in = [sem(f"pair_in{i}") for i in range(2)]
        quarter_hi, quarter_lo = sem("quarter_hi"), sem("quarter_lo")
        part_used = sem("part_used")
        branch_high, branch_ready = sem("branch_high"), sem("branch_ready")
        x_back, m_hi_ok, m_ready = sem("x_back"), sem("m_hi_ok"), sem("m_ready")
        acc_copied = sem("acc_copied")
        head_sq, head_ss, head_rt, head_ok = sem("head_sq"), sem("head_ss"), sem("head_rt"), sem("head_ok")
        lin_copied, v_copied = sem("lin_copied"), sem("v_copied")
        xl_zero = sem("xl_zero")
        lw_zero, lw_in = sem("lw_zero"), sem("lw_in")
        lam_abs, lam_exp, sp_ok = sem("lam_abs"), sem("lam_exp"), sem("sp_ok")
        conv_ok, lru_mm, lru_sig, lru_tanh, lru_m2, lru_mult, lru_ok = (
            sem("conv_ok"), sem("lru_mm"), sem("lru_sig"), sem("lru_tanh"), sem("lru_m2"), sem("lru_mult"), sem("lru_ok"))
        rel_in, rel_filled, rel_out, bias_in, bias_ok = (
            sem("rel_in"), sem("rel_filled"), sem("rel_out"), sem("bias_in"), sem("bias_ok"))

        class Attention:
            def __init__(self, n):
                self.staged_q = sem(f"{n}_staged_q")
                self.staged_v = sem(f"{n}_staged_v")
                self.scores = sem(f"{n}_scores")
                self.taken = sem(f"{n}_taken")
                self.shifted = sem(f"{n}_shifted")
                self.exped = sem(f"{n}_exped")
                self.probs = sem(f"{n}_probs")
                self.turned = sem(f"{n}_turned")
                self.probsT = sem(f"{n}_probsT")
                self.mixed = sem(f"{n}_mixed")
                self.out = sem(f"{n}_out")

        at_a, at_c = Attention("band"), Attention("cross")
        gate_ok, y_used, merged_ok = sem("gate_ok"), sem("y_used"), sem("merged_ok")
        x2_ok, x2_sq, x2_sum = sem("x2_ok"), sem("x2_sq"), sem("x2_sum")
        h2_ready = sem("h2_ready")
        h2_made, h2_hi = sem("h2_made"), sem("h2_hi")
        raw_in = [sem(f"raw_in{i}") for i in range(2)]
        split_hi, split_lo = sem("split_hi"), sem("split_lo")
        keys_in, pq_copied, pq_scores, sc_copied, sc_free = (
            sem("keys_in"), sem("pq_copied"), sem("pq_scores"), sem("sc_copied"), sem("sc_free"))
        g_shift, g_exp, route_ok, route_tr, route_copied = (
            sem("g_shift"), sem("g_exp"), sem("route_ok"), sem("route_tr"), sem("route_copied"))
        ident_ok, tok_mm, tok_copied = sem("ident_ok"), sem("tok_mm"), sem("tok_copied")
        acc_zero, gath_col, gath_free, gath_gelu, gath_act = (
            sem("acc_zero"), sem("gath_col"), sem("gath_free"), sem("gath_gelu"), sem("gath_act"))
        gath_in = [sem(f"gath_in{i}") for i in range(2)]
        tail_tr, tail_added = sem("tail_tr"), sem("tail_added")
        first_weighed, first_hi = sem("first_weighed"), sem("first_hi")
        oh_a, oh_j, oh_b = sem("oh_a"), sem("oh_j"), sem("oh_b")
        tab_mm, tab_copied = sem("tab_mm"), sem("tab_copied")
        tab_out = [sem(f"tab_out{i}") for i in range(2)]
        wg_in, u_gelu, act_part, act_ok, y_added = (
            sem("wg_in"), sem("u_gelu"), sem("act_part"), sem("act_ok"), sem("y_added"))
        out_done = sem("out_done")
        wait_held, pool_held = sem("wait_held"), sem("pool_held")
        dve_step, pool_step = sem("dve_step"), sem("pool_step")

        def band_s(e, q):
            return s_sb[e][:, s_at[q]:s_at[q + 1]]

        def cross_s(e, q):
            return s_sb[e][:, MEM * q:MEM * (q + 1)]

        def head_place(t, k):
            return arena[:, bass.ds((4 * t + k) * S + (t // 4) * (QC - 2 * HA * S), S)]

        def in_pairs(eng, heads, start, step):
            for e in range(2):
                start(e, e)
            with eng.Fori(0, heads // 2 - 1) as t:
                for e in range(2):
                    step(2 * t + e, e, True)
            for e in range(2):
                step(heads - 2 + e, e, False)

        def landed(eng, tile):
            eng.wait_ge(slot_in[tile % SLOTS], 16 * (tile // SLOTS + 1))

        block = ctx.enter_context(nc.Block())

        @block.sync
        def _(sync):
            def load(tile, src):
                if tile >= SLOTS:
                    sync.wait_ge(tile_done, tile - SLOTS + 1)
                slot = ring[tile % SLOTS][:, :, :].rearrange("p a b -> p (a b)")
                sync.dma_start(slot, src).then_inc(slot_in[tile % SLOTS], 16)

            def row(w, n):
                return w[bass.ds(n, 1)].rearrange("a p n -> p (a n)")

            for q in range(4):
                sync.dma_start(memT[:, 4 * q:4 * q + 4, :], mem_t[:, 4 * q:4 * q + 4, :]).then_inc(mem_in[q], 16)
            load(0, w_memk[0])
            for q in range(4):
                sync.dma_start(xT[:, 4 * q:4 * q + 4, :], x_t[:, 4 * q:4 * q + 4, :]).then_inc(x_in[q], 16)
            for k in range(1, HC):
                load(T_MK + k, w_memk[k])
            for k in range(4):
                load(T_MV + k, w_memv[k])

            def load_half(slot, src):
                sync.dma_start(ring[slot][:, :, :].rearrange("p a b -> p (a b)"), src).then_inc(pair_in[slot], 16)

            for k in range(2):
                sync.wait_ge(tile_done, T_MV + k + 1)
                load_half(k, w_lru_in[k])

            def load_pairs(w, split, first, turns):
                with sync.Fori(0, turns) as t:
                    for k in range(2):
                        sync.wait_ge(quarter_lo, 8 * t + 4 * (split + k + 1))
                        load_half(k, row(w, 2 * t + first + k))

            load_pairs(w_lru_in, 0, 2, LC - 1)
            load_pairs(w_qk, S_QK - 2, 0, N_QK // 2)
            load_pairs(w_v, S_V - 2, 0, 4)
            load_pairs(w_mix, S_MIX - 2, 0, 2 * KC)
            for k in range(2):
                sync.wait_ge(quarter_lo, 4 * (S_WO - 1 + k))
                load_half(k, w_o[k])
            sync.wait_ge(tile_done, T_WO - 1)
            for q in range(4):
                sync.dma_start(xT[:, 4 * q:4 * q + 4, :], x_t[:, 4 * q:4 * q + 4, :]).then_inc(x_back, 16)
            load_pairs(w_o, S_WO, 2, KC // 2 - 1)

            def load_raw(m, src):
                sync.wait_ge(split_lo, m - 1)
                sync.dma_start(ring[m_slot][:, :, :].rearrange("p a b -> p (a b)"), src).then_inc(raw_in[m_slot], 16)

            for m_slot in range(2):
                sync.wait_ge(quarter_lo, 4 * (S_WO + KC - 1 + m_slot))
                sync.dma_start(ring[m_slot][:, :, :].rearrange("p a b -> p (a b)"), w_pq[m_slot]).then_inc(raw_in[m_slot], 16)
            with sync.Fori(1, PH) as t:
                for m_slot in range(2):
                    load_raw(2 * t + m_slot, row(w_pq, 2 * t + m_slot))
            for q in range(JG + 2):
                m_slot = q % 2
                load_raw(2 * PH + q, w_exp[q])
            with sync.Fori(0, NTB // 2) as t:
                for b in range(2):
                    sync.wait_ge(tab_copied, 16 * t + 8 * b + 8)
                    sync.dma_start(table_dram[bass.ds(2 * t + b, 1)].rearrange("a p n -> p (a n)"),
                                   wt[b][:, :, :].rearrange("p a b -> p (a b)")).then_inc(tab_out[b], 16)
            def load_tables(g):
                sync.dma_start(wg[:, :, :, :].rearrange("p a b c -> p a (b c)"),
                               table_dram[:, :, bass.ds(JG * TB * g, JG * TB)].rearrange("t p n -> p t n")
                               ).then_inc(wg_in, 16)

            for q in range(JG + 2, 16):
                m_slot = q % 2
                load_raw(2 * PH + q, w_exp[q])
            for b in range(2):
                sync.wait_ge(tab_out[b], 16 * (NTB // 2))
            with sync.Fori(1, NG) as g:
                sync.wait_ge(act_ok, JG * g)
                load_tables(g)
                for q in range(16):
                    m_slot = q % 2
                    load_raw(16 * g + 2 * PH + q, row(w_exp, 16 * g + q))
            for b in range(4):
                sync.wait_ge(y_added, KC * (NG - 1) + 4 * b + 4)
                sync.dma_start(out_t[:, 4 * b:4 * b + 4, 0:ND], xT[:, 4 * b:4 * b + 4, 0:ND]).then_inc(out_done, 16)
            for b in range(4):
                sync.wait_ge(tail_added, b + 1)
                sync.dma_start(out_t[:, 4 * b:4 * b + 4, ND:], xT[:, 4 * b:4 * b + 4, ND:]).then_inc(out_done, 16)
            sync.wait_ge(out_done, 16 * 8)

        @block.gpsimd
        def _(pool):
            nc.gpsimd.memset(ident[:, :], 0.0).then_inc(pool_step, 1)
            pool.iota(iota[:, :], [[1, P]], base=0, channel_multiplier=0,
                      allow_small_or_imprecise_dtypes=True).then_inc(const_made, 1)
            pool.wait_ge(pool_step, 1)
            pool.affine_select(out=ident[:, :], in_=ident[:, :], compare_op=ALU.not_equal, fill=1.0, base=0,
                               pattern=[[-1, P]], channel_multiplier=1).then_inc(const_made, 1)
            nc.gpsimd.memset(xl[:, :, 0:TAPS - 1], 0.0).then_inc(xl_zero, 1)
            nc.gpsimd.memset(lw, 0.0).then_inc(lw_zero, 1)

            def low_part(slot, number):
                for q in range(4):
                    part = slice(4 * q, 4 * q + 4)
                    pool.wait_ge(quarter_hi, 4 * number + q + 1)
                    nc.gpsimd.tensor_tensor(p_lo[:, part, :], ring[slot][:, part, :], p_hi[:, part, :].bitcast(F32),
                                            ALU.subtract).then_inc(quarter_lo, 1)

            with pool.Fori(0, S_MIX // 2) as t:
                for k in range(2):
                    low_part(k, 2 * t + k)
            low_part(0, S_MIX)

            pool.wait_ge(lru_ok, LC)
            pool.wait_ge(head_ok, HC + N_QK)
            pool.wait_ge(v_copied, MT + 2 * TT)

            def stage(a, heads, q_of, v_of, v_tiles):
                def q_stage(h, e):
                    nc.gpsimd.tensor_copy(qs[e], q_of[:, bass.ds(h, 1), :].rearrange("p a s -> p (a s)")).then_inc(a.staged_q, 1)

                def v_stage(h, e):
                    nc.gpsimd.tensor_copy(vs[e][:, 0:v_tiles, :], v_of[:, :, bass.ds(h * DH, DH)]).then_inc(a.staged_v, 1)

                for e in range(2):
                    q_stage(e, e)
                    v_stage(e, e)
                with pool.Fori(0, heads // 2 - 1) as t:
                    for e in range(2):
                        pool.wait_ge(a.scores, TT * (2 * t + e + 1))
                        q_stage(2 * t + e + 2, e)
                        pool.wait_ge(a.mixed, 2 * t + e + 1)
                        v_stage(2 * t + e + 2, e)

            stage(at_a, HA, qT, vA, TT)
            pool.wait_ge(at_a.mixed, HA)
            stage(at_c, HC, qkc, mv, MT)

            with pool.Fori(0, 2 * KC) as t:
                for k in range(2):
                    low_part(1 - k, 2 * t + S_MIX + 1 + k)

            pool.wait_ge(merged_ok, KC)
            nc.gpsimd.memset(sumsq, 0.0).then_inc(x2_sum, 1)

            def add_square(c):
                pool.wait_ge(x2_ok, c + 1)
                pool.wait_ge(x2_sum, c + 1)
                xk = xT[:, bass.ds(c, 1), :].rearrange("p a s -> p (a s)")
                nc.gpsimd.tensor_tensor(sqx, xk, xk, ALU.mult).then_inc(x2_sq, 1)
                pool.wait_ge(x2_sq, c + 1)
                nc.gpsimd.tensor_tensor(sumsq, sumsq, sqx, ALU.add).then_inc(x2_sum, 1)

            with pool.Fori(0, KC // 2 - 1) as t:
                for k in range(2):
                    low_part(1 - k, 2 * t + S_WO + 1 + k)
                    add_square(2 * t + k)
            low_part(1, S_WO + KC - 1)
            for c in (KC - 2, KC - 1):
                add_square(c)

            with pool.Fori(0, PH + JG // 2) as t:
                for b in range(2):
                    pool.wait_ge(split_hi, 2 * t + b + 1)
                    nc.gpsimd.tensor_tensor(w_lo[b][:, :, :], ring[b][:, :, :], w_hi[b][:, :, :].bitcast(F32),
                                            ALU.subtract).then_inc(split_lo, 1)

            def gather(number, rows, t):
                for b in range(2):
                    pool.wait_ge(gath_free, 2 * t + b + 1 + number * PAIRS)
                    nc.gpsimd.tensor_copy(g_col[b][:, :], g_idx[:, bass.ds(2 * t + b, 1)]).then_inc(gath_col, 1)
                    pool.wait_ge(gath_col, 2 * t + b + 1 + number * PAIRS)
                    pool.sem_inc(pool_held, 1)
                    pool.indirect_dma_start(grow[b][:, :], None, rows, bass.IndirectOffsetOnAxis(g_col[b][:, :], 0)
                                            ).then_inc(gath_in[b], 16)

            gather(0, u_rows, 0)
            def weigh_first(t, b):
                pool.wait_ge(tab_copied, 8 * t + 8)
                part = gel_first[:, :, bass.ds(TB * t, TB)]
                nc.gpsimd.tensor_tensor(part, part, wt[b][:, 0:JG, :], ALU.mult).then_inc(first_weighed, 1)

            pool.wait_ge(route_copied, 3)
            pool.wait_ge(u_gelu, JG)
            with pool.Fori(0, NTB // 6) as u:
                for i in range(6):
                    for q in range(4):
                        rows = ohB[(4 * i + q) % 3][:, :, :]
                        pool.wait_ge(oh_j, 24 * u + 4 * i + q + 1)
                        weights = routeT[:, 2, bass.ds(6 * TB * u + TB * i + HT * q, HT)]
                        nc.gpsimd.tensor_tensor(rows, rows, weights.unsqueeze(2).to_broadcast([P, HT, P]), ALU.mult
                                                ).then_inc(oh_b, 1)
                        if i and q == 1:
                            weigh_first(6 * u + i - 1, (i - 1) % 2)
                weigh_first(6 * u + 5, 1)
            with pool.Fori(1, PAIRS // 2) as t:
                gather(0, u_rows, t)
            with pool.Fori(0, PAIRS // 2) as t:
                gather(1, v_rows, t)

        @block.scalar
        def _(act_e):
            def f(out, in_, func=ACT.Copy, **kw):
                return nc.scalar.activation(out, in_, func, **kw)

            for dst, src in ((vecs[:, 0:KC], g1), (vecs[:, KC:2 * KC], g2), (vecs[:, 2 * KC:], gmem),
                             (hgain[:, :], head_g), (bgate[:, :], b_gate), (lvec[:, :, :], lru_vec)):
                act_e.dma_start(dst, src).then_inc(vec_in, 16)
            act_e.dma_start(rext[:, P - 1:], rel_rev).then_inc(rel_in, 16)
            act_e.wait_ge(lw_zero, 1)
            for side in range(2):
                for half in range(2):
                    sl = slice(64 * half, 64 * half + 64)
                    act_e.dma_start(lw[sl, side, :, sl], lru_w[side, half]).then_inc(lw_in, 16)

            for q in range(4):
                act_e.wait_ge(mem_in[q], 16)
                f(msq[:, 4 * q:4 * q + 4, :], memT[:, 4 * q:4 * q + 4, :], ACT.Square).then_inc(mem_sq, 1)
            act_e.wait_ge(const_made, 4)
            act_e.wait_ge(norm_ss, 1)
            f(rt[0][:, 0:MEM], bank[6][:, 0:MEM], ACT.Sqrt, scale=1.0 / D, bias=eps[:, 0:1]).then_inc(norm_rt, 1)
            for q in range(4):
                act_e.wait_ge(x_in[q], 16)
                f(xsq[:, 4 * q:4 * q + 4, :], xT[:, 4 * q:4 * q + 4, :], ACT.Square).then_inc(x_sq, 1)

            def head_root(n, width, number):
                act_e.wait_ge(head_ss, number)
                f(rt[n % 2][:, 0:width], bank[4 + n % 2][:, 0:width], ACT.Sqrt, scale=1.0 / DH,
                  bias=eps[:, 0:1]).then_inc(head_rt, 1)

            for k in range(HC):
                act_e.wait_ge(tile_done, T_MK + k + 1)
                f(mk[:, k, :], bank[k][:, 0:MEM]).then_inc(acc_copied, 1)
                if k >= 2:
                    act_e.wait_ge(head_ss, k - 1)
                f(sq[k % 2][:, 0:MEM], bank[k][:, 0:MEM], ACT.Square).then_inc(head_sq, 1)
                if k >= 2:
                    act_e.wait_ge(head_ok, k - 1)
                if k == 0:
                    act_e.wait_ge(mem_h, KC)
                head_root(k, MEM, k + 1)
            act_e.wait_ge(norm_ss, 2)
            act_e.wait_ge(head_ok, HC)
            f(rt[0], bank[6][:, :], ACT.Sqrt, scale=1.0 / D, bias=eps[:, 0:1]).then_inc(norm_rt, 1)
            for c in range(KC):
                act_e.wait_ge(h_made, c + 1)
                f(norm_hi[:, c, :], hT[:, c, :]).then_inc(h_high, 1)
            act_e.wait_ge(tile_done, T_MV + 4)
            for m in range(MT):
                f(mv[:, m, :], bank[2 + m][:, :]).then_inc(v_copied, 1)

            def high_part(slot, number, tiles, used, quarters=range(4)):
                act_e.wait_ge(pair_in[slot], 16 * tiles)
                for q in quarters:
                    if q < 3:
                        act_e.wait_ge(part_used, 3 * number + q - 2)
                    else:
                        act_e.wait_ge(tile_done, used)
                    part = slice(4 * q, 4 * q + 4)
                    f(p_hi[:, part, :], ring[slot][:, part, :]).then_inc(quarter_hi, 1)

            act_e.wait_ge(tile_done, T_LRU)
            act_e.wait_ge(pair_in[0], 16)
            for q in range(4):
                f(p_hi[:, 4 * q:4 * q + 4, :], ring[0][:, 4 * q:4 * q + 4, :]).then_inc(quarter_hi, 1)
            high_part(1, 1, 1, T_LRU + 1)

            act_e.wait_ge(vec_in, 16 * 6)
            act_e.wait_ge(lam_abs, 1)
            f(sp[:, 1, :], sp[:, 0, :], ACT.Exp, scale=-1.0).then_inc(lam_exp, 1)
            act_e.wait_ge(rel_filled, 1)
            act_e.dma_start(rel_dram.ap().rearrange("p h n -> h p n"),
                            rext[:, :].unsqueeze(1).to_broadcast([HA, P, EXT])).then_inc(rel_out, 16)

            def two_ahead(n, quarters=range(4)):
                high_part(n % 2, n + 2 - T_LRU, (n - T_LRU) // 2 + 2, n + 2, quarters)

            def gates(side, dst):
                for k in range(LC):
                    act_e.wait_ge(lru_mm, LC * side + k + 1)
                    f(dst[:, k, :], bank[4 + k][:, :], ACT.Sigmoid, bias=lvec[:, 5 + side, k:k + 1]).then_inc(lru_sig, 1)

            act_e.wait_ge(xl_zero, 1)
            for k in range(LC):
                act_e.wait_ge(tile_done, T_LRU + k + 1)
                f(xl[:, k, TAPS - 1:], bank[k][:, :]).then_inc(lin_copied, 1)
                two_ahead(T_LRU + k)
            for k in range(LC):
                act_e.wait_ge(tile_done, T_LRU + LC + k + 1)
                f(gl[:, k, :], bank[k][:, :], ACT.Gelu_apprx_tanh).then_inc(lin_copied, 1)
                if k < LC - 1:
                    two_ahead(T_LRU + LC + k)
            gates(0, rg)
            two_ahead(T_QK - 1, (0,))
            act_e.wait_ge(conv_ok, LC)
            gates(1, ig)
            act_e.wait_ge(sp_ok, 1)
            act_e.wait_ge(lru_sig, LC)
            for k in range(LC):
                f(rg[:, k, :], rg[:, k, :], ACT.Tanh, scale=sp[:, 5, k:k + 1]).then_inc(lru_tanh, 1)
            two_ahead(T_QK - 1, (1, 2, 3))

            act_e.wait_ge(h_ready, KC)

            def heads(t, first):
                for k in range(4):
                    act_e.wait_ge(tile_done, 4 * t + T_QK + k + 1)
                    f(head_place(t, k), bank[k][:, :]).then_inc(acc_copied, 1)
                    act_e.wait_ge(head_ss, 4 * t + k + HC - 1)
                    f(sq[k % 2], bank[k][:, :], ACT.Square).then_inc(head_sq, 1)
                    ahead = (k % 2, 4 * t + S_QK + k + 2, 2 * t + S_QK // 2 + k // 2 + 2, 4 * t + T_QK + k + 2)
                    high_part(*ahead, quarters=(0,))
                    act_e.wait_ge(head_ok, 4 * t + k + HC - 1)
                    head_root(k, S, 4 * t + k + HC + 1)
                    high_part(*ahead, quarters=(1, 2, 3))
                    if first:
                        act_e.wait_ge(lru_m2, k + 1)
                        f(rg[:, k, :], rg[:, k, :], ACT.Sqrt).then_inc(lru_mult, 1)

            heads(0, True)
            with act_e.Fori(1, N_QK // 4) as t:
                heads(t, False)
            act_e.wait_ge(lru_ok, LC)
            act_e.wait_ge(rel_out, 16)
            act_e.dma_start(tb, bass.AP(rel_dram, P - 1, [[HA * EXT - 1, P], [EXT, HA], [1, 2 * P]])).then_inc(bias_in, 16)
            for half in range(2):
                for n in range(3):
                    two_ahead(T_V + 4 * half + n)
                act_e.wait_ge(tile_done, T_V + 4 * half + 4)
                for m in range(TT):
                    f(vA[:, m, 512 * half:512 * half + 512], bank[4 * half + m][:, :]).then_inc(v_copied, 1)
                if half == 0:
                    two_ahead(T_V + 3)

            def attention(a, heads, tiles, s_of, exp_in, turned_ps, dst, scale):
                def exps(h, e):
                    for q in range(TT):
                        act_e.wait_ge(a.shifted, TT * h + q + 1)
                        f(s_of(e, q), exp_in(e, q), ACT.Exp, bias=nmax[:, e, q:q + 1], scale=scale,
                          accum_out=ssum[:, e, q:q + 1]).then_inc(a.exped, 1)

                def copies(h, e, more):
                    act_e.wait_ge(a.mixed, h)
                    for kt in range(tiles):
                        act_e.wait_ge(a.turned, tiles * h + (tiles if kt else 1))
                        f(dst[kt], turned_ps[kt]).then_inc(a.probsT, 1)
                    if more:
                        exps(h + 2, e)

                in_pairs(act_e, heads, exps, copies)

            attention(at_a, HA, TT, band_s, band_s, t_ps, pT, 1.0)
            attention(at_c, HC, MT, cross_s, lambda e, q: bank[q][:, 0:MEM], [bank[4][:, :], bank[5][:, :]], pTc, SCALE)

            def next_tile(c, b, quarters=range(4)):
                high_part((b + 1) % 2, 4 * c + S_MIX + b + 1, 2 * c + (S_MIX + b + 1) // 2 + 1, 4 * c + T_MIX + b + 1,
                          quarters)

            def chunk_gates(c):
                for b in range(3):
                    next_tile(c, b)
                    act_e.wait_ge(tile_done, 4 * c + T_MIX + b + 1)
                    if b == 0:
                        act_e.wait_ge(merged_ok, c)
                    f(sig[:, b, :], bank[b][:, :], ACT.Sigmoid, bias=bgate[:, bass.ds(KC * b + c, 1)]
                      ).then_inc(gate_ok, 1)

            def merged_high(c):
                act_e.wait_ge(merged_ok, c + 1)
                f(h_hi[:, c, :], merged[:, c, :]).then_inc(m_hi_ok, 1)

            with act_e.Fori(0, KC - 1) as c:
                chunk_gates(c)
                next_tile(c, 3)
            chunk_gates(KC - 1)
            for q in range(3):
                for c in range(5 * q, 5 * q + 5):
                    merged_high(c)
                next_tile(KC - 1, 3, (q,))
            next_tile(KC - 1, 3, (3,))
            merged_high(KC - 1)

            with act_e.Fori(0, KC // 2 - 1) as t:
                for k in range(2):
                    high_part(1 - k, 2 * t + S_WO + 1 + k, t + (S_WO + 1 + k) // 2 + 1, 2 * t + T_WO + k + 1)
            high_part(1, S_WO + KC - 1, (S_WO + KC) // 2, T_WO + KC - 1)

            act_e.wait_ge(tile_done, T_WO)
            act_e.dma_start(kys, keys).then_inc(keys_in, 16)
            def high(n, b, free):
                act_e.wait_ge(raw_in[b], 16 * (n // 2) + 16)
                if free:
                    act_e.wait_ge(tile_done, n + T_PQ - 1)
                f(w_hi[b][:, :, :], ring[b][:, :, :]).then_inc(split_hi, 1)

            act_e.wait_ge(tile_done, T_PQ)
            high(0, 0, False)
            act_e.wait_ge(norm_ss, 3)
            f(rt2, bank[6][:, :], ACT.Sqrt, scale=1.0 / D, bias=eps[:, 0:1]).then_inc(norm_rt, 1)
            for c in range(KC):
                act_e.wait_ge(h2_made, c + 1)
                f(h_hi[:, c, :], h2[c % 2]).then_inc(h2_hi, 1)
                if c == 3 * KC // 4 - 1:
                    high(1, 1, False)
            act_e.wait_ge(keys_in, 16)

            def queries(t):
                for k in range(4):
                    act_e.wait_ge(tile_done, 4 * t + T_PQ + k + 1)
                    act_e.wait_ge(pq_scores, 4 * t)
                    f(qp[:, k, :], bank[k][:, :]).then_inc(pq_copied, 1)
                    high_in_turn(t, k)
                    act_e.wait_ge(pq_scores, 4 * t + k + 1)
                    act_e.wait_ge(sc_free, 4 * t + k + 1)
                    f(sc[:, k, :, :], bank[4 + k][:, :].rearrange("p (a b) -> p a b", a=TT)).then_inc(sc_copied, 1)

            def high_in_turn(t, k):
                b = k % 2
                act_e.wait_ge(raw_in[b], 32 * t + 16 * (k // 2 + 1) + 16)
                act_e.wait_ge(tile_done, 4 * t + T_PQ + k + 1)
                f(w_hi[b][:, :, :], ring[b][:, :, :]).then_inc(split_hi, 1)

            with act_e.Fori(0, PH // 2) as t:
                queries(t)

            act_e.wait_ge(tok_mm, 1)
            for b in range(4):
                f(h_tok[:, 4 * b:4 * b + 4, :], bank[b][:, :].rearrange("p (a n) -> p a n", a=4)).then_inc(tok_copied, 1)
            for q in range(JG):
                act_e.wait_ge(tile_done, T_EXP + q + 1)
                f(gel_first[:, q, :], bank[q % 4][:, 0:ND], ACT.Gelu_apprx_tanh).then_inc(u_gelu, 1)
                if q < JG - 2:
                    high(2 * PH + q + 2, q % 2, True)
            act_e.wait_ge(g_shift, 1)
            gv = route[:, 2, :, :, :].rearrange("p m h k -> p (m h k)")
            f(gv, gv, ACT.Exp).then_inc(g_exp, 1)
            for k in range(3):
                act_e.wait_ge(route_tr, k + 1)
                f(routeT[:, k, :], bank[4 + k][:, 0:ND]).then_inc(route_copied, 1)

            with act_e.Fori(0, NTB // 2) as t:
                for b in range(2):
                    act_e.wait_ge(tab_out[b], 16 * t)
                    if b:
                        act_e.wait_ge(first_weighed, 2 * t)
                    for q in range(8):
                        act_e.wait_ge(tab_mm, 16 * t + 8 * b + q + 1)
                        f(wt[b][:, :, 4 * q:4 * q + 4].rearrange("p j t -> p t j"),
                          bank[q][:, :].rearrange("p (t j) -> p t j", t=4)).then_inc(tab_copied, 1)
                act_e.wait_ge(first_weighed, 2 * t + 1)
            act_e.wait_ge(tab_out[0], 16 * (NTB // 2))
            act_e.wait_ge(first_weighed, NTB - 1)
            high(2 * PH + JG, 0, True)
            act_e.wait_ge(first_weighed, NTB)
            for j in range(JG):
                f(act_lo[:, j, :], gel_first[:, j, :]).then_inc(first_hi, 1)
            act_e.wait_ge(tab_out[1], 16 * (NTB // 2))
            high(2 * PH + JG + 1, 1, True)

            def experts(g, last, steps=range(16)):
                for q in steps:
                    act_e.wait_ge(tile_done, 16 * g + T_EXP + q + 1)
                    if q < JG:
                        act_e.wait_ge(act_ok, JG * g + max(q - 1, 0))
                        f(gel[q % 2][:, :], bank[q % 4][:, 0:ND], ACT.Gelu_apprx_tanh).then_inc(u_gelu, 1)
                    if not (last and q >= 14):
                        act_e.wait_ge(raw_in[q % 2], 128 * g + 16 * (PH + q // 2 + 1) + 16)
                        f(w_hi[q % 2][:, :, :], ring[q % 2][:, :, :]).then_inc(split_hi, 1)

            experts(0, False, range(JG, 16))
            with act_e.Fori(1, NG // 2) as g:
                experts(g, False)
            act_e.wait_ge(gath_free, 2 + PAIRS)
            f(g_act[:, :], g_dot[:, :], ACT.Gelu_apprx_tanh).then_inc(gath_gelu, 1)
            with act_e.Fori(NG // 2, NG - 1) as g:
                experts(g, False)
            experts(NG - 1, True)

        @block.vector
        def _(dve):
            v = nc.vector
            st = Steps(dve, dve_step)

            v.memset(ones[:, :], 1.0).then_inc(const_made, 1)
            v.memset(eps[:, :], EPS).then_inc(const_made, 1)

            dve.wait_ge(vec_in, 16 * 6)
            dve.wait_ge(norm_rt, 1)
            st.did(v.reciprocal(rt[0][:, 0:MEM], rt[0][:, 0:MEM]))
            st.wait()
            for c in range(KC):
                v.scalar_tensor_tensor(out=memT[:, c, :], in0=memT[:, c, :], scalar=vecs[:, 2 * KC + c:2 * KC + c + 1],
                                       in1=rt[0][:, 0:MEM], op0=ALU.mult, op1=ALU.mult).then_inc(mem_h, 1)

            dve.wait_ge(rel_in, 16)
            v.tensor_copy(rext[:, 0:P - 1], rext[:, P - 1:P].to_broadcast([HA, P - 1])).then_inc(rel_filled, 1)

            lam = lvec[:, 7, :]
            v.scalar_tensor_tensor(out=sp[:, 0, :], in0=lam, scalar=-1.0, in1=lam, op0=ALU.mult, op1=ALU.max).then_inc(lam_abs, 1)

            def head_norm(n, dst, width, gain, number):
                dve.wait_ge(head_rt, number)
                r = rt[n % 2][:, 0:width]
                st.did(v.reciprocal(r, r))
                st.wait()
                v.scalar_tensor_tensor(out=dst, in0=dst, scalar=gain, in1=r, op0=ALU.mult, op1=ALU.mult
                                       ).then_inc(head_ok, 1)

            for k in range(HC):
                head_norm(k, mk[:, k, :], MEM, hgain[:, 3:4], k + 1)

            dve.wait_ge(norm_rt, 2)
            st.did(v.reciprocal(rt[0], rt[0]))
            st.wait()
            for c in range(KC + 1):
                if c < KC:
                    v.scalar_tensor_tensor(out=hT[:, c, :], in0=xT[:, c, :], scalar=vecs[:, c:c + 1],
                                           in1=rt[0], op0=ALU.mult, op1=ALU.mult).then_inc(h_made, 1)
                if c:
                    dve.wait_ge(h_high, c)
                    v.tensor_tensor(norm_lo[:, c - 1, :], hT[:, c - 1, :], norm_hi[:, c - 1, :].bitcast(F32),
                                    ALU.subtract).then_inc(h_ready, 1)

            dve.wait_ge(lam_exp, 1)
            y, z, z2, s4 = sp[:, 1, :], sp[:, 2, :], sp[:, 3, :], sp[:, 4, :]

            def step(ins):
                st.did(ins)
                st.wait()

            step(v.tensor_scalar(z, y, 2.0, None, ALU.add))
            step(v.reciprocal(z, z))
            step(v.tensor_tensor(z, z, y, ALU.mult))
            step(v.tensor_tensor(z2, z, z, ALU.mult))
            step(v.memset(s4, 1.0 / 17))
            for odd in (15, 13, 11, 9, 7, 5, 3, 1):
                step(v.tensor_tensor(s4, s4, z2, ALU.mult))
                step(v.tensor_scalar(s4, s4, 1.0 / odd, None, ALU.add))
            step(v.tensor_tensor(s4, s4, z, ALU.mult))
            step(v.tensor_scalar(s4, s4, 8.0, None, ALU.mult))
            step(v.tensor_scalar(z, lam, -4.0, 0.0, ALU.mult, ALU.max))
            v.tensor_tensor(sp[:, 5, :], s4, z, ALU.add).then_inc(sp_ok, 1)

            for k in range(LC):
                dve.wait_ge(lin_copied, k + 1)
                step(v.tensor_scalar(xc[:, k, :], xl[:, k, 0:S], lvec[:, 0, k:k + 1], lvec[:, 4, k:k + 1],
                                     ALU.mult, ALU.add))
                for tap in range(1, TAPS):
                    ins = v.scalar_tensor_tensor(out=xc[:, k, :], in0=xl[:, k, tap:tap + S], scalar=lvec[:, tap, k:k + 1],
                                                 in1=xc[:, k, :], op0=ALU.mult, op1=ALU.add)
                    if tap < TAPS - 1:
                        step(ins)
                    else:
                        ins.then_inc(conv_ok, 1)

            def lru_factors(k):
                t = rg[:, k, :]
                dve.wait_ge(lru_tanh, k + 1)
                dve.wait_ge(lru_ok, k)
                step(v.tensor_scalar(lr, t, 1.0, None, ALU.add))
                step(v.reciprocal(lr, lr))
                step(v.tensor_scalar(la, t, -1.0, 1.0, ALU.mult, ALU.add))
                step(v.tensor_tensor(la, la, lr, ALU.mult))
                step(v.scalar_tensor_tensor(out=t, in0=t, scalar=4.0, in1=lr, op0=ALU.mult, op1=ALU.mult))
                step(v.tensor_tensor(t, t, lr, ALU.mult))
                v.tensor_scalar(t, t, 1e-12, 1.0, ALU.max, ALU.min).then_inc(lru_m2, 1)

            def lru_scan(k):
                u = ig[:, k, :]
                dve.wait_ge(lru_sig, LC + k + 1)
                step(v.tensor_tensor(u, u, xc[:, k, :], ALU.mult))
                dve.wait_ge(lru_mult, k + 1)
                step(v.tensor_tensor(u, u, rg[:, k, :], ALU.mult))
                step(v.tensor_tensor_scan(out=xc[:, k, :], data0=la, data1=u, initial=0.0, op0=ALU.mult, op1=ALU.add))
                dve.wait_ge(lin_copied, 2 * LC)
                v.tensor_tensor(gl[:, k, :], gl[:, k, :], xc[:, k, :], ALU.mult).then_inc(lru_ok, 1)

            dve.wait_ge(conv_ok, LC)
            for k in range(LC):
                lru_factors(k)
                head_norm(k, head_place(0, k), S, hgain[:, 0:1], k + HC + 1)
                lru_scan(k)
            with dve.Fori(1, N_QK // 4) as t:
                st.loop(t, 4, 1)
                for k in range(4):
                    head_norm(k, head_place(t, k), S, hgain[:, bass.ds(t // 2, 1)], 4 * t + k + HC + 1)
                st.end(N_QK // 4)

            dve.wait_ge(bias_in, 16)
            v.memset(tb[0:CHUNK, :, 2 * P - CHUNK:], NEG).then_inc(bias_ok, 1)
            dve.wait_ge(bias_ok, 1)

            def attention(a, heads, scores, s_of, dst, steps):
                def step(h, e, more):
                    for q in range(TT):
                        dve.wait_ge(a.exped, TT * h + q + 1)
                        st.did(v.reciprocal(rinv[:, e, q:q + 1], ssum[:, e, q:q + 1]))
                        st.wait()
                        v.tensor_scalar(s_of(e, q), s_of(e, q), rinv[:, e, q:q + 1], None, ALU.mult).then_inc(a.probs, 1)
                    if more:
                        scores(h + 2, e)
                    dve.wait_ge(a.mixed, h + 1)
                    v.tensor_scalar(dst[:, bass.ds(h, 1), :].rearrange("p a s -> p (a s)"), bank[7][:, :], 1.0, None,
                                    ALU.mult).then_inc(a.out, 1)

                for e in range(2):
                    scores(e, e)
                with dve.Fori(0, heads // 2 - 1) as t:
                    st.loop(t, 2 * (steps + TT))
                    for e in range(2):
                        step(2 * t + e, e, True)
                    st.end(heads // 2 - 1)
                for e in range(2):
                    step(heads - 2 + e, e, False)

            def band_scores(h, e):
                if not isinstance(h, int):
                    dve.wait_ge(at_a.turned, TT * (h - 1))
                for q in range(TT):
                    dve.wait_ge(at_a.scores, TT * h + q + 1)
                    near = max(q - 1, 0) * P
                    w = (q + 1) * P
                    row = band_s(e, q)
                    if near:
                        st.did(v.tensor_scalar(row[:, 0:near], bank[q][:, 0:near], SCALE,
                                               tb[:, bass.ds(h, 1), 0:1].rearrange("p a b -> p (a b)"), ALU.mult, ALU.add))
                    v.scalar_tensor_tensor(
                        out=row[:, near:w], in0=bank[q][:, near:w], scalar=SCALE,
                        in1=tb[:, bass.ds(h, 1), 2 * P - (w - near):].rearrange("p a b -> p (a b)"),
                        op0=ALU.mult, op1=ALU.add).then_inc(at_a.taken, 1)
                    if near:
                        st.wait()
                    dve.wait_ge(at_a.taken, TT * h + q + 1)
                    st.did(v.reduce_max(smax[:, e, q:q + 1], row, AX_X))
                    st.wait()
                    v.tensor_scalar(nmax[:, e, q:q + 1], smax[:, e, q:q + 1], -1.0, None, ALU.mult).then_inc(at_a.shifted, 1)

            def cross_scores(h, e):
                for q in range(TT):
                    dve.wait_ge(at_c.scores, TT * h + q + 1)
                    st.did(v.reduce_max(smax[:, e, q:q + 1], bank[q][:, 0:MEM], AX_X))
                    st.wait()
                    v.tensor_scalar(nmax[:, e, q:q + 1], smax[:, e, q:q + 1], -SCALE, None, ALU.mult).then_inc(at_c.shifted, 1)

            attention(at_a, HA, band_scores, band_s, qT, TT + 2)
            attention(at_c, HC, cross_scores, cross_s, qkc, TT)

            dve.wait_ge(at_c.out, HC)
            for k in range(KC):
                v.tensor_copy(branch_hi[k], branches[k]).then_inc(branch_high, 1)
            for k in range(KC):
                dve.wait_ge(branch_high, k + 1)
                v.tensor_tensor(branch_lo[k], branches[k], branch_hi[k].bitcast(F32), ALU.subtract).then_inc(branch_ready, 1)

            def merge(c):
                dve.wait_ge(tile_done, 4 * c + T_MIX + 4)
                for b in range(3):
                    dve.wait_ge(gate_ok, 3 * c + b + 1)
                    v.tensor_tensor(sig[:, b, :], sig[:, b, :], bank[3 + b][:, :], ALU.mult).then_inc(y_used, 1)
                dve.wait_ge(y_used, 3 * c + 3)
                st.did(v.tensor_tensor(sig[:, 0, :], sig[:, 0, :], sig[:, 1, :], ALU.add))
                st.wait()
                v.tensor_tensor(merged[:, bass.ds(c, 1), :].rearrange("p a s -> p (a s)"), sig[:, 0, :], sig[:, 2, :],
                                ALU.add).then_inc(merged_ok, 1)

            def merged_low(c):
                dve.wait_ge(m_hi_ok, c + 1)
                v.tensor_tensor(h_lo[:, c, :], merged[:, c, :], h_hi[:, c, :].bitcast(F32), ALU.subtract
                                ).then_inc(m_ready, 1)

            with dve.Fori(0, KC - 1) as c:
                st.loop(c, 1)
                merge(c)
                st.end(KC - 1)
            for c in range(KC - 1):
                merged_low(c)
            merge(KC - 1)
            merged_low(KC - 1)

            dve.wait_ge(x_back, 64)
            with dve.Fori(0, KC // 4) as t:
                for k in range(4):
                    dve.wait_ge(tile_done, 4 * t + T_WO + k + 1)
                    xk = xT[:, bass.ds(4 * t + k, 1), :].rearrange("p a s -> p (a s)")
                    v.tensor_tensor(xk, xk, bank[k][:, :], ALU.add).then_inc(x2_ok, 1)
            dve.wait_ge(norm_rt, 3)
            step(v.reciprocal(rt2, rt2))
            for c in range(KC + 1):
                if c < KC:
                    if c >= 2:
                        dve.wait_ge(h2_ready, c - 1)
                    v.scalar_tensor_tensor(out=h2[c % 2], in0=xT[:, c, :], scalar=vecs[:, KC + c:KC + c + 1],
                                           in1=rt2, op0=ALU.mult, op1=ALU.mult).then_inc(h2_made, 1)
                if c:
                    dve.wait_ge(h2_hi, c)
                    v.tensor_tensor(h_lo[:, c - 1, :], h2[(c - 1) % 2], h_hi[:, c - 1, :].bitcast(F32), ALU.subtract
                                    ).then_inc(h2_ready, 1)
            dve.wait_ge(const_made, 4)
            v.tensor_copy(ident_r[:, :], ident[:, :]).then_inc(ident_ok, 1)
            dve.sem_inc(sc_free, 4)

            def best16(groups):
                def pause():
                    st.wait()
                    dve.sem_inc(wait_held, 1)

                dve.sem_inc(wait_held, 1)
                for half in (slice(0, 8), slice(8, 16)):
                    for s, val, idx in groups:
                        st.did(v.max(val[:, half], s))
                    pause()
                    for s, val, idx in groups:
                        st.did(v.max_index(idx[:, half], val[:, half], s))
                    pause()
                    if half.start == 0:
                        for s, val, idx in groups:
                            st.did(v.match_replace(s, val[:, half], s, LOWEST))
                        pause()

            with dve.Fori(0, PH // 2) as t:
                st.loop(t, 2 * (15 * TT + 12))
                for e in range(2):
                    for side in range(2):
                        k = 2 * e + side
                        dve.wait_ge(sc_copied, 4 * t + k + 1)
                        best16([(sc[:, k, m, :], sv[:, e, side, m, :], si[:, e, side, m, :]) for m in range(TT)])
                        dve.sem_inc(sc_free, 1)
                    step(v.tensor_tensor(cand, sv[:, e, 0, :, :].unsqueeze(3).to_broadcast([P, TT, TOPK, TOPK]),
                                         sv[:, e, 1, :, :].unsqueeze(2).to_broadcast([P, TT, TOPK, TOPK]), ALU.add))
                    best16([(cand[:, m, :, :].rearrange("p a b -> p (a b)"), fv[:, m, :], fpos[:, m, :]) for m in range(TT)])
                    pos = fpos.rearrange("p a b -> p (a b)")
                    st.did(v.tensor_scalar(fa, pos, 4, None, ALU.logical_shift_right))
                    step(v.tensor_scalar(fb, pos, TOPK - 1, None, ALU.bitwise_and))
                    for side, which in ((0, fa), (1, fb)):
                        st.did(v.tensor_tensor(pick[:, side, :, :], which.unsqueeze(2).to_broadcast([P, TT * TOPK, TOPK]),
                                               iota[:, 0:TOPK].unsqueeze(1).to_broadcast([P, TT * TOPK, TOPK]), ALU.is_equal))
                    st.wait()
                    for side in range(2):
                        pk = pick[:, side, :, :].rearrange("p (m k) n -> p m k n", m=TT)
                        st.did(v.tensor_tensor(pk, pk, si[:, e, side, :, :].unsqueeze(2).to_broadcast([P, TT, TOPK, TOPK]), ALU.mult))
                    st.wait()
                    for side, dst in ((0, ires), (1, jres)):
                        st.did(v.reduce_sum(dst.rearrange("p m k -> p (m k)"), pick[:, side, :, :], AX_X))
                    st.wait()
                    for which, src in ((0, ires), (1, jres), (2, fv)):
                        dst = route[:, which, :, bass.ds(2 * t + e, 1), :].rearrange("p m a k -> p m (a k)")
                        st.did(v.tensor_scalar(dst, src, 0.0, None, ALU.add))
                    st.wait()
                st.end(PH // 2)

            gv = route[:, 2, :, :, :].rearrange("p m h k -> p (m h) k")
            step(v.reduce_max(gmx, gv, AX_X))
            v.tensor_tensor(gv, gv, gmx.unsqueeze(2).to_broadcast([P, TT * PH, TOPK]), ALU.subtract).then_inc(g_shift, 1)
            dve.wait_ge(g_exp, 1)
            step(v.reduce_sum(gsum, gv, AX_X))
            step(v.reciprocal(grec, gsum))
            v.tensor_tensor(gv, gv, grec.unsqueeze(2).to_broadcast([P, TT * PH, TOPK]), ALU.mult).then_inc(route_ok, 1)

            gi, gj, gw = (route[:, w, TG, :, :].rearrange("p h k -> p (h k)") for w in range(3))
            step(v.scalar_tensor_tensor(out=g_idx[:, :], in0=gi, scalar=float(NKEYS), in1=gj, op0=ALU.mult, op1=ALU.add))
            step(v.tensor_copy(g_w[:, :], gw))
            dve.wait_ge(route_tr, 3)
            dve.sem_inc(gath_free, 2)
            dve.wait_ge(tok_mm, 1)
            v.memset(g_acc, 0.0).then_inc(acc_zero, 1)

            dve.wait_ge(route_copied, 3)

            def one_hots(t, first):
                for k in range(12):
                    token = 3 * TB * t + HT * k
                    for which, made, rows, free in ((1, oh_j, ohB[k % 3], 3), (0, oh_a, ohA[k % 2], 2)):
                        if not first or k >= free:
                            dve.wait_ge(tab_mm, 24 * t + 2 * (k - free) + 2)
                        v.tensor_tensor(rows[:, :, :], iota[:, :].unsqueeze(1).to_broadcast([P, HT, P]),
                                        routeT[:, which, bass.ds(token, HT)].unsqueeze(2).to_broadcast([P, HT, P]),
                                        ALU.is_equal).then_inc(made, 1)

            one_hots(0, True)
            with dve.Fori(1, NTB // 3) as t:
                one_hots(t, False)

            def low(b, number):
                dve.wait_ge(split_hi, number)
                v.tensor_tensor(w_lo[b][:, :, :], ring[b][:, :, :], w_hi[b][:, :, :].bitcast(F32), ALU.subtract
                                ).then_inc(split_lo, 1)

            low(0, 2 * PH + JG + 1)
            for j in range(JG):
                dve.wait_ge(first_hi, j + 1)
                v.tensor_tensor(act_hi[:, j, :], gel_first[:, j, :], act_lo[:, j, :].bitcast(F32), ALU.subtract
                                ).then_inc(act_ok, 1)
            low(1, 2 * PH + JG + 2)
            dve.wait_ge(tok_copied, 4)

            def dot(g, q):
                dve.wait_ge(gath_in[q % 2], 128 * g + 16 * (q // 2) + 16)
                row = grow[q % 2][:, :].rearrange("p (a n) -> p a n", a=KC)
                v.scalar_tensor_tensor(out=row, in0=row, scalar=1.0, in1=h_tok, op0=ALU.mult, op1=ALU.mult,
                                       accum_out=g_dot[:, bass.ds(16 * g + q, 1)]).then_inc(gath_free, 1)

            def gather_add(g, q):
                dve.wait_ge(gath_in[q % 2], 128 * g + 16 * (q // 2) + 16)
                dve.wait_ge(gath_free, 16 * g + q + 2)
                row = grow[q % 2][:, :].rearrange("p (a n) -> p a n", a=KC)
                v.scalar_tensor_tensor(out=g_acc, in0=row, scalar=g_act[:, bass.ds(16 * g + q - PAIRS, 1)], in1=g_acc,
                                       op0=ALU.mult, op1=ALU.add).then_inc(gath_free, 1)

            def weigh(g, q):
                prod = gel[q % 2][:, :]
                v.tensor_tensor(prod.rearrange("p (a b) -> p a b", a=NTB), prod.rearrange("p (a b) -> p a b", a=NTB),
                                wg[:, :, q, :], ALU.mult).then_inc(act_part, 1)
                dve.wait_ge(act_part, 2 * JG * (g - 1) + 2 * q + 1)
                v.tensor_copy(act_hi[:, q, :], prod).then_inc(act_part, 1)
                dve.wait_ge(act_part, 2 * JG * (g - 1) + 2 * q + 2)
                v.tensor_tensor(act_lo[:, q, :], prod, act_hi[:, q, :].bitcast(F32), ALU.subtract).then_inc(act_ok, 1)

            def add_outputs(g, q):
                dve.wait_ge(tile_done, 16 * g + T_EXP + q + 1)
                for c in (2 * (q - JG), 2 * (q - JG) + 1):
                    v.tensor_tensor(xT[:, c, 0:ND], xT[:, c, 0:ND], bank[4 + c % 4][:, 0:ND], ALU.add).then_inc(y_added, 1)

            def experts(g, last, gathered):
                dve.wait_ge(wg_in, 16 * g)
                for q in range(16):
                    if q < JG:
                        dve.wait_ge(u_gelu, JG * g + q + 1)
                        weigh(g, q)
                    else:
                        add_outputs(g, q)
                    if not (last and q >= 14):
                        low(q % 2, 16 * g + q + 2 * PH + 3)
                    gathered(g, q)

            for q in range(JG, 16):
                add_outputs(0, q)
                low(q % 2, q + 2 * PH + 3)
                dot(0, 2 * (q - JG))
                dot(0, 2 * (q - JG) + 1)
            with dve.Fori(1, NG // 2) as g:
                experts(g, False, dot)
            dve.wait_ge(gath_gelu, 1)
            v.tensor_tensor(g_act[:, :], g_act[:, :], g_w[:, :], ALU.mult).then_inc(gath_act, 1)
            dve.wait_ge(gath_act, 1)
            dve.wait_ge(acc_zero, 1)
            with dve.Fori(NG // 2, NG - 1) as g:
                experts(g, False, gather_add)
            experts(NG - 1, True, gather_add)
            for b in range(4):
                dve.wait_ge(tail_tr, b + 1)
                v.tensor_tensor(xT[:, 4 * b:4 * b + 4, ND:], xT[:, 4 * b:4 * b + 4, ND:],
                                bank[b][:, :].rearrange("p (a n) -> p a n", a=4), ALU.add).then_inc(tail_added, 1)

        @block.tensor
        def _(pe):
            def mm(out, lhsT, rhs, start=True, stop=True):
                return nc.tensor.matmul(out, lhsT, rhs, start=start, stop=stop)

            def project(n, out, rhs):
                landed(pe, n)
                for k in range(KC):
                    ins = mm(out, ring[n % SLOTS][:, k, :], rhs(k), start=(k == 0), stop=(k == KC - 1))
                ins.then_inc(tile_done, 1)

            def head_sum(n, width, number):
                pe.wait_ge(head_sq, number)
                mm(bank[4 + n % 2][:, 0:width], ones[:, :], sq[n % 2][:, 0:width]).then_inc(head_ss, 1)

            pe.wait_ge(const_made, 4)
            for c in range(KC):
                pe.wait_ge(mem_sq, c // 4 + 1)
                ins = mm(bank[6][:, 0:MEM], ones[:, :], msq[:, c, :], start=(c == 0), stop=(c == KC - 1))
            ins.then_inc(norm_ss, 1)
            landed(pe, T_MK)
            for c in range(KC):
                pe.wait_ge(mem_h, c + 1)
                ins = mm(bank[0][:, 0:MEM], ring[0][:, c, :], memT[:, c, :], start=(c == 0), stop=(c == KC - 1))
            ins.then_inc(tile_done, 1)
            for k in range(HC):
                if k:
                    project(T_MK + k, bank[k][:, 0:MEM], lambda c: memT[:, c, :])
                if k:
                    if k >= 3:
                        pe.wait_ge(head_rt, k - 2)
                    head_sum(k - 1, MEM, k)
            for c in range(KC):
                pe.wait_ge(x_sq, c // 4 + 1)
                ins = mm(bank[6][:, :], ones[:, :], xsq[:, c, :], start=(c == 0), stop=(c == KC - 1))
            ins.then_inc(norm_ss, 1)
            pe.wait_ge(head_rt, HC - 2)
            head_sum(HC - 1, MEM, HC)

            pe.wait_ge(acc_copied, HC)
            pe.wait_ge(head_sq, HC)
            for n in range(4):
                landed(pe, T_MV + n)
                w = ring[n][:, :, :].rearrange("p (c a) b -> p c (a b)", c=4)
                for c in range(4):
                    for m in range(MT):
                        ins = mm(bank[2 + m][:, :], memT[:, 4 * n + c, m * P:(m + 1) * P], w[:, c, :],
                                 start=(n == 0 and c == 0), stop=(n == 3 and c == 3))
                ins.then_inc(tile_done, 1)

            def split_mm(out, wh, wl, rh, rl, start, stop):
                mm(out, wh, rh, start=start, stop=False)
                mm(out, wh, rl, start=False, stop=False)
                return mm(out, wl, rh, start=False, stop=stop)

            def project_split(number, out, r_hi, r_lo, between=None):
                for q in range(4):
                    pe.wait_ge(quarter_lo, 4 * number + q + 1)
                    for c in range(4 * q, 4 * q + 4):
                        ins = split_mm(out, p_hi[:, c, :], p_lo[:, c, :], r_hi[:, c, :], r_lo[:, c, :], c == 0, c == KC - 1)
                    ins.then_inc(part_used if q < 3 else tile_done, 1)
                    if q == 0 and between is not None:
                        between()

            pe.wait_ge(h_ready, KC)
            pe.wait_ge(v_copied, MT)
            pe.wait_ge(head_rt, HC)

            def lru_gates(side):
                pe.wait_ge(lw_in, 64)
                pe.wait_ge(conv_ok, LC)
                for k in range(LC):
                    if side:
                        pe.wait_ge(lru_sig, k + 1)
                    mm(bank[4 + k][:, :], lw[:, side, k, :], xc[:, k, :]).then_inc(lru_mm, 1)

            for k in range(2 * LC):
                if k >= LC:
                    pe.wait_ge(lin_copied, k - LC + 1)
                project_split(k, bank[k % LC][:, :], norm_hi, norm_lo, (lambda: lru_gates(0)) if k == 2 * LC - 1 else None)

            def last_head(t, k):
                pe.wait_ge(head_rt, 4 * t + k + HC - 2)
                head_sum((k - 1) % 4, S, 4 * t + k + HC)

            def heads(t, first):
                for k in range(4):
                    if first:
                        pe.wait_ge(lin_copied, LC + k + 1)
                    else:
                        pe.wait_ge(head_sq, 4 * t + HC + k - 3)
                    if first and k == 1:
                        pe.wait_ge(lru_sig, 2 * LC)
                    project_split(4 * t + S_QK + k, bank[k][:, :], norm_hi, norm_lo,
                                  (lambda: lru_gates(1)) if first and k == 0 else lambda: last_head(t, k))

            heads(0, True)
            with pe.Fori(1, N_QK // 4) as t:
                heads(t, False)
            for half in range(2):
                if half:
                    pe.wait_ge(head_rt, HC + N_QK)
                for n in range(4):
                    wh, wl = (w[:, :, :].rearrange("p (c a) b -> p c (a b)", c=4) for w in (p_hi, p_lo))
                    for c in range(4):
                        pe.wait_ge(quarter_lo, 4 * (S_V + 4 * half + n) + c + 1)
                        for m in range(TT):
                            if half == 0 and n == 0 and c == 0:
                                pe.wait_ge(head_sq, HC + N_QK - TT + m + 1)
                            tok = slice(m * P, (m + 1) * P)
                            ins = split_mm(bank[4 * half + m][:, :], norm_hi[:, 4 * n + c, tok], norm_lo[:, 4 * n + c, tok],
                                           wh[:, c, :], wl[:, c, :], n == 0 and c == 0, n == 3 and c == 3)
                        ins.then_inc(part_used if c < 3 else tile_done, 1)
                        if half == 0 and n == 0 and c == 0:
                            last_head(N_QK // 4, 0)


            def band_scores(h, e):
                pe.wait_ge(at_a.staged_q, h + 1)
                pe.wait_ge(at_a.taken, TT * h)
                for q in range(TT):
                    mm(bank[q][:, 0:(q + 1) * P], qs[e][:, q * P:(q + 1) * P],
                       kT[:, bass.ds(h, 1), 0:(q + 1) * P].rearrange("p a s -> p (a s)")).then_inc(at_a.scores, 1)

            def cross_scores(h, e):
                pe.wait_ge(at_c.staged_q, h + 1)
                pe.wait_ge(at_c.exped, TT * h)
                for q in range(TT):
                    mm(bank[q][:, 0:MEM], qs[e][:, q * P:(q + 1) * P],
                       mk[:, bass.ds(h, 1), :].rearrange("p a s -> p (a s)")).then_inc(at_c.scores, 1)

            def attention(a, heads, scores, turn, tiles, mix):
                def step(h, e, more):
                    pe.wait_ge(a.probsT, tiles * h)
                    for q in range(TT):
                        pe.wait_ge(a.probs, TT * h + q + 1)
                        turn(e, q)
                    if more:
                        scores(h + 2, e)
                    pe.wait_ge(a.staged_v, h + 1)
                    pe.wait_ge(a.out, h)
                    for kt in range(tiles):
                        pe.wait_ge(a.probsT, tiles * h + kt + 1)
                        ins = mix(e, kt)
                    ins.then_inc(a.mixed, 1)

                in_pairs(pe, heads, scores, step)

            def band_turn(e, q):
                for kt in range(q + 1):
                    ins = nc.tensor.transpose(t_ps[kt][:, (q - kt) * P:(q - kt + 1) * P],
                                              band_s(e, q)[:, kt * P:(kt + 1) * P], ident[:, :])
                    if q == TT - 1:
                        ins.then_inc(at_a.turned, 1)

            def cross_turn(e, q):
                for kt in range(MT):
                    ins = nc.tensor.transpose(bank[4 + kt][:, q * P:(q + 1) * P], cross_s(e, q)[:, kt * P:(kt + 1) * P],
                                              ident[:, :])
                    if q == TT - 1:
                        ins.then_inc(at_c.turned, 1)

            attention(at_a, HA, band_scores, band_turn, TT,
                      lambda e, kt: mm(bank[7][:, kt * P:], vs[e][:, kt, :], pT[kt], start=(kt == 0), stop=(kt == TT - 1)))
            pe.wait_ge(at_a.out, HA)
            attention(at_c, HC, cross_scores, cross_turn, MT,
                      lambda e, kt: mm(bank[7][:, :], vs[e][:, kt, :], pTc[kt], start=(kt == 0), stop=(kt == MT - 1)))

            pe.wait_ge(at_c.out, HC)
            with pe.Fori(0, KC) as c:
                for b in range(3):
                    pe.wait_ge(gate_ok, 3 * c)
                    project_split(4 * c + S_MIX + b, bank[b][:, :], norm_hi, norm_lo)
                pe.wait_ge(y_used, 3 * c)
                pe.wait_ge(branch_ready, KC)
                first = (0, HA, HA + LC, KC)
                for n in range(KC):
                    if n % 4 == 0:
                        pe.wait_ge(quarter_lo, 16 * c + 4 * (S_MIX + 3) + n // 4 + 1)
                    b = 2 if n >= first[2] else int(n >= first[1])
                    ins = split_mm(bank[3 + b][:, :], p_hi[:, n, :], p_lo[:, n, :], branch_hi[n], branch_lo[n],
                                   n == first[b], n + 1 == first[b + 1])
                    if n % 4 == 3:
                        ins.then_inc(part_used if n < KC - 1 else tile_done, 1)

            pe.wait_ge(m_ready, KC)
            with pe.Fori(0, KC // 4) as t:
                for k in range(4):
                    pe.wait_ge(x2_ok, 4 * t)
                    project_split(4 * t + S_WO + k, bank[k][:, :], h_hi, h_lo)
            pe.wait_ge(x2_sum, KC + 1)
            mm(bank[6][:, :], ones[:, :], sumsq).then_inc(norm_ss, 1)

            pe.wait_ge(keys_in, 16)

            def scores(n, k):
                pe.wait_ge(pq_copied, n + 1)
                for m in range(TT):
                    ins = mm(bank[4 + k][:, m * P:(m + 1) * P], qp[:, k, m * P:(m + 1) * P],
                             kys[:, bass.ds(n, 1), :].rearrange("p a n -> p (a n)"))
                ins.then_inc(pq_scores, 1)

            def queries(t, first):
                for k in range(4):
                    b = k % 2
                    pe.wait_ge(split_lo, 4 * t + k + 1)
                    for c in range(KC):
                        pe.wait_ge(h2_ready, c + 1)
                        ins = split_mm(bank[k][:, :], w_hi[b][:, c, :], w_lo[b][:, c, :], h_hi[:, c, :], h_lo[:, c, :],
                                       c == 0, c == KC - 1)
                        if c == KC // 2 - 1 and not (first and k == 0):
                            if not first:
                                pe.wait_ge(sc_copied, 4 * t + k - 4)
                            scores(4 * t + k - 1, (k - 1) % 4)
                    ins.then_inc(tile_done, 1)

            queries(0, True)
            with pe.Fori(1, PH // 2) as t:
                queries(t, False)
            scores(2 * PH - 1, 3)

            pe.wait_ge(ident_ok, 1)
            pe.wait_ge(pq_copied, 2 * PH)
            for c in range(KC):
                dst = bank[c // 4][:, (c % 4) * P:(c % 4 + 1) * P]
                mm(dst, h_hi[:, c, ND:], ident_r[:, :], start=True, stop=False)
                ins = mm(dst, h_lo[:, c, ND:], ident_r[:, :], start=False, stop=True)
            ins.then_inc(tok_mm, 1)

            def u_products(g):
                for j in range(JG):
                    b = j % 2
                    pe.wait_ge(split_lo, 16 * g + 2 * PH + j + 1)
                    pe.wait_ge(u_gelu, JG * g + max(j - 3, 0))
                    for c in range(KC):
                        ins = split_mm(bank[j % 4][:, 0:ND], w_hi[b][:, c, :], w_lo[b][:, c, :],
                                       h_hi[:, c, 0:ND], h_lo[:, c, 0:ND], c == 0, c == KC - 1)
                    ins.then_inc(tile_done, 1)

            pe.wait_ge(tok_copied, 4)
            u_products(0)

            pe.wait_ge(route_ok, 1)
            pe.wait_ge(sc_copied, 2 * PH)
            for w in range(3):
                for m in range(TG):
                    ins = nc.tensor.transpose(bank[4 + w][:, m * P:(m + 1) * P],
                                              route[:, w, m, :, :].rearrange("p h k -> p (h k)"), ident[:, :])
                ins.then_inc(route_tr, 1)

            pe.wait_ge(route_copied, 3)
            pe.wait_ge(u_gelu, JG)

            def tables(t, first):
                for k in range(12):
                    pe.wait_ge(oh_a, 12 * t + k + 1)
                    pe.wait_ge(oh_b, 12 * t + k + 1)
                    for b in (2 * k, 2 * k + 1):
                        if not first or b >= 8:
                            pe.wait_ge(tab_copied, 24 * t + b - 7)
                        for n in range(4):
                            row = 4 * (b % 2) + n
                            ins = mm(bank[b % 8][:, n * P:(n + 1) * P], ohA[k % 2][:, row, :], ohB[k % 3][:, row, :])
                        ins.then_inc(tab_mm, 1)

            tables(0, True)
            with pe.Fori(1, NTB // 3) as t:
                tables(t, False)

            pe.wait_ge(tab_copied, 8 * NTB)

            def v_products(g, a_hi, a_lo):
                for c in range(KC):
                    b = (c // 2) % 2
                    if c % 2 == 0:
                        pe.wait_ge(split_lo, 16 * g + 2 * PH + JG + c // 2 + 1)
                    pe.wait_ge(y_added, KC * g + max(c - 3, 0))
                    for j in range(JG):
                        if c == 0:
                            pe.wait_ge(act_ok, JG * g + j + 1)
                        part = JG * (c % 2) + j
                        ins = split_mm(bank[4 + c % 4][:, 0:ND], w_hi[b][:, part, :], w_lo[b][:, part, :],
                                       a_hi[:, j, :], a_lo[:, j, :], j == 0, j == JG - 1)
                    if c % 2:
                        ins.then_inc(tile_done, 1)

            v_products(0, act_lo, act_hi)
            with pe.Fori(1, NG) as g:
                u_products(g)
                v_products(g, act_hi, act_lo)

            pe.wait_ge(gath_free, 2 + 2 * PAIRS)
            for c in range(KC):
                ins = nc.tensor.transpose(bank[c // 4][:, (c % 4) * P:(c % 4 + 1) * P], g_acc[:, c, :], ident[:, :])
                if c % 4 == 3:
                    ins.then_inc(tail_tr, 1)


def stationary(w):
    k, n = w.shape
    return np.ascontiguousarray(w.reshape(k // P, P, n // P, P).transpose(2, 1, 0, 3)).reshape(n // P, P, -1)


def moving(w):
    k, n = w.shape
    v = w.reshape(4, 4, P, n // 512, 512).transpose(3, 0, 2, 1, 4)
    return np.ascontiguousarray(v).reshape(-1, P, 2048)


def by_partition(vec):
    return np.ascontiguousarray(vec.reshape(-1, P).T)


def layout(a):
    w_in = a["w_in"]
    qkv = HA * DH
    lru0 = 3 * qkv
    xq0 = lru0 + 2 * LC * P
    lru_w = np.stack([a[n].reshape(LC, 2, 64, 64).transpose(1, 2, 0, 3) for n in ("lru_wa", "lru_wx")])
    lru_vec = np.stack([*(a["conv_w"][i] for i in range(TAPS)), a["conv_b"], a["lru_ba"], a["lru_bx"], a["lru_lambda"]])
    mix = np.stack([*(stationary(a["w_gate"][:, b * D:(b + 1) * D]) for b in range(3)), stationary(a["w_branch"])], axis=1)
    u = a["peer_u"].reshape(P, NG, JG, KC, P).transpose(1, 2, 4, 3, 0).reshape(NG, JG, P, 2048)
    v = a["peer_v"].reshape(P, NG, JG, KC // 2, 2, P).transpose(1, 3, 0, 4, 2, 5).reshape(NG, KC // 2, P, 2048)
    tokens = lambda x: np.ascontiguousarray(x[0].T.reshape(KC, P, -1).transpose(1, 0, 2))
    return {
        "x_t": tokens(a["x"]), "mem_t": tokens(a["mem"]),
        "g1": by_partition(a["norm1_g"]), "g2": by_partition(a["norm2_g"]), "gmem": by_partition(a["mem_norm_g"]),
        "head_g": np.stack([a[n] for n in ("attn_q_norm_g", "attn_k_norm_g", "xq_norm_g", "xk_norm_g")], axis=1),
        "w_memk": stationary(a["w_mem_kv"][:, :HC * DH]), "w_memv": moving(a["w_mem_kv"][:, HC * DH:]),
        "w_qk": np.concatenate([stationary(w_in[:, :2 * qkv]), stationary(w_in[:, xq0:])]),
        "w_lru_in": stationary(w_in[:, lru0:xq0]), "w_v": moving(w_in[:, 2 * qkv:lru0]),
        "rel_rev": np.ascontiguousarray(a["rel_bias"][:, ::-1]), "lru_w": np.ascontiguousarray(lru_w),
        "lru_vec": np.ascontiguousarray(lru_vec.reshape(8, LC, P).transpose(2, 0, 1)),
        "w_mix": mix.reshape(4 * KC, P, 2048), "b_gate": by_partition(a["b_gate"]),
        "w_o": stationary(a["w_o"]), "w_pq": stationary(a["w_peer_q"]),
        "keys": np.ascontiguousarray(a["peer_keys"].reshape(2 * PH, NKEYS, P).transpose(2, 0, 1)),
        "w_exp": np.concatenate([u, v], axis=1).reshape(16 * NG, P, 2048),
        "u_rows": a["peer_u"], "v_rows": a["peer_v"],
    }


def kernel(**inputs):
    import concourse.bacc as bacc
    from concourse.bass_utils import run_bass_kernel_spmd

    nc = bacc.Bacc("TRN2", target_bir_lowering=False, num_devices=1)
    arrays = {n: np.ascontiguousarray(v) for n, v in layout({n: np.asarray(v) for n, v in inputs.items()}).items()}
    args = [nc.dram_tensor(n, v.shape, mybir.dt.from_np(v.dtype), kind="ExternalInput").ap() for n, v in arrays.items()]
    out_t = nc.dram_tensor("out_t", (P, KC, S), F32, kind="ExternalOutput").ap()
    hybrid_block(nc, *args, out_t)
    r = run_bass_kernel_spmd(nc, [arrays], core_ids=[0])
    o = r.results[0]["out_t"]
    return np.ascontiguousarray(o.transpose(2, 1, 0).reshape(1, S, D))
```
